# Optimizing a Trainium2 kernel written in Bass

```python
import math
import jax, jax.numpy as jnp
from jax import lax
import numpy as np

D_MODEL = 1024
BATCH = 1
SEQ = 2048
DEPTH = 2

N_MIXERS = 2
N_GLA = (DEPTH + 1) // 2
N_POOL = DEPTH // 2

GLA_HEADS = 4
GLA_KD = D_MODEL // 2
GLA_VD = D_MODEL
GLA_DK = GLA_KD // GLA_HEADS
GLA_DV = GLA_VD // GLA_HEADS
GLA_GATE_RANK = 16
GLA_GATE_NORMALIZER = 16.0
GLA_CHUNK = 64
GLA_IN = 2 * GLA_KD + 2 * GLA_VD + GLA_GATE_RANK

POOL_EXPAND = 2
POOL_WIDTH = POOL_EXPAND * D_MODEL
POOL_WINDOWS = (2, 4, 8, 16)
POOL_GROUPS = len(POOL_WINDOWS)
POOL_GW = POOL_WIDTH // POOL_GROUPS

DEEPNORM_ALPHA = (2.0 * DEPTH) ** 0.25
DEEPNORM_BETA = (8.0 * DEPTH) ** -0.25
LN_EPS = 1e-5
RMS_EPS = 1e-6

kernel_name = "gla_pool_interleaved_deepnorm"

def _layernorm(x, g, b):
    xf = x.astype(jnp.float32)
    mu = jnp.mean(xf, axis=-1, keepdims=True)
    var = jnp.mean(jnp.square(xf - mu), axis=-1, keepdims=True)
    y = (xf - mu) * lax.rsqrt(var + LN_EPS) * g.astype(jnp.float32) + b.astype(jnp.float32)
    return y.astype(x.dtype)

def _gla_mixer(x, w_in, w_gk, b_gk, norm_w, w_out):
    B, T, _ = x.shape
    nc = T // GLA_CHUNK
    h = (x @ w_in).astype(jnp.float32)
    q, k, v, g, lr = jnp.split(
        h, [GLA_KD, 2 * GLA_KD, 2 * GLA_KD + GLA_VD, 2 * GLA_KD + 2 * GLA_VD], axis=-1)
    gk = jax.nn.log_sigmoid(lr @ w_gk.astype(jnp.float32) + b_gk.astype(jnp.float32))
    gk = gk / GLA_GATE_NORMALIZER

    def heads(t, dh):
        return t.reshape(B, nc, GLA_CHUNK, GLA_HEADS, dh).transpose(0, 3, 1, 2, 4)

    q = heads(q, GLA_DK) * (GLA_DK ** -0.5)
    k = heads(k, GLA_DK)
    v = heads(v, GLA_DV)
    gk = heads(gk, GLA_DK)

    bcum = jnp.cumsum(gk, axis=-2)
    b_last = bcum[..., -1:, :]
    qe = q * jnp.exp(bcum)
    ke = k * jnp.exp(-bcum)
    kd = k * jnp.exp(b_last - bcum)

    mask = jnp.tril(jnp.ones((GLA_CHUNK, GLA_CHUNK), dtype=bool))
    scores = jnp.einsum('bhncd,bhnsd->bhncs', qe, ke)
    scores = jnp.where(mask, scores, 0.0)
    o_intra = jnp.einsum('bhncs,bhnsv->bhncv', scores, v)

    kv = jnp.einsum('bhncd,bhncv->bhndv', kd, v)
    decay = jnp.exp(b_last[..., 0, :])

    def step(S, inp):
        dec, kvc = inp
        return dec[..., None] * S + kvc, S

    S0 = jnp.zeros((B, GLA_HEADS, GLA_DK, GLA_DV), jnp.float32)
    _, S_prev = lax.scan(step, S0, (jnp.moveaxis(decay, 2, 0), jnp.moveaxis(kv, 2, 0)))
    S_prev = jnp.moveaxis(S_prev, 0, 2)
    o = o_intra + jnp.einsum('bhncd,bhndv->bhncv', qe, S_prev)

    o = o.transpose(0, 2, 3, 1, 4).reshape(B, T, GLA_HEADS, GLA_DV)
    o = o * lax.rsqrt(jnp.mean(jnp.square(o), axis=-1, keepdims=True) + RMS_EPS)
    o = o * norm_w.astype(jnp.float32)
    o = o.reshape(B, T, GLA_VD) * jax.nn.silu(g)
    return o.astype(x.dtype) @ w_out

def _pool_mixer(x, w_in, w_grp, b_grp, scale, w_out):
    B, T, _ = x.shape
    h = x @ w_in
    u, z = jnp.split(h, [POOL_WIDTH], axis=-1)
    u = u.astype(jnp.float32).reshape(B, T, POOL_GROUPS, POOL_GW)
    cs = jnp.cumsum(u, axis=1)
    pos = jnp.arange(1, T + 1, dtype=jnp.float32)
    pooled = []
    for gi, w in enumerate(POOL_WINDOWS):
        cs_g = cs[:, :, gi]
        lag = jnp.pad(cs_g, ((0, 0), (w, 0), (0, 0)))[:, :T]
        cnt = jnp.minimum(pos, float(w))[None, :, None]
        pooled.append((cs_g - lag) / cnt)
    p = jnp.stack(pooled, axis=2) - u
    m = jnp.einsum('btgc,gcd->btgd', p, w_grp.astype(jnp.float32)) + b_grp.astype(jnp.float32)
    m = m.reshape(B, T, POOL_WIDTH) * scale.astype(jnp.float32)
    y = m * jax.nn.silu(z.astype(jnp.float32))
    return y.astype(x.dtype) @ w_out

def setup_inputs(seed: int = 0) -> dict:
    key = jax.random.key(seed)
    ks = jax.random.split(key, 16)
    f32 = jnp.float32
    nrm = lambda k, s, sc: (jax.random.normal(k, s, f32) * sc)
    return {
        "x": jax.random.normal(ks[0], (BATCH, SEQ, D_MODEL), f32),
        "gla_w_in": nrm(ks[1], (N_GLA, D_MODEL, GLA_IN), D_MODEL ** -0.5),
        "gla_w_gk": nrm(ks[2], (N_GLA, GLA_GATE_RANK, GLA_KD), GLA_GATE_RANK ** -0.5),
        "gla_b_gk": nrm(ks[3], (N_GLA, GLA_KD), 0.02),
        "gla_norm_w": 1.0 + nrm(ks[4], (N_GLA, GLA_DV), 0.02),
        "gla_w_out": nrm(ks[5], (N_GLA, GLA_VD, D_MODEL), GLA_VD ** -0.5 * DEEPNORM_BETA),
        "pool_w_in": nrm(ks[6], (N_POOL, D_MODEL, 2 * POOL_WIDTH), D_MODEL ** -0.5),
        "pool_w_grp": nrm(ks[7], (N_POOL, POOL_GROUPS, POOL_GW, POOL_GW), POOL_GW ** -0.5),
        "pool_b_grp": nrm(ks[8], (N_POOL, POOL_GROUPS, POOL_GW), 0.02),
        "pool_scale": 1.0 + nrm(ks[9], (N_POOL, POOL_WIDTH), 0.02),
        "pool_w_out": nrm(ks[10], (N_POOL, POOL_WIDTH, D_MODEL), POOL_WIDTH ** -0.5 * DEEPNORM_BETA),
        "ln_g": 1.0 + nrm(ks[11], (DEPTH, D_MODEL), 0.02),
        "ln_b": nrm(ks[12], (DEPTH, D_MODEL), 0.02),
    }

def reference(x, gla_w_in, gla_w_gk, gla_b_gk, gla_norm_w, gla_w_out,
              pool_w_in, pool_w_grp, pool_b_grp, pool_scale, pool_w_out, ln_g, ln_b):
    for i in range(DEPTH):
        j = i // N_MIXERS
        if i % N_MIXERS == 0:
            y = _gla_mixer(x, gla_w_in[j], gla_w_gk[j], gla_b_gk[j], gla_norm_w[j], gla_w_out[j])
        else:
            y = _pool_mixer(x, pool_w_in[j], pool_w_grp[j], pool_b_grp[j], pool_scale[j], pool_w_out[j])
        x = _layernorm(DEEPNORM_ALPHA * x + y, ln_g[i], ln_b[i])
    return x


_drawn_inputs = setup_inputs


def setup_inputs(seed=0):
    import zlib

    import numpy as np

    out = dict(_drawn_inputs(seed))
    spreads = {}
    factors = {'gla_b_gk': 8.0, 'gla_norm_w': 8.0, 'pool_b_grp': 8.0, 'pool_scale': 8.0}
    for name, (base, spread) in spreads.items():
        noise = np.random.default_rng([zlib.crc32(name.encode()), seed]).standard_normal(out[name].shape)
        drawn = base * np.exp(spread * noise) if base else spread * noise
        out[name] = __import__('jax').numpy.asarray(drawn.astype(out[name].dtype))
    for name, factor in factors.items():
        out[name] = (out[name] * factor).astype(out[name].dtype)
    return out
```

```python
import concourse.bass as bass
from concourse import mybir
from contextlib import ExitStack

F32 = mybir.dt.float32
F32R = mybir.dt.float32r
I32 = mybir.dt.int32
ALU = mybir.AluOpType
ACT = mybir.ActivationFunctionType
ds = bass.ds

P = 128
SEQ = 2048
D = 1024
KT = D // P
HEADS = 4
DK = 128
DV = 256
CHUNK = 64
GATE_RANK = 16
GATE_NORMALIZER = 16.0
NT = SEQ // P
BLK = 512
NB = SEQ // BLK
KD = HEADS * DK
VD = HEADS * DV
POOL_W = 2048
WINDOWS = (2, 4, 8, 16)
GROUPS = len(WINDOWS)
GW = POOL_W // GROUPS
GT = GW // P
MT = POOL_W // P
PAD = max(WINDOWS)
ALPHA = 4.0 ** 0.25
LN_EPS = 1e-5
RMS_EPS = 1e-6
SBUF_START = 16512
DMA = 16



class Program:

    def __init__(self, nc, ctx):
        self.nc, self.ctx, self.at = nc, ctx, SBUF_START

    def sem(self, name):
        return self.ctx.enter_context(self.nc.semaphore(name))

    def sems(self, name, n):
        return [self.sem(f"{name}{i}") for i in range(n)]

    def place(self, name, shape, dtype=F32):
        size = 4
        for n in shape[1:]:
            size *= n
        t = self.nc.alloc_sbuf_tensor_at(name, shape, dtype, offset=self.at)
        self.at += (size + 31) // 32 * 32
        return t


def split_product(nc, out, a_hi, a_lo, b_hi, b_lo, first, last):
    nc.tensor.matmul(out, a_hi, b_hi, start=first, stop=False, skip_group_check=True)
    nc.tensor.matmul(out, a_hi, b_lo, start=False, stop=False, skip_group_check=True)
    return nc.tensor.matmul(out, a_lo, b_hi, start=False, stop=last, skip_group_check=True)


def constants(nc, p, a):
    made, ones_in, loaded, masked, pe = (p.sem(f"const_{n}") for n in ("made", "ones", "loaded", "masked", "x"))
    with nc.Block() as block:

        @block.sync
        def _(sp):
            with nc.allow_non_contiguous_dma(reason="small parameter vectors as columns"):
                sp.dma_start(p.b_gk[:], a["gla_b_gk"][0].rearrange("(h d) -> d h", d=P)).then_inc(loaded, DMA)
                sp.dma_start(p.norm_w[:], a["gla_norm_w"][0].rearrange("(j d) -> d j", d=P)).then_inc(loaded, DMA)
                sp.dma_start(p.b_grp[:], a["pool_b_grp"][0].rearrange("g (m d) -> d (g m)", d=P)).then_inc(loaded, DMA)
                sp.dma_start(p.scale[:], a["pool_scale"][0].rearrange("(m d) -> d m", d=P)).then_inc(loaded, DMA)
            sp.wait_ge(loaded, 4 * DMA)

        @block.vector
        def _(dve):
            nc.vector.memset(p.mean_w[:], 1.0 / DV)
            nc.vector.memset(p.keep[:], 1.0).then_inc(ones_in, 1)
            nc.vector.memset(p.eps_rms[:], RMS_EPS)
            nc.vector.memset(p.eps_ln[:], LN_EPS)
            nc.vector.memset(p.correct[:], 1.0).then_inc(ones_in, 1)
            dve.wait_ge(ones_in, 2)
            nc.vector.memset(p.keep[:].rearrange("p (c s) -> p c s", s=CHUNK)[:, :, 0:1], 0.0)
            for g, w in enumerate(WINDOWS):
                for t in range(w - 1):
                    nc.vector.memset(p.correct[:, g, t:t + 1], w / (t + 1.0))

        @block.gpsimd
        def _(pool):
            nc.gpsimd.memset(p.ident[:], 0.0)
            nc.gpsimd.memset(p.mask[:], 1.0).then_inc(made, 1)
            pool.wait_ge(made, 1)
            nc.gpsimd.affine_select(out=p.ident[:], in_=p.ident[:], compare_op=ALU.not_equal, fill=1.0,
                                    base=0, pattern=[[-1, P]], channel_multiplier=1)
            nc.gpsimd.affine_select(out=p.mask[:], in_=p.mask[:], compare_op=ALU.is_ge, fill=0.0,
                                    base=0, pattern=[[0, HEADS], [1, P]], channel_multiplier=-1).then_inc(masked, 1)
            pool.wait_ge(masked, 1)
            late = p.mask[:, :, CHUNK:P]
            nc.gpsimd.affine_select(out=late, in_=late, compare_op=ALU.is_ge, fill=0.0,
                                    base=-CHUNK, pattern=[[0, HEADS], [0, CHUNK]], channel_multiplier=1)


def fuse_pool_weights(nc, p, a):
    p.at = p.work_at
    w_in = [p.place(f"fuse_in{s}", [P, KT, GW]) for s in range(2)]
    w_grp = [p.place(f"fuse_grp{s}", [P, GT, GW]) for s in range(2)]
    grp_hi = [p.place(f"fuse_grp_hi{s}", [P, GT, GW], F32R) for s in range(2)]
    grp_lo = [p.place(f"fuse_grp_lo{s}", [P, GT, GW], F32R) for s in range(2)]
    t_hi = [p.place(f"fuse_t_hi{s}", [P, GT, P], F32R) for s in range(2)]
    t_lo = [p.place(f"fuse_t_lo{s}", [P, GT, P], F32R) for s in range(2)]
    out = [p.place(f"fuse_out{s}", [P, GW]) for s in range(2)]
    loaded = p.sems("fuse_loaded", 2)
    g_hi, g_lo, turned, hi, lo, multiplied, copied = (
        p.sem(f"fuse_{n}") for n in ("g_hi", "g_lo", "turned", "hi", "lo", "multiplied", "copied"))
    stored = p.sems("fuse_stored", 2)
    src_in = a["pool_w_in"][0].rearrange("(k p) c -> p k c", p=P)
    src_grp = a["pool_w_grp"][0].rearrange("g (k p) c -> p g k c", p=P)
    turned_ps = [p.ps[:, s, :] for s in range(2)]
    out_ps = [p.ps[:, 2 + s, :] for s in range(2)]
    PAIR = 2 * KT

    with nc.Block() as block:

        @block.sync
        def _(sp):
            with sp.Fori(0, GROUPS // 2) as pair:
                for s in range(2):
                    sp.wait_ge(multiplied, pair * PAIR - (1 - s) * 0)
                    g = pair * 2 + s
                    sp.dma_start(w_in[s][:], src_in[:, :, ds(g * GW, GW)]).then_inc(loaded[s], DMA)
                    sp.dma_start(w_grp[s][:], src_grp[:, ds(g, 1), :, :].rearrange("p o k c -> p (o k) c")
                                 ).then_inc(loaded[s], DMA)
                for s in range(2):
                    for k in range(KT):
                        n = pair * PAIR + s * KT + k
                        g = pair * 2 + s
                        sp.wait_ge(copied, n + 1)
                        sp.dma_start(p.w_fused[ds(g * GT, GT), :, k, :].rearrange("m p c -> p m c"),
                                     out[k % 2][:].rearrange("p (m c) -> p m c", c=P)).then_inc(stored[k % 2], DMA)
            sp.wait_ge(stored[0], DMA * GROUPS * KT // 2)
            sp.wait_ge(stored[1], DMA * GROUPS * KT // 2)

        @block.tensor
        def _(pe):
            def turn(pair, i):
                s, k = i // KT, i % KT
                if k == 0:
                    pe.wait_ge(loaded[s], (pair + 1) * 2 * DMA)
                if i >= 2:
                    pe.wait_ge(lo, pair * PAIR + i - 1)
                else:
                    pe.wait_ge(lo, pair * PAIR)
                for c in range(GT):
                    last = nc.tensor.transpose(turned_ps[i % 2][:, c * P:(c + 1) * P],
                                               w_in[s][:, k, c * P:(c + 1) * P], p.ident[:])
                last.then_inc(turned, 1)

            with pe.Fori(0, GROUPS // 2) as pair:
                turn(pair, 0)
                for i in range(PAIR):
                    if i + 1 < PAIR:
                        turn(pair, i + 1)
                    s = i // KT
                    pe.wait_ge(lo, pair * PAIR + i + 1)
                    pe.wait_ge(g_lo, pair * 2 + s + 1)
                    pe.wait_ge(copied, pair * PAIR + max(i - 1, 0))
                    for c in range(GT):
                        last = split_product(nc, out_ps[i % 2], t_hi[i % 2][:, c, :], t_lo[i % 2][:, c, :],
                                             grp_hi[s][:, c, :], grp_lo[s][:, c, :], c == 0, c == GT - 1)
                    last.then_inc(multiplied, 1)

        @block.scalar
        def _(act):
            with act.Fori(0, GROUPS // 2) as pair:
                for i in range(PAIR):
                    s, n = i // KT, pair * PAIR + i
                    if i % KT == 0:
                        act.wait_ge(loaded[s], (pair + 1) * 2 * DMA)
                        act.wait_ge(multiplied, pair * PAIR)
                        nc.scalar.activation(grp_hi[s][:], w_grp[s][:], ACT.Copy).then_inc(g_hi, 1)
                    act.wait_ge(turned, n + 1)
                    act.wait_ge(multiplied, pair * PAIR + max(i - 1, 0))
                    nc.scalar.activation(t_hi[i % 2][:].rearrange("p c d -> p (c d)"), turned_ps[i % 2],
                                         ACT.Copy).then_inc(hi, 1)
                    if i >= 1:
                        act.wait_ge(multiplied, n)
                        act.wait_ge(stored[(i - 1) % 2], (pair * KT + (i - 1) // 2) * DMA)
                        nc.scalar.activation(out[(i - 1) % 2][:], out_ps[(i - 1) % 2], ACT.Copy).then_inc(copied, 1)
                act.wait_ge(multiplied, (pair + 1) * PAIR)
                act.wait_ge(stored[1], (pair * KT + KT - 1) * DMA)
                nc.scalar.activation(out[1][:], out_ps[1], ACT.Copy).then_inc(copied, 1)

        @block.vector
        def _(dve):
            with dve.Fori(0, GROUPS // 2) as pair:
                for i in range(PAIR):
                    s, n = i // KT, pair * PAIR + i
                    if i % KT == 0:
                        dve.wait_ge(g_hi, pair * 2 + s + 1)
                        nc.vector.tensor_tensor(grp_lo[s][:], w_grp[s][:], grp_hi[s][:].bitcast(F32),
                                                ALU.subtract).then_inc(g_lo, 1)
                    dve.wait_ge(hi, n + 1)
                    nc.vector.tensor_tensor(t_lo[i % 2][:].rearrange("p c d -> p (c d)"), turned_ps[i % 2],
                                            t_hi[i % 2][:].rearrange("p c d -> p (c d)").bitcast(F32),
                                            ALU.subtract).then_inc(lo, 1)


def transpose_input(nc, p, name, x):
    SLOTS = 4
    p.at = p.stream_at
    rows = [p.place(f"{name}_rows{s}", [P, D]) for s in range(SLOTS)]
    loaded = p.sems(f"{name}_loaded", SLOTS)
    turned, hi, lo = (p.sem(f"{name}_{n}") for n in ("turned", "hi", "lo"))
    turned_ps = [p.ps[:, 2 * s:2 * s + 2, :].rearrange("p b (k t) -> p (b k) t", t=P) for s in range(2)]

    with nc.Block() as block:

        @block.sync
        def _(sp):
            for s in range(SLOTS):
                sp.dma_start(rows[s][:], x[s * P:(s + 1) * P, :]).then_inc(loaded[s], DMA)
            with sp.Fori(1, NT // SLOTS) as q:
                for s in range(SLOTS):
                    sp.wait_ge(turned, q * SLOTS + s - SLOTS + 1)
                    sp.dma_start(rows[s][:], x[ds((q * SLOTS + s) * P, P), :]).then_inc(loaded[s], DMA)

        @block.tensor
        def _(pe):
            with pe.Fori(0, NT // SLOTS) as q:
                for s in range(SLOTS):
                    pe.wait_ge(loaded[s], (q + 1) * DMA)
                    pe.wait_ge(lo, q * SLOTS + max(s - 1, 0))
                    for k in range(KT):
                        last = nc.tensor.transpose(turned_ps[s % 2][:, k, :], rows[s][:, k * P:(k + 1) * P],
                                                   p.ident[:])
                    last.then_inc(turned, 1)

        @block.scalar
        def _(act):
            with act.Fori(0, NT // 2) as u:
                for s in range(2):
                    t = u * 2 + s
                    act.wait_ge(turned, t + 1)
                    nc.scalar.activation(p.x_hi[:, :, ds(t * P, P)], turned_ps[s], ACT.Copy).then_inc(hi, 1)

        @block.vector
        def _(dve):
            with dve.Fori(0, NT // 2) as u:
                for s in range(2):
                    t = u * 2 + s
                    dve.wait_ge(hi, t + 1)
                    nc.vector.tensor_tensor(p.x_lo[:, :, ds(t * P, P)], turned_ps[s],
                                            p.x_hi[:, :, ds(t * P, P)].bitcast(F32), ALU.subtract).then_inc(lo, 1)


def project_values(nc, p, a):
    HALVES = 2
    RAW, OUT, BANKS = 4, 4, 4
    p.at = p.stream_at
    raw = [p.place(f"v_raw{s}", [P, BLK]) for s in range(RAW)]
    w_hi = p.place("v_w_hi", [P, KT, BLK], F32R)
    w_lo = p.place("v_w_lo", [P, KT, BLK], F32R)
    out = [p.place(f"v_out{s}", [P, BLK]) for s in range(OUT)]
    loaded = p.sems("v_loaded", RAW)
    stored = p.sems("v_stored", OUT)
    hi, lo, multiplied, copied = (p.sem(f"v_{n}") for n in ("hi", "lo", "multiplied", "copied"))
    w_src = a["gla_w_in"][0].rearrange("(k p) c -> p k c", p=P)

    with nc.Block() as block:

        @block.sync
        def _(sp):
            with sp.Fori(0, HALVES) as half:
                for k in range(KT):
                    sp.wait_ge(lo, half * KT + max(k - RAW + 1, 0))
                    sp.dma_start(raw[k % RAW][:], w_src[:, k, ds(half * BLK + 2 * KD, BLK)]
                                 ).then_inc(loaded[k % RAW], DMA)

        @block.tensor
        def _(pe):
            with pe.Fori(0, HALVES) as half:
                for t in range(NT):
                    pe.wait_ge(copied, half * NT + max(t - BANKS + 1, 0))
                    for k in range(KT):
                        if t == 0:
                            pe.wait_ge(lo, half * KT + k + 1)
                        last = split_product(nc, p.ps[:, t % BANKS, :], p.x_hi[:, k, t * P:(t + 1) * P],
                                             p.x_lo[:, k, t * P:(t + 1) * P], w_hi[:, k, :], w_lo[:, k, :],
                                             k == 0, k == KT - 1)
                    last.then_inc(multiplied, 1)

        @block.scalar
        def _(act):
            with act.Fori(0, HALVES) as half:
                act.wait_ge(multiplied, half * NT)
                for k in range(KT):
                    act.wait_ge(loaded[k % RAW], (half * (KT // RAW) + k // RAW + 1) * DMA)
                    nc.scalar.activation(w_hi[:, k, :], raw[k % RAW][:], ACT.Copy).then_inc(hi, 1)
                for t in range(NT):
                    act.wait_ge(multiplied, half * NT + t + 1)
                    act.wait_ge(stored[t % OUT], (half * (NT // OUT) + t // OUT) * DMA)
                    nc.scalar.activation(out[t % OUT][:], p.ps[:, t % BANKS, :], ACT.Copy).then_inc(copied, 1)
                    act.wait_ge(copied, half * NT + t + 1)
                    act.dma_start(p.v_tiles[t, :, ds(half * BLK, BLK)], out[t % OUT][:]).then_inc(stored[t % OUT], DMA)
            for s in range(OUT):
                act.wait_ge(stored[s], HALVES * NT // OUT * DMA)

        @block.vector
        def _(dve):
            with dve.Fori(0, HALVES) as half:
                for k in range(KT):
                    dve.wait_ge(hi, half * KT + k + 1)
                    nc.vector.tensor_tensor(w_lo[:, k, :], raw[k % RAW][:], w_hi[:, k, :].bitcast(F32),
                                            ALU.subtract).then_inc(lo, 1)


def project_heads(nc, p, a):
    p.at = p.stream_at
    raw = [p.place(f"h_raw{s}", [P, KT, P]) for s in range(2)]
    w_hi = [p.place(f"h_w_hi{s}", [P, KT, P], F32R) for s in range(2)]
    w_lo = [p.place(f"h_w_lo{s}", [P, KT, P], F32R) for s in range(2)]
    rank = p.place("h_rank", [2 * GATE_RANK, SEQ])
    w_gk = p.place("h_w_gk", [2 * GATE_RANK, P])
    sums = p.place("h_sums", [P, SEQ])
    shared_at = p.at
    rank_raw = p.place("h_rank_raw", [P, KT, GATE_RANK])
    rank_w = p.place("h_rank_w", [P, KT, P], F32R)
    p.at = shared_at
    e_q = p.place("h_e_q", [P, SEQ])
    e_k = p.place("h_e_k", [P, SEQ])
    chunk_end = p.place("h_chunk_end", [P, SEQ // CHUNK])
    q_out = [p.place(f"h_q_out{s}", [P, BLK]) for s in range(2)]
    k_out = [p.place(f"h_k_out{s}", [P, BLK]) for s in range(2)]
    kn_out = [p.place(f"h_kn_out{s}", [P, BLK]) for s in range(2)]
    g_out = [p.place(f"h_g_out{s}", [P, BLK]) for s in range(2)]

    loaded = p.sems("h_loaded", 2)
    rank_loaded, gk_loaded = p.sem("h_rank_loaded"), p.sem("h_gk_loaded")
    (zeroed, rank_hi, rank_lo, rank_mm, rank_ready, hi, lo, used, gk_mm, abs_done, min_done, ln_done, chain,
     sums_ready, exps_ready, qk_done, tiles_mm, turned, kn_copied, silu, g_done) = (
        p.sem(f"h_{n}") for n in (
            "zeroed", "rank_hi", "rank_lo", "rank_mm", "rank_ready", "hi", "lo", "used", "gk_mm", "abs",
            "min", "ln", "chain", "sums_ready", "exps_ready", "qk_done", "tiles_mm", "turned", "kn_copied", "silu",
            "g_done"))
    q_stored, k_stored, kn_stored, g_stored = (p.sems(f"h_{n}_stored", 2) for n in ("q", "k", "kn", "g"))
    w_src = a["gla_w_in"][0].rearrange("(k p) c -> p k c", p=P)
    gk_ps = p.ps[:, NB:2 * NB, :].rearrange("p b t -> p (b t)")
    CHAINED = 3

    def w_cols(h, j):
        return (h * DK, h * DK + KD, h * DV + 2 * KD + VD, h * DV + 2 * KD + VD + P)[j]

    with nc.Block() as block:

        @block.sync
        def _(sp):
            def load(h, j):
                sp.dma_start(raw[j % 2][:], w_src[:, :, ds(w_cols(h, j), P)]).then_inc(loaded[j % 2], DMA)

            def load_gk(h):
                for r in range(2):
                    sp.dma_start(w_gk[r * GATE_RANK:(r + 1) * GATE_RANK, :],
                                 a["gla_w_gk"][0][:, ds(h * DK, DK)]).then_inc(gk_loaded, DMA)

            def store(scratch, unit, n, out, sem):
                sp.dma_start(scratch[n * NB:(n + 1) * NB, :, ds(unit * P, P)].rearrange("t p c -> p t c"),
                             out[n % 2][:].rearrange("p (t c) -> p t c", c=P)).then_inc(sem[n % 2], DMA)

            def head(h, last):
                sp.wait_ge(lo, h * 4 + 1)
                load(h, 2)
                for n in range(NB):
                    sp.wait_ge(qk_done, h * 8 + n + 1)
                    store(p.q_tiles, h, n, q_out, q_stored)
                sp.wait_ge(lo, h * 4 + 2)
                load(h, 3)
                for n in range(NB):
                    sp.wait_ge(qk_done, h * 8 + NB + n + 1)
                    store(p.k_tiles, h, n, k_out, k_stored)
                if not last:
                    sp.wait_ge(gk_mm, h * NB + NB)
                    load_gk(h + 1)
                    sp.wait_ge(lo, h * 4 + 3)
                    load(h + 1, 0)
                for n in range(NB):
                    sp.wait_ge(g_done, h * 8 + n + 1)
                    store(p.g_tiles, h * 2, n, g_out, g_stored)
                if not last:
                    sp.wait_ge(lo, h * 4 + 4)
                    load(h + 1, 1)
                for n in range(NB):
                    sp.wait_ge(kn_copied, h * NB + n + 1)
                    store(p.kn_tiles, h, n, kn_out, kn_stored)
                for n in range(NB):
                    sp.wait_ge(g_done, h * 8 + NB + n + 1)
                    store(p.g_tiles, h * 2 + 1, n, g_out, g_stored)

            with nc.allow_non_contiguous_dma(reason="16 columns of the gates' first factor"):
                sp.dma_start(rank_raw[:], w_src[:, :, 2 * KD + 2 * VD:2 * KD + 2 * VD + GATE_RANK]
                             ).then_inc(rank_loaded, DMA)
            load_gk(0)
            load(0, 0)
            load(0, 1)
            with sp.Fori(0, HEADS - 1) as h:
                head(h, False)
            head(HEADS - 1, True)
            for s in range(2):
                for sem, units in ((q_stored, 1), (k_stored, 1), (kn_stored, 1), (g_stored, 2)):
                    sp.wait_ge(sem[s], HEADS * units * NB // 2 * DMA)

        @block.tensor
        def _(pe):
            pe.wait_ge(rank_lo, 1)
            for n in range(NB):
                for k in range(KT):
                    nc.tensor.matmul(p.ps[:, n, :], rank_w[:, k, :], p.x_hi[:, k, n * BLK:(n + 1) * BLK],
                                     start=k == 0, stop=False)
                    last = nc.tensor.matmul(p.ps[:, n, :], rank_w[:, k, :], p.x_lo[:, k, n * BLK:(n + 1) * BLK],
                                            start=False, stop=k == KT - 1)
                last.then_inc(rank_mm, 1)

            def tile(w, j, bank_free):
                pe.wait_ge(lo, w + 1)
                for n in range(NB):
                    pe.wait_ge(*bank_free(n))
                    for k in range(KT):
                        last = split_product(nc, p.ps[:, n, :], w_hi[j % 2][:, k, :], w_lo[j % 2][:, k, :],
                                             p.x_hi[:, k, n * BLK:(n + 1) * BLK],
                                             p.x_lo[:, k, n * BLK:(n + 1) * BLK], k == 0, k == KT - 1)
                    last.then_inc(tiles_mm, 1)

            with pe.Fori(0, HEADS) as h:
                pe.wait_ge(gk_loaded, (h + 1) * 2 * DMA)
                pe.wait_ge(rank_ready, NB)
                pe.wait_ge(kn_copied, h * NB)
                for n in range(NB):
                    nc.tensor.matmul(p.ps[:, NB + n, :], w_gk[:], rank[:, n * BLK:(n + 1) * BLK],
                                     start=True, stop=True).then_inc(gk_mm, 1)
                tile(h * 4, 0, lambda n: (g_done, h * 8))
                tile(h * 4 + 1, 1, lambda n: (qk_done, h * 8 + n + 1))
                tile(h * 4 + 2, 2, lambda n: (qk_done, h * 8 + NB + n + 1))
                for n in range(NB):
                    pe.wait_ge(qk_done, h * 8 + NB + n + 1)
                    for c in range(NB):
                        last = nc.tensor.transpose(p.ps[:, NB + n, c * P:(c + 1) * P],
                                                   sums[:, (n * NB + c) * P:(n * NB + c + 1) * P], p.ident[:])
                    last.then_inc(turned, 1)
                tile(h * 4 + 3, 3, lambda n: (silu, h * 8 + n + 1))

        @block.scalar
        def _(act):
            act.wait_ge(rank_loaded, DMA)
            act.wait_ge(zeroed, 1)
            nc.scalar.activation(rank_w[:, :, 0:GATE_RANK], rank_raw[:], ACT.Copy).then_inc(rank_hi, 1)
            act.wait_ge(loaded[0], DMA)
            nc.scalar.activation(w_hi[0][:], raw[0][:], ACT.Copy).then_inc(hi, 1)
            for n in range(NB):
                act.wait_ge(rank_mm, n + 1)
                nc.scalar.activation(rank[:, n * BLK:(n + 1) * BLK], p.ps[0:2 * GATE_RANK, n, :],
                                     ACT.Copy).then_inc(rank_ready, 1)

            def part(h, j, w):
                act.wait_ge(loaded[j % 2], (h * 2 + j // 2 + 1) * DMA)
                if isinstance(w, int) and w < 2:
                    pass
                else:
                    act.wait_ge(tiles_mm, (w - 1) * NB)
                nc.scalar.activation(w_hi[j % 2][:], raw[j % 2][:], ACT.Copy).then_inc(hi, 1)

            def head(h, last):
                act.wait_ge(gk_mm, h * NB + NB)
                act.wait_ge(qk_done, h * 8)
                nc.scalar.activation(e_q[:], gk_ps, ACT.Abs, bias=p.b_gk[:, ds(h, 1)]).then_inc(abs_done, 1)
                act.wait_ge(abs_done, h + 1)
                nc.scalar.activation(e_q[:], e_q[:], ACT.Exp, scale=-1.0).then_inc(ln_done, 1)
                act.wait_ge(ln_done, h * 2 + 1)
                nc.scalar.activation(e_q[:], e_q[:], ACT.Ln, bias=1.0).then_inc(ln_done, 1)
                act.wait_ge(loaded[1], (h * 2 + 1) * DMA)
                act.wait_ge(tiles_mm, h * 4 * NB)
                nc.scalar.activation(w_hi[1][:], raw[1][:], ACT.Copy).then_inc(hi, 1)
                act.wait_ge(sums_ready, h + 1)
                nc.scalar.activation(e_q[:], sums[:], ACT.Exp, scale=1.0 / GATE_NORMALIZER)
                nc.scalar.activation(e_k[:], sums[:], ACT.Exp, scale=-1.0 / GATE_NORMALIZER)
                nc.scalar.activation(p.decay[:, ds(h, 1), :].rearrange("p o c -> p (o c)"), chunk_end[:], ACT.Exp,
                                     scale=1.0 / GATE_NORMALIZER).then_inc(exps_ready, 1)
                act.wait_ge(chain, h * CHAINED + 3)
                nc.scalar.activation(sums[:], sums[:], ACT.Exp, scale=1.0 / GATE_NORMALIZER).then_inc(exps_ready, 1)
                part(h, 2, h * 4 + 2)
                part(h, 3, h * 4 + 3)

                def gate(j, n):
                    act.wait_ge(tiles_mm, (h * 4 + j) * NB + n + 1)
                    act.wait_ge(g_stored[n % 2], (h * 4 + (j - 2) * 2 + n // 2) * DMA)
                    nc.scalar.activation(g_out[n % 2][:], p.ps[:, n, :], ACT.Silu).then_inc(silu, 1)

                for n in range(NB):
                    gate(2, n)
                if not last:
                    part(h + 1, 0, h * 4 + 4)
                for n in range(NB):
                    act.wait_ge(turned, h * NB + n + 1)
                    act.wait_ge(kn_stored[n % 2], (h * 2 + n // 2) * DMA)
                    nc.scalar.activation(kn_out[n % 2][:], p.ps[:, NB + n, :], ACT.Copy).then_inc(kn_copied, 1)
                for n in range(NB):
                    gate(3, n)

            with act.Fori(0, HEADS - 1) as h:
                head(h, False)
            head(HEADS - 1, True)

        @block.vector
        def _(dve):
            nc.vector.memset(rank_w[:].bitcast(F32), 0.0).then_inc(zeroed, 1)
            dve.wait_ge(rank_hi, 1)
            nc.vector.tensor_tensor(rank_w[:, :, GATE_RANK:2 * GATE_RANK], rank_raw[:],
                                    rank_w[:, :, 0:GATE_RANK].bitcast(F32), ALU.subtract).then_inc(rank_lo, 1)

            def part(w, s):
                dve.wait_ge(hi, w + 1)
                nc.vector.tensor_tensor(w_lo[s][:], raw[s][:], w_hi[s][:].bitcast(F32), ALU.subtract).then_inc(lo, 1)

            def head(h, last):
                dve.wait_ge(abs_done, h + 1)
                dve.wait_ge(qk_done, h * 8)
                dve.wait_ge(turned, h * NB)
                nc.vector.tensor_scalar(e_k[:], gk_ps, p.b_gk[:, ds(h, 1)], 0.0, ALU.add, ALU.min).then_inc(chain, 1)
                dve.wait_ge(ln_done, h * 2 + 2)
                dve.wait_ge(chain, h * CHAINED + 1)
                nc.vector.tensor_tensor(e_k[:], e_k[:], e_q[:], ALU.subtract).then_inc(chain, 1)
                part(h * 4 + 1, 1)
                dve.wait_ge(chain, h * CHAINED + 2)
                for n in range(NB):
                    cols = slice(n * BLK, (n + 1) * BLK)
                    scan = nc.vector.tensor_tensor_scan(sums[:, cols], p.keep[:], e_k[:, cols], 0.0, ALU.mult, ALU.add)
                scan.then_inc(min_done, 1)
                dve.wait_ge(min_done, h + 1)
                by_chunk = sums[:].rearrange("p (c s) -> p c s", s=CHUNK)
                nc.vector.tensor_copy(chunk_end[:], by_chunk[:, :, CHUNK - 1]).then_inc(sums_ready, 1)
                dve.wait_ge(sums_ready, h + 1)
                dve.wait_ge(exps_ready, h * 2 + 1)
                nc.vector.tensor_tensor(by_chunk, chunk_end[:].unsqueeze(2).to_broadcast([P, SEQ // CHUNK, CHUNK]),
                                        by_chunk, ALU.subtract).then_inc(chain, 1)
                for n in range(NB):
                    dve.wait_ge(tiles_mm, h * 4 * NB + n + 1)
                    dve.wait_ge(q_stored[n % 2], (h * 2 + n // 2) * DMA)
                    nc.vector.scalar_tensor_tensor(out=q_out[n % 2][:], in0=p.ps[:, n, :], scalar=float(DK) ** -0.5,
                                                   in1=e_q[:, n * BLK:(n + 1) * BLK], op0=ALU.mult, op1=ALU.mult
                                                   ).then_inc(qk_done, 1)
                part(h * 4 + 2, 0)
                dve.wait_ge(exps_ready, h * 2 + 2)
                for n in range(NB):
                    cols = slice(n * BLK, (n + 1) * BLK)
                    dve.wait_ge(tiles_mm, (h * 4 + 1) * NB + n + 1)
                    dve.wait_ge(k_stored[n % 2], (h * 2 + n // 2) * DMA)
                    nc.vector.tensor_tensor(k_out[n % 2][:], p.ps[:, n, :], e_k[:, cols], ALU.mult)
                    nc.vector.tensor_tensor(sums[:, cols], p.ps[:, n, :], sums[:, cols], ALU.mult).then_inc(qk_done, 1)
                part(h * 4 + 3, 1)

                def gate(j, n):
                    dve.wait_ge(silu, h * 8 + (j - 2) * NB + n + 1)
                    nc.vector.tensor_scalar(g_out[n % 2][:], g_out[n % 2][:], p.norm_w[:, j - 2:j - 1], None,
                                            ALU.mult).then_inc(g_done, 1)

                for n in range(NB):
                    gate(2, n)
                if not last:
                    part(h * 4 + 4, 0)
                for n in range(NB):
                    gate(3, n)

            dve.wait_ge(hi, 1)
            nc.vector.tensor_tensor(w_lo[0][:], raw[0][:], w_hi[0][:].bitcast(F32), ALU.subtract).then_inc(lo, 1)
            with dve.Fori(0, HEADS - 1) as h:
                head(h, False)
            head(HEADS - 1, True)


def attend_and_norm(nc, p, a):
    p.at = p.ln_at
    ln_g = p.place("a_ln_g", [P, D])
    ln_b = p.place("a_ln_b", [P, D])
    raw = [p.place(f"a_raw{s}", [P, D]) for s in range(2)]
    w_hi = p.place("a_w_hi", [P, KT, D], F32R)
    w_lo = p.place("a_w_lo", [P, KT, D], F32R)
    q, k, kn, scores = ([p.place(f"a_{n}{s}", [P, KD]) for s in range(2)] for n in ("q", "k", "kn", "scores"))
    v, g, x = ([p.place(f"a_{n}{s}", [P, D]) for s in range(2)] for n in ("v", "g", "x"))
    STATES = 4
    state = [p.place(f"a_state{s}", [P, VD]) for s in range(STATES)]
    square = p.place("a_square", [P, VD])
    rms = p.place("a_rms", [P, HEADS, P])
    gated = p.place("a_gated", [P, VD])
    o_hi = [p.place(f"a_o_hi{s}", [P, KT, P], F32R) for s in range(2)]
    o_lo = [p.place(f"a_o_lo{s}", [P, KT, P], F32R) for s in range(2)]
    res = p.place("a_res", [P, D])
    stats = p.place("a_stats", [P, 2, 6])
    moments = p.place("a_moments", [P, 2])
    rstd = p.place("a_rstd", [P, 1])
    out = [p.place(f"a_out{s}", [P, D]) for s in range(2)]

    ln_loaded = p.sem("a_ln_loaded")
    raw_loaded, in_loaded, g_loaded, x_loaded, out_stored = (
        p.sems(f"a_{n}", 2) for n in ("raw_loaded", "in_loaded", "g_loaded", "x_loaded", "out_stored"))
    (w_hi_done, w_lo_done, zeroed, scored, masked, kv_mm, states, o_mm, squared, summed, rms_mid, rms_done, o_read,
     gated_done, o_hi_done, o_lo_done, y_mm, y_read, stats_done, moments_done, rstd_mid, rstd_done, normed,
     scaled, out_done) = (
        p.sem(f"a_{n}") for n in (
            "w_hi_done", "w_lo_done", "zeroed", "scored", "masked", "kv_mm", "states", "o_mm", "squared", "summed",
            "rms_mid", "rms_done", "o_read", "gated_done", "o_hi_done", "o_lo_done", "y_mm", "y_read", "stats_done",
            "moments_done", "rstd_mid", "rstd_done", "normed", "scaled", "out_done"))

    w_src = a["gla_w_out"][0].rearrange("(k p) c -> p k c", p=P)
    score_ps = p.ps[:, 0, :]
    o_ps = p.ps[:, 1:3, :].rearrange("p b c -> p (b c)")
    kv_ps = p.ps[:, 3:5, :].rearrange("p b c -> p (b c)")
    sum_ps = p.ps[:, 5, :]
    y_ps = [p.ps[:, 6 + half, :] for half in range(2)]
    LAG = 2

    def run(engine, step):
        for t in range(LAG):
            step(t, t % 2, t, t // 2)
        with engine.Fori(LAG // 2, NT // 2) as pair:
            for s in range(2):
                step(pair * 2 + s, s, LAG, pair)
        for t in range(NT, NT + LAG):
            step(t, t % 2, LAG, t // 2)

    with nc.Block() as block:

        @block.sync
        def _(sp):
            def load(t, s):
                for dst, src in ((q, p.q_tiles), (k, p.k_tiles), (kn, p.kn_tiles), (v, p.v_tiles)):
                    sp.dma_start(dst[s][:], src[ds(t, 1), :, :].rearrange("o p c -> (o p) c")).then_inc(in_loaded[s], DMA)

            def load_g(t, s):
                sp.dma_start(g[s][:], p.g_tiles[ds(t, 1), :, :].rearrange("o p c -> (o p) c")).then_inc(g_loaded[s], DMA)

            def load_x(t, s):
                sp.dma_start(x[s][:], a["x"][0][ds(t * P, P), :]).then_inc(x_loaded[s], DMA)

            load(0, 0)
            load_g(0, 0)
            load(1, 1)
            load_g(1, 1)
            load_x(0, 0)
            load_x(1, 1)
            for kt in range(KT):
                if kt >= 2:
                    sp.wait_ge(w_lo_done, kt - 1)
                sp.dma_start(raw[kt % 2][:], w_src[:, kt, :]).then_inc(raw_loaded[kt % 2], DMA)
            for n, ln in enumerate((ln_g, ln_b)):
                row = a["ln_g" if n == 0 else "ln_b"][0:1, :]
                sp.dma_start(ln[:], row.to_broadcast([P, D])).then_inc(ln_loaded, DMA)

            def step(t, s, lag):
                static = isinstance(t, int)
                if not static or t + 2 < NT:
                    sp.wait_ge(o_mm, t + 1)
                    load(t + 2, s)
                if lag >= LAG:
                    u = t - LAG
                    sp.wait_ge(out_done, u + 1)
                    sp.dma_start(p.x1[ds(u * P, P), :], out[s][:]).then_inc(out_stored[s], DMA)
                    if not static:
                        load_x(u + 2, s)
                if static and t >= NT:
                    return
                if not static or t + 2 < NT:
                    sp.wait_ge(gated_done, t + 1)
                    load_g(t + 2, s)

            for t in range(LAG):
                step(t, t % 2, t)
            with sp.Fori(LAG // 2, NT // 2 - 1) as u:
                for s in range(2):
                    step(u * 2 + s, s, LAG)
            for t in range(NT - 2, NT + LAG):
                if t < NT:
                    sp.wait_ge(out_done, t - LAG + 1)
                    sp.dma_start(p.x1[(t - LAG) * P:(t - LAG + 1) * P, :], out[t % 2][:]).then_inc(out_stored[t % 2], DMA)
                    load_x(t, t % 2)
                else:
                    step(t, t % 2, t)
            for s in range(2):
                sp.wait_ge(out_stored[s], NT // 2 * DMA)

        @block.tensor
        def _(pe):
            def y_half(t, s, half):
                u = t - LAG
                if half == 0:
                    pe.wait_ge(o_lo_done, u + 1)
                    pe.wait_ge(w_lo_done, KT)
                    pe.wait_ge(y_read, u * 2)
                for kt in range(KT):
                    last = split_product(nc, y_ps[half], o_hi[s][:, kt, :], o_lo[s][:, kt, :],
                                         w_hi[:, kt, half * BLK:(half + 1) * BLK],
                                         w_lo[:, kt, half * BLK:(half + 1) * BLK], kt == 0, kt == KT - 1)
                last.then_inc(y_mm, 1)

            def kv(s, c):
                rows = slice(c * CHUNK, (c + 1) * CHUNK)
                for h in range(HEADS):
                    last = nc.tensor.matmul(kv_ps[:, h * DV:(h + 1) * DV], kn[s][rows, h * DK:(h + 1) * DK],
                                            v[s][rows, h * DV:(h + 1) * DV], start=True, stop=True)
                last.then_inc(kv_mm, 1)

            def inter(s, c, b, last_group):
                st = state[(2 * s + c) % STATES]
                for j in range(4 * b, 4 * b + 4):
                    cols = slice(j * P + c * CHUNK, j * P + (c + 1) * CHUNK)
                    h = j // 2
                    last = nc.tensor.matmul(o_ps[:, cols], st[:, j * P:(j + 1) * P],
                                            q[s][:, h * DK + c * CHUNK:h * DK + (c + 1) * CHUNK],
                                            start=False, stop=last_group, skip_group_check=True)
                return last

            def step(t, s, lag, pair):
                attends = not (isinstance(t, int) and t >= NT)
                if attends:
                    pe.wait_ge(in_loaded[s], (pair + 1) * (4 * DMA))
                    pe.wait_ge(masked, t)
                    for h in range(HEADS):
                        last = nc.tensor.matmul(score_ps[:, h * P:(h + 1) * P], k[s][:, h * P:(h + 1) * P],
                                                q[s][:, h * P:(h + 1) * P], start=True, stop=True)
                    last.then_inc(scored, 1)
                    pe.wait_ge(states, t * 2)
                    kv(s, 0)
                if lag >= 1 and not (isinstance(t, int) and t > NT):
                    pe.wait_ge(squared, t)
                    pe.wait_ge(rms_mid, t - 1)
                    for h in range(HEADS):
                        for j in range(2):
                            last = nc.tensor.matmul(sum_ps[:, h * P:(h + 1) * P], p.mean_w[:],
                                                    square[:, (2 * h + j) * P:(2 * h + j + 1) * P],
                                                    start=j == 0, stop=j == 1)
                    last.then_inc(summed, 1)
                if lag >= LAG:
                    y_half(t, s, 0)
                if attends:
                    pe.wait_ge(masked, t + 1)
                    pe.wait_ge(zeroed, 1)
                    pe.wait_ge(o_read, t)
                    for b in range(2):
                        for j in range(4 * b, 4 * b + 4):
                            h = j // 2
                            nc.tensor.matmul(o_ps[:, j * P:(j + 1) * P], v[s][:, j * P:(j + 1) * P],
                                             scores[s][:, h * P:(h + 1) * P], start=j == 4 * b, stop=False,
                                             skip_group_check=True)
                        inter(s, 0, b, False)
                    pe.wait_ge(states, t * 2 + 1)
                    kv(s, 1)
                if lag >= LAG:
                    y_half(t, s, 1)
                if attends:
                    inter(s, 1, 0, True)
                    inter(s, 1, 1, True).then_inc(o_mm, 1)

            run(pe, step)

        @block.scalar
        def _(act):
            for kt in range(KT):
                act.wait_ge(raw_loaded[kt % 2], (kt // 2 + 1) * DMA)
                nc.scalar.activation(w_hi[:, kt, :], raw[kt % 2][:], ACT.Copy).then_inc(w_hi_done, 1)

            def step(t, s, lag, pair):
                if lag >= 1 and not (isinstance(t, int) and t > NT):
                    u = t - 1
                    act.wait_ge(summed, t)
                    act.wait_ge(o_read, u)
                    nc.scalar.activation(rms[:].rearrange("p h c -> p (h c)"), sum_ps, ACT.Ln,
                                         bias=p.eps_rms[:]).then_inc(rms_mid, 1)
                    act.wait_ge(rms_mid, t)
                    nc.scalar.activation(rms[:], rms[:], ACT.Exp, scale=-0.5).then_inc(rms_done, 1)
                    act.wait_ge(gated_done, t)
                    if lag >= LAG:
                        act.wait_ge(y_mm, t * 2 - 4)
                    nc.scalar.activation(o_hi[1 - s][:].rearrange("p k c -> p (k c)"), gated[:], ACT.Copy
                                         ).then_inc(o_hi_done, 1)
                if not (isinstance(t, int) and t >= NT):
                    act.wait_ge(o_mm, t + 1)
                    nc.scalar.activation(square[:], o_ps, ACT.Square).then_inc(squared, 1)
                if lag >= LAG:
                    u = t - LAG
                    act.wait_ge(moments_done, u + 1)
                    nc.scalar.activation(rstd[:], moments[:, 1:2], ACT.Ln, bias=p.eps_ln[:]).then_inc(rstd_mid, 1)
                    act.wait_ge(rstd_mid, u + 1)
                    nc.scalar.activation(rstd[:], rstd[:], ACT.Exp, scale=-0.5).then_inc(rstd_done, 1)

            run(act, step)

        @block.vector
        def _(dve):
            for s in range(2):
                nc.vector.memset(scores[s][:], 0.0)
            nc.vector.memset(state[0][:], 0.0).then_inc(zeroed, 1)
            for kt in range(KT):
                dve.wait_ge(w_hi_done, kt + 1)
                nc.vector.tensor_tensor(w_lo[:, kt, :], raw[kt % 2][:], w_hi[:, kt, :].bitcast(F32),
                                        ALU.subtract).then_inc(w_lo_done, 1)
            dve.wait_ge(zeroed, 1)
            dve.wait_ge(ln_loaded, 2 * DMA)

            def advance(t, s, c):
                now, then = state[(2 * s + c) % STATES], state[(2 * s + c + 1) % STATES]
                dve.wait_ge(kv_mm, t * 2 + c + 1)
                dve.wait_ge(states, t * 2 + c)
                for h in range(HEADS):
                    cols = slice(h * DV, (h + 1) * DV)
                    last = nc.vector.scalar_tensor_tensor(
                        out=then[:, cols], in0=now[:, cols], scalar=p.decay[:, h, ds(t * 2 + c, 1)],
                        in1=kv_ps[:, cols], op0=ALU.mult, op1=ALU.add)
                last.then_inc(states, 1)

            def step(t, s, lag, pair):
                attends = not (isinstance(t, int) and t >= NT)
                if attends:
                    dve.wait_ge(scored, t + 1)
                    nc.vector.memset(p.carrier[:], 0.0)
                    nc.vector.copy_predicated(scores[s][:], p.mask[:].rearrange("p h c -> p (h c)").bitcast(I32),
                                              score_ps).then_inc(masked, 1)
                    advance(t, s, 0)
                gates = lag >= 1 and not (isinstance(t, int) and t > NT)
                if gates:
                    dve.wait_ge(rms_done, t)
                    dve.wait_ge(o_lo_done, t - 1)
                    split = lambda ap: ap.rearrange("p (h j c) -> p h j c", j=2, c=P)
                    nc.vector.tensor_tensor(split(gated[:]), split(o_ps),
                                            rms[:].unsqueeze(2).to_broadcast([P, HEADS, 2, P]), ALU.mult
                                            ).then_inc(o_read, 1)
                    dve.wait_ge(o_read, t)
                    dve.wait_ge(g_loaded[1 - s], (pair + s) * DMA)
                    nc.vector.tensor_tensor(gated[:], gated[:], g[1 - s][:], ALU.mult).then_inc(gated_done, 1)
                if attends:
                    advance(t, s, 1)
                if gates:
                    dve.wait_ge(o_hi_done, t)
                    dve.wait_ge(gated_done, t)
                    nc.vector.tensor_tensor(o_lo[1 - s][:].rearrange("p k c -> p (k c)"), gated[:],
                                            o_hi[1 - s][:].rearrange("p k c -> p (k c)").bitcast(F32), ALU.subtract
                                            ).then_inc(o_lo_done, 1)
                if lag >= LAG:
                    u = t - LAG
                    dve.wait_ge(x_loaded[s], pair * DMA)
                    dve.wait_ge(normed, u)
                    for half in range(2):
                        cols = slice(half * BLK, (half + 1) * BLK)
                        dve.wait_ge(y_mm, u * 2 + half + 1)
                        nc.vector.scalar_tensor_tensor(out=res[:, cols], in0=x[s][:, cols], scalar=ALPHA,
                                                       in1=y_ps[half], op0=ALU.mult, op1=ALU.add).then_inc(y_read, 1)
                        dve.wait_ge(y_read, u * 2 + half + 1)
                        nc.vector.bn_stats(stats[:, half, :], res[:, cols]).then_inc(stats_done, 1)
                    dve.wait_ge(stats_done, u * 2 + 2)
                    nc.vector.memset(p.carrier[:], 0.0)
                    nc.vector.bn_aggr(moments[:], stats[:].rearrange("p a b -> p (a b)")).then_inc(moments_done, 1)
                    dve.wait_ge(rstd_done, u + 1)
                    dve.wait_ge(moments_done, u + 1)
                    dve.wait_ge(out_stored[s], (pair - 1) * DMA)
                    nc.vector.tensor_scalar(out[s][:], res[:], moments[:, 0:1], rstd[:, 0:1], ALU.subtract, ALU.mult
                                            ).then_inc(normed, 1)
                    dve.wait_ge(normed, u + 1)
                    nc.vector.tensor_tensor(out[s][:], out[s][:], ln_g[:], ALU.mult).then_inc(scaled, 1)
                    dve.wait_ge(scaled, u + 1)
                    nc.vector.tensor_tensor(out[s][:], out[s][:], ln_b[:], ALU.add).then_inc(out_done, 1)

            run(dve, step)


def pool_mix(nc, p, a):
    p.at = p.stream_at
    raw = [p.place(f"m_raw{s}", [P, KT, P]) for s in range(2)]
    w_hi = [p.place(f"m_w_hi{s}", [P, KT, P], F32R) for s in range(2)]
    w_lo = [p.place(f"m_w_lo{s}", [P, KT, P], F32R) for s in range(2)]
    h_in, win_a, win_b = (p.place(f"m_{n}", [P, PAD + SEQ]) for n in ("h", "win_a", "win_b"))
    z = p.place("m_z", [P, SEQ])
    loaded = p.sems("m_loaded", 2)
    stored = p.sem("m_stored")
    hi, lo, h_mm, z_mm, h_copied, silu, chain, pooled, mixed = (
        p.sem(f"m_{n}") for n in ("hi", "lo", "h_mm", "z_mm", "h_copied", "silu", "chain", "pooled", "mixed"))
    z_src = a["pool_w_in"][0].rearrange("(k p) c -> p k c", p=P)

    with nc.Block() as block:

        @block.sync
        def _(sp):
            def load(m):
                sp.dma_start(raw[0][:], p.w_fused[ds(m, 1), :, :, :].rearrange("o p k c -> (o p) k c")
                             ).then_inc(loaded[0], DMA)

            def load_z(m):
                sp.dma_start(raw[1][:], z_src[:, :, ds(m * P + POOL_W, P)]).then_inc(loaded[1], DMA)

            load(0)
            load_z(0)
            with sp.Fori(1, MT) as m:
                sp.wait_ge(lo, m * 2 - 1)
                load(m)
                sp.wait_ge(lo, m * 2)
                load_z(m)
                sp.wait_ge(mixed, m)
                sp.dma_start(p.mixed[ds(m - 1, 1), :, :].rearrange("o p c -> (o p) c"), z[:]).then_inc(stored, DMA)
            sp.wait_ge(mixed, MT)
            sp.dma_start(p.mixed[MT - 1, :, :], z[:]).then_inc(stored, DMA)
            sp.wait_ge(stored, MT * DMA)

        @block.tensor
        def _(pe):
            with pe.Fori(0, MT) as m:
                for s, done, free in ((0, h_mm, h_copied), (1, z_mm, silu)):
                    pe.wait_ge(lo, m * 2 + s + 1)
                    pe.wait_ge(free, m * NB)
                    for n in range(NB):
                        for k in range(KT):
                            last = split_product(nc, p.ps[:, s * NB + n, :], w_hi[s][:, k, :], w_lo[s][:, k, :],
                                                 p.x_hi[:, k, n * BLK:(n + 1) * BLK],
                                                 p.x_lo[:, k, n * BLK:(n + 1) * BLK], k == 0, k == KT - 1)
                        last.then_inc(done, 1)

        @block.scalar
        def _(act):
            act.wait_ge(loaded[0], DMA)
            nc.scalar.activation(w_hi[0][:], raw[0][:], ACT.Copy).then_inc(hi, 1)

            def tile(m, last):
                act.wait_ge(loaded[1], (m + 1) * DMA)
                act.wait_ge(z_mm, m * NB)
                nc.scalar.activation(w_hi[1][:], raw[1][:], ACT.Copy).then_inc(hi, 1)
                act.wait_ge(pooled, m)
                for n in range(NB):
                    act.wait_ge(h_mm, m * NB + n + 1)
                    nc.scalar.activation(h_in[:, PAD + n * BLK:PAD + (n + 1) * BLK], p.ps[:, n, :],
                                         ACT.Copy).then_inc(h_copied, 1)
                if not last:
                    act.wait_ge(loaded[0], (m + 2) * DMA)
                    nc.scalar.activation(w_hi[0][:], raw[0][:], ACT.Copy).then_inc(hi, 1)
                act.wait_ge(stored, m * DMA)
                for n in range(NB):
                    act.wait_ge(z_mm, m * NB + n + 1)
                    nc.scalar.activation(z[:, n * BLK:(n + 1) * BLK], p.ps[:, NB + n, :], ACT.Silu).then_inc(silu, 1)

            with act.Fori(0, MT - 1) as m:
                tile(m, False)
            tile(MT - 1, True)

        @block.vector
        def _(dve):
            for n, t in enumerate((h_in, win_a, win_b)):
                last = nc.vector.memset(t[:, 0:PAD], 0.0)
            last.then_inc(chain, 1)
            dve.wait_ge(chain, 1)
            dve.wait_ge(hi, 1)
            nc.vector.tensor_tensor(w_lo[0][:], raw[0][:], w_hi[0][:].bitcast(F32), ALU.subtract).then_inc(lo, 1)
            body = slice(PAD, PAD + SEQ)
            base = 1

            def tile(m, g, base, last):
                dve.wait_ge(hi, m * 2 + 2)
                nc.vector.tensor_tensor(w_lo[1][:], raw[1][:], w_hi[1][:].bitcast(F32), ALU.subtract).then_inc(lo, 1)
                if not last:
                    dve.wait_ge(hi, m * 2 + 3)
                    nc.vector.tensor_tensor(w_lo[0][:], raw[0][:], w_hi[0][:].bitcast(F32), ALU.subtract).then_inc(lo, 1)
                dve.wait_ge(mixed, m)
                dve.wait_ge(h_copied, m * NB + NB)
                src, step = h_in, 1
                for i in range(g + 1):
                    dst = (win_a, win_b)[i % 2]
                    nc.vector.tensor_tensor(dst[:, body], src[:, body], src[:, PAD - step:PAD + SEQ - step],
                                            ALU.add).then_inc(chain, 1)
                    dve.wait_ge(chain, base + i + 1)
                    src, step = dst, step * 2
                nc.vector.tensor_tensor(src[:, PAD:2 * PAD], src[:, PAD:2 * PAD], p.correct[:, g, :],
                                        ALU.mult).then_inc(chain, 1)
                dve.wait_ge(chain, base + g + 2)
                other = win_b if src is win_a else win_a
                nc.vector.scalar_tensor_tensor(out=other[:, body], in0=src[:, body], scalar=1.0 / WINDOWS[g],
                                               in1=h_in[:, body], op0=ALU.mult, op1=ALU.subtract).then_inc(pooled, 1)
                dve.wait_ge(pooled, m + 1)
                nc.vector.tensor_scalar(other[:, body], other[:, body], p.b_grp[:, ds(m, 1)], p.scale[:, ds(m, 1)],
                                        ALU.add, ALU.mult).then_inc(chain, 1)
                dve.wait_ge(chain, base + g + 3)
                dve.wait_ge(silu, m * NB + NB)
                nc.vector.tensor_tensor(z[:], z[:], other[:, body], ALU.mult).then_inc(mixed, 1)

            for g in range(GROUPS):
                per_tile = g + 3
                rolled = GT - 1 if g == GROUPS - 1 else GT
                with dve.Fori(0, rolled) as i:
                    tile(i + g * GT, g, i * per_tile + base, False)
                if rolled < GT:
                    tile(MT - 1, g, base + rolled * per_tile, True)
                base += GT * per_tile


def pool_out_and_norm(nc, p, a, out_dram):
    p.at = p.ln_at
    ln_g = p.place("o_ln_g", [P, D])
    ln_b = p.place("o_ln_b", [P, D])
    w_hi = p.place("o_w_hi", [P, MT, D], F32R)
    w_lo = p.place("o_w_lo", [P, MT, D], F32R)
    raw = [p.place(f"o_raw{s}", [P, D]) for s in range(2)]
    SLOTS = 4
    m_raw = [p.place(f"o_m_raw{s}", [P, BLK]) for s in range(SLOTS)]
    m_hi = [p.place(f"o_m_hi{s}", [P, BLK], F32R) for s in range(SLOTS)]
    m_lo = [p.place(f"o_m_lo{s}", [P, BLK], F32R) for s in range(SLOTS)]
    x = [p.place(f"o_x{s}", [P, D]) for s in range(2)]
    res = [p.place(f"o_res{s}", [P, D]) for s in range(NB)]
    stats = p.place("o_stats", [P, 2, 6])
    moments = p.place("o_moments", [P, 2])
    rstd = p.place("o_rstd", [P, 1])
    ln_loaded = p.sem("o_ln_loaded")
    raw_loaded, x_loaded = p.sems("o_raw_loaded", 2), p.sems("o_x_loaded", 2)
    m_loaded, stored = p.sems("o_m_loaded", SLOTS), p.sems("o_stored", NB)
    (w_hi_done, w_lo_done, hi, lo, step_mm, y_mm, y_read, stats_done, moments_done, rstd_mid, rstd_done, normed,
     scaled, out_done) = (
        p.sem(f"o_{n}") for n in ("w_hi_done", "w_lo_done", "hi", "lo", "step_mm", "y_mm", "y_read", "stats_done",
                                  "moments_done", "rstd_mid", "rstd_done", "normed", "scaled", "out_done"))
    TB = BLK // P
    w_src = a["pool_w_out"][0].rearrange("(k p) c -> p k c", p=P)
    RESIDUAL_AFTER = {3: (0, 1), 5: (2, 3)}
    NORM_AT = {4: 0, 7: 1, 10: 2, 13: 3}
    STORE_AFTER = {7: 0, 10: 1, 13: 2, 15: 3}

    with nc.Block() as block:

        @block.sync
        def _(sp):
            def load_m(b, k):
                sp.dma_start(m_raw[k % SLOTS][:], p.mixed[k, :, ds(b * BLK, BLK)]).then_inc(m_loaded[k % SLOTS], DMA)

            def load_x(t, s):
                sp.dma_start(x[s][:], p.x1[ds(t * P, P), :]).then_inc(x_loaded[s], DMA)

            for k in range(MT):
                if k >= SLOTS:
                    sp.wait_ge(lo, k - SLOTS + 1)
                load_m(0, k)
                if k >= 2:
                    sp.wait_ge(w_lo_done, k - 1)
                sp.dma_start(raw[k % 2][:], w_src[:, k, :]).then_inc(raw_loaded[k % 2], DMA)
            for ln, src in ((ln_g, a["ln_g"]), (ln_b, a["ln_b"])):
                sp.dma_start(ln[:], src[1:2, :].to_broadcast([P, D])).then_inc(ln_loaded, DMA)
            load_x(0, 0)
            load_x(1, 1)

            def outputs(b, i):
                sp.wait_ge(out_done, b * TB + i + 1)
                sp.dma_start(out_dram[ds((b * TB + i) * P, P), :], res[i][:]).then_inc(stored[i], DMA)

            with sp.Fori(1, NB) as b:
                for k in range(MT):
                    sp.wait_ge(lo, b * MT + k - SLOTS + 1)
                    load_m(b, k)
                    for i in RESIDUAL_AFTER.get(k, ()):
                        sp.wait_ge(y_read, ((b - 1) * TB + i + 1) * 2)
                        load_x((b - 1) * TB + i + 2, i % 2)
                    if k in STORE_AFTER:
                        outputs(b - 1, STORE_AFTER[k])
            for i in range(TB):
                if i < 2:
                    sp.wait_ge(y_read, ((NB - 1) * TB + i + 1) * 2)
                    load_x((NB - 1) * TB + i + 2, i % 2)
            for i in range(TB):
                outputs(NB - 1, i)
            for i in range(TB):
                sp.wait_ge(stored[i], NB * DMA)

        @block.tensor
        def _(pe):
            with pe.Fori(0, NB) as b:
                for k in range(MT):
                    pe.wait_ge(lo, b * MT + k + 1)
                    pe.wait_ge(w_lo_done, k + 1)
                    for i in range(TB):
                        for half in range(2):
                            if k == 0:
                                pe.wait_ge(y_read, b * TB * 2)
                            cols = slice(half * BLK, (half + 1) * BLK)
                            last = split_product(nc, p.ps[:, i * 2 + half, :],
                                                 m_hi[k % SLOTS][:, i * P:(i + 1) * P],
                                                 m_lo[k % SLOTS][:, i * P:(i + 1) * P],
                                                 w_hi[:, k, cols], w_lo[:, k, cols], k == 0, k == MT - 1)
                            if k == MT - 1:
                                last.then_inc(y_mm, 1)
                    if k < MT - 1:
                        last.then_inc(step_mm, 1)

        def norm_rstd(act, t):
            act.wait_ge(moments_done, t + 1)
            nc.scalar.activation(rstd[:], moments[:, 1:2], ACT.Ln, bias=p.eps_ln[:]).then_inc(rstd_mid, 1)
            act.wait_ge(rstd_mid, t + 1)
            nc.scalar.activation(rstd[:], rstd[:], ACT.Exp, scale=-0.5).then_inc(rstd_done, 1)

        STEPS = MT - 1

        @block.scalar
        def _(act):
            def part(b, k, first):
                act.wait_ge(m_loaded[k % SLOTS], (b * (MT // SLOTS) + k // SLOTS + 1) * DMA)
                if not (first and k < SLOTS):
                    if k >= SLOTS:
                        act.wait_ge(step_mm, b * STEPS + k - SLOTS + 1)
                    else:
                        act.wait_ge(step_mm, (b - 1) * STEPS + min(MT + k - SLOTS + 1, STEPS))
                        if MT + k - SLOTS == MT - 1:
                            act.wait_ge(y_mm, b * TB * 2)
                nc.scalar.activation(m_hi[k % SLOTS][:], m_raw[k % SLOTS][:], ACT.Copy).then_inc(hi, 1)

            for k in range(MT):
                part(0, k, True)
                act.wait_ge(raw_loaded[k % 2], (k // 2 + 1) * DMA)
                nc.scalar.activation(w_hi[:, k, :], raw[k % 2][:], ACT.Copy).then_inc(w_hi_done, 1)
            with act.Fori(1, NB) as b:
                for k in range(MT):
                    part(b, k, False)
                    if k in NORM_AT:
                        norm_rstd(act, (b - 1) * TB + NORM_AT[k])
            for i in range(TB):
                norm_rstd(act, (NB - 1) * TB + i)

        @block.vector
        def _(dve):
            def part(b, k):
                dve.wait_ge(hi, b * MT + k + 1)
                nc.vector.tensor_tensor(m_lo[k % SLOTS][:], m_raw[k % SLOTS][:], m_hi[k % SLOTS][:].bitcast(F32),
                                        ALU.subtract).then_inc(lo, 1)

            def residual(b, i):
                t = b * TB + i
                dve.wait_ge(x_loaded[i % 2], (b * (TB // 2) + i // 2 + 1) * DMA)
                dve.wait_ge(stored[i], b * DMA)
                for half in range(2):
                    cols = slice(half * BLK, (half + 1) * BLK)
                    dve.wait_ge(y_mm, t * 2 + half + 1)
                    nc.vector.scalar_tensor_tensor(out=res[i][:, cols], in0=x[i % 2][:, cols], scalar=ALPHA,
                                                   in1=p.ps[:, i * 2 + half, :], op0=ALU.mult, op1=ALU.add
                                                   ).then_inc(y_read, 1)

            def norm(b, i):
                t = b * TB + i
                dve.wait_ge(y_read, t * 2 + 2)
                for half in range(2):
                    nc.vector.bn_stats(stats[:, half, :], res[i][:, half * BLK:(half + 1) * BLK]).then_inc(stats_done, 1)
                dve.wait_ge(stats_done, t * 2 + 2)
                dve.wait_ge(normed, t)
                nc.vector.memset(p.carrier[:], 0.0)
                nc.vector.bn_aggr(moments[:], stats[:].rearrange("p a b -> p (a b)")).then_inc(moments_done, 1)
                dve.wait_ge(rstd_done, t + 1)
                nc.vector.tensor_scalar(res[i][:], res[i][:], moments[:, 0:1], rstd[:, 0:1], ALU.subtract, ALU.mult
                                        ).then_inc(normed, 1)
                dve.wait_ge(normed, t + 1)
                nc.vector.tensor_tensor(res[i][:], res[i][:], ln_g[:], ALU.mult).then_inc(scaled, 1)
                dve.wait_ge(scaled, t + 1)
                nc.vector.tensor_tensor(res[i][:], res[i][:], ln_b[:], ALU.add).then_inc(out_done, 1)

            for k in range(MT):
                part(0, k)
                dve.wait_ge(w_hi_done, k + 1)
                nc.vector.tensor_tensor(w_lo[:, k, :], raw[k % 2][:], w_hi[:, k, :].bitcast(F32),
                                        ALU.subtract).then_inc(w_lo_done, 1)
            dve.wait_ge(ln_loaded, 2 * DMA)
            with dve.Fori(1, NB) as b:
                for k in range(SLOTS - 1):
                    part(b, k)
                for i in range(TB):
                    residual(b - 1, i)
                for k in range(SLOTS - 1, MT):
                    part(b, k)
                    if k in NORM_AT:
                        norm(b - 1, NORM_AT[k])
            for i in range(TB):
                residual(NB - 1, i)
            for i in range(TB):
                norm(NB - 1, i)


def gla_pool_trunk(nc, a, out_dram):
    with ExitStack() as ctx:
        p = Program(nc, ctx)
        p.ps = ctx.enter_context(nc.psum_tensor("banks", [P, 8, BLK], F32))
        p.w_fused = nc.dram_tensor("w_fused", [MT, P, KT, P], F32).ap()
        p.q_tiles = nc.dram_tensor("q_tiles", [NT, P, KD], F32).ap()
        p.k_tiles = nc.dram_tensor("k_tiles", [NT, P, KD], F32).ap()
        p.kn_tiles = nc.dram_tensor("kn_tiles", [NT, P, KD], F32).ap()
        p.v_tiles = nc.dram_tensor("v_tiles", [NT, P, VD], F32).ap()
        p.g_tiles = nc.dram_tensor("g_tiles", [NT, P, VD], F32).ap()
        p.x1 = nc.dram_tensor("x1", [SEQ, D], F32).ap()
        p.mixed = nc.dram_tensor("mixed", [MT, P, SEQ], F32).ap()
        p.ident = p.place("ident", [P, P])
        p.mean_w = p.place("mean_w", [P, P])
        p.mask = p.place("mask", [P, HEADS, P])
        p.keep = p.place("keep", [P, BLK])
        p.correct = p.place("correct", [P, GROUPS, PAD])
        p.decay = p.place("decay", [P, HEADS, SEQ // CHUNK])
        p.b_gk = p.place("b_gk", [P, HEADS])
        p.norm_w = p.place("norm_w", [P, DV // P])
        p.b_grp = p.place("b_grp", [P, MT])
        p.scale = p.place("scale", [P, MT])
        p.carrier = p.place("carrier", [P, 1])
        p.eps_rms = p.place("eps_rms", [P, 1])
        p.eps_ln = p.place("eps_ln", [P, 1])
        p.work_at = p.ln_at = p.at
        p.x_hi = p.place("x_hi", [P, KT, SEQ], F32R)
        p.x_lo = p.place("x_lo", [P, KT, SEQ], F32R)
        p.stream_at = p.at

        constants(nc, p, a)
        fuse_pool_weights(nc, p, a)
        transpose_input(nc, p, "x0", a["x"][0])
        project_values(nc, p, a)
        project_heads(nc, p, a)
        attend_and_norm(nc, p, a)
        transpose_input(nc, p, "x1", p.x1)
        pool_mix(nc, p, a)
        pool_out_and_norm(nc, p, a, out_dram)


_INS = ["x", "gla_w_in", "gla_w_gk", "gla_b_gk", "gla_norm_w", "gla_w_out", "pool_w_in", "pool_w_grp",
        "pool_b_grp", "pool_scale", "pool_w_out", "ln_g", "ln_b"]


def kernel(**inputs):
    import numpy as np
    import concourse.bacc as bacc
    from concourse.bass_utils import run_bass_kernel_spmd

    nc = bacc.Bacc("TRN2", target_bir_lowering=False, num_devices=1)
    arrays, a = {}, {}
    for name in _INS:
        arrays[f"in_{name}"] = np.ascontiguousarray(inputs[name])
        a[name] = nc.dram_tensor(f"in_{name}", arrays[f"in_{name}"].shape, F32, kind="ExternalInput").ap()
    out = nc.dram_tensor("out", (1, SEQ, D), F32, kind="ExternalOutput").ap()
    gla_pool_trunk(nc, a, out[0])
    r = run_bass_kernel_spmd(nc, [arrays], core_ids=[0])
    return r.results[0]["out"]
```

```python
import concourse.bass as bass
from concourse import mybir
from contextlib import ExitStack

F32 = mybir.dt.float32
F32R = mybir.dt.float32r
I32 = mybir.dt.int32
ALU = mybir.AluOpType
ACT = mybir.ActivationFunctionType
ds = bass.ds

P = 128
SEQ = 2048
D = 1024
KT = D // P
HEADS = 4
DK = 128
DV = 256
CHUNK = 64
GATE_RANK = 16
GATE_NORMALIZER = 16.0
NT = SEQ // P
BLK = 512
NB = SEQ // BLK
KD = HEADS * DK
VD = HEADS * DV
POOL_W = 2048
WINDOWS = (2, 4, 8, 16)
GROUPS = len(WINDOWS)
GW = POOL_W // GROUPS
GT = GW // P
MT = POOL_W // P
PAD = max(WINDOWS)
ALPHA = 4.0 ** 0.25
LN_EPS = 1e-5
RMS_EPS = 1e-6
SBUF_START, SBUF_END = 16512, 229344
DMA = 16



class Program:

    V_RAW, V_PREFETCHED = 4, 2
    ROWS, ROWS_PREFETCHED = 4, 4
    OUT_PREFETCHED = 4
    M_RAW, M_PREFETCHED = 4, 1
    BT = 256

    def __init__(self, nc, ctx, a):
        self.nc, self.at, self.a = nc, SBUF_START, a
        sems = lambda name, n: [ctx.enter_context(nc.semaphore(f"{name}{i}")) for i in range(n)]
        self.ps = ctx.enter_context(nc.psum_tensor("banks", [P, 8, BLK], F32))
        scratch = lambda name, shape: nc.dram_tensor(name, shape, F32).ap()
        self.w_fused = scratch("w_fused", [MT, P, KT, P])
        self.q_tiles, self.k_tiles, self.kn_tiles = (scratch(n, [NT, P, KD]) for n in ("q_tiles", "k_tiles", "kn_tiles"))
        self.v_tiles, self.g_tiles = (scratch(n, [NT, P, VD]) for n in ("v_tiles", "g_tiles"))
        self.x1 = scratch("x1", [SEQ, D])
        self.mixed = scratch("mixed", [MT, P, SEQ])
        self.ident = self.place("ident", [P, P])
        self.mean_w = self.place("mean_w", [P, P])
        self.mask = self.place("mask", [P, HEADS, P])
        self.keep = self.place("keep", [P, BLK])
        self.correct = self.place("correct", [P, GROUPS, PAD])
        self.decay = self.place("decay", [P, HEADS, SEQ // CHUNK])
        self.b_gk = self.place("b_gk", [P, HEADS])
        self.norm_w = self.place("norm_w", [P, DV // P])
        self.b_grp = self.place("b_grp", [P, MT])
        self.scale = self.place("scale", [P, MT])
        self.score_carrier = self.place("score_carrier", [P, 1])
        self.stats_carrier = self.place("stats_carrier", [P, 1])
        self.eps_rms = self.place("eps_rms", [P, 1])
        self.eps_ln = self.place("eps_ln", [P, 1])
        self.ln_at = self.at
        self.x_hi = self.place("x_hi", [P, KT, SEQ], F32R)
        self.x_lo = self.place("x_lo", [P, KT, SEQ], F32R)
        self.stream_at = self.at
        self.v_raw_at = SBUF_END - self.V_RAW * BLK * 4
        self.at = self.v_raw_at
        late = [self.place(f"v_raw{s}", [P, BLK]) for s in (2, 3)]
        self.v_raw = [self.place(f"v_raw{s}", [P, BLK]) for s in (0, 1)] + late
        self.v_loaded = sems("v_loaded", self.V_RAW)
        self.rows_at = SBUF_END - self.ROWS * D * 4
        self.at = self.rows_at
        self.rows = [self.place(f"rows{s}", [P, D]) for s in range(self.ROWS)]
        self.rows_loaded = sems("rows_loaded", self.ROWS)
        self.at = self.rows_at
        self.out_raw = [self.place(f"out_raw{s}", [P, D]) for s in range(self.ROWS)]
        self.out_raw_loaded = sems("out_raw_loaded", self.ROWS)
        self.mix_raw_at = self.rows_at - 2 * KT * P * 4
        self.at = self.mix_raw_at
        self.mix_raw = [self.place(f"mix_raw{s}", [P, KT, P]) for s in range(2)]
        self.mix_loaded = sems("mix_loaded", 2)
        self.out_m_at = self.mix_raw_at - self.BT * 4
        self.at = self.out_m_at
        self.m_raw0 = self.place("m_raw0", [P, self.BT])
        self.m_loaded = sems("m_loaded", self.M_RAW)

    def place(self, name, shape, dtype=F32):
        size = 4
        for n in shape[1:]:
            size *= n
        t = self.nc.alloc_sbuf_tensor_at(name, shape, dtype, offset=self.at)
        self.at += (size + 31) // 32 * 32
        return t

    def prefetch_values(self, sp):
        w_src = self.a["gla_w_in"][0].rearrange("(k p) c -> p k c", p=P)
        for k in range(self.V_PREFETCHED):
            sp.dma_start(self.v_raw[k][:], w_src[:, k, 2 * KD:2 * KD + BLK]).then_inc(self.v_loaded[k], DMA)

    def load_mix(self, sp, m):
        z_src = self.a["pool_w_in"][0].rearrange("(k p) c -> p k c", p=P)
        sp.dma_start(self.mix_raw[0][:], self.w_fused[ds(m, 1), :, :, :].rearrange("o p k c -> (o p) k c")
                     ).then_inc(self.mix_loaded[0], DMA)
        sp.dma_start(self.mix_raw[1][:], z_src[:, :, ds(m * P + POOL_W, P)]).then_inc(self.mix_loaded[1], DMA)

    def prefetch_mix(self, sp):
        for t in range(self.ROWS_PREFETCHED):
            sp.dma_start(self.rows[t][:], self.x1[t * P:(t + 1) * P, :]).then_inc(self.rows_loaded[t], DMA)
        self.load_mix(sp, 0)

    def load_m(self, sp, m_raw, b, k):
        sp.dma_start(m_raw[k % self.M_RAW][:], self.mixed[k, :, ds(b * self.BT, self.BT)]
                     ).then_inc(self.m_loaded[k % self.M_RAW], DMA)

    def load_out(self, sp, k):
        w_src = self.a["pool_w_out"][0].rearrange("(k p) c -> p k c", p=P)
        sp.dma_start(self.out_raw[k % self.ROWS][:], w_src[:, k, :]).then_inc(self.out_raw_loaded[k % self.ROWS], DMA)

    def prefetch_out(self, sp):
        for k in range(self.OUT_PREFETCHED):
            self.load_out(sp, k)
        self.load_m(sp, [self.m_raw0], 0, 0)


def split_product(nc, out, a_hi, a_lo, b_hi, b_lo, first, last):
    nc.tensor.matmul(out, a_hi, b_hi, start=first, stop=False, skip_group_check=True)
    nc.tensor.matmul(out, a_hi, b_lo, start=False, stop=False, skip_group_check=True)
    return nc.tensor.matmul(out, a_lo, b_hi, start=False, stop=last, skip_group_check=True)


def prepare(nc, p, a):
    IN, ROWS = 4, 2
    p.at = p.stream_at
    w_in = [p.place(f"p_in{s}", [P, GW]) for s in range(IN)]
    w_grp = p.place("p_grp", [P, GT, GW])
    grp_hi = [p.place(f"p_grp_hi{s}", [P, GT, GW], F32R) for s in range(2)]
    grp_lo = [p.place(f"p_grp_lo{s}", [P, GT, GW], F32R) for s in range(2)]
    t_hi = [p.place(f"p_t_hi{s}", [P, GT, P], F32R) for s in range(2)]
    t_lo = [p.place(f"p_t_lo{s}", [P, GT, P], F32R) for s in range(2)]
    out = [p.place(f"p_out{s}", [P, GW]) for s in range(2)]
    rows = [p.place(f"p_rows{s}", [P, D]) for s in range(ROWS)]
    with ExitStack() as phase:
        sem = lambda name: phase.enter_context(nc.semaphore("p_" + name))
        in_loaded = [sem(f"in_loaded{s}") for s in range(IN)]
        rows_loaded = [sem(f"rows_loaded{s}") for s in range(ROWS)]
        stored = [sem(f"stored{s}") for s in range(2)]
        (grp_loaded, g_hi, g_lo, turned, hi, lo, multiplied, copied, x_turned, x_hi, x_lo, cleared, ones_in,
         ident_in, masked, columns) = (
            sem(n) for n in ("grp_loaded", "g_hi", "g_lo", "turned", "hi", "lo", "multiplied", "copied", "x_turned",
                             "x_hi", "x_lo", "cleared", "ones_in", "ident_in", "masked", "columns"))
        src_in = a["pool_w_in"][0].rearrange("(k p) c -> k p c", p=P)
        src_grp = a["pool_w_grp"][0].rearrange("g (k p) c -> p g k c", p=P)
        turned_ps = [p.ps[:, s, :] for s in range(2)]
        out_ps = [p.ps[:, 2 + s, :] for s in range(2)]
        x_ps = [p.ps[:, 4 + 2 * s:6 + 2 * s, :].rearrange("p b (k t) -> p (b k) t", t=P) for s in range(2)]
        PAIR = 2 * KT
        XT = PAIR // 2
        GRP_AT = (0, KT // 2)

        with nc.Block() as block:

            @block.sync
            def _(sp):
                with sp.Fori(0, GROUPS // 2) as pair:
                    for i in range(PAIR):
                        s, k, n = i // KT, i % KT, pair * PAIR + i
                        if i % 2 == 0:
                            for j in (i, i + 1):
                                sp.wait_ge(turned, pair * PAIR + j + 1)
                                sp.dma_start(w_in[j % IN][:], src_in[j % KT, :, ds((pair * 2 + j // KT) * GW, GW)]
                                             ).then_inc(in_loaded[j % IN], DMA)
                        if i in GRP_AT:
                            g = pair * 2 + GRP_AT.index(i)
                            sp.wait_ge(g_lo, g)
                            sp.dma_start(w_grp[:], src_grp[:, ds(g, 1), :, :].rearrange("p o k c -> p (o k) c")
                                         ).then_inc(grp_loaded, DMA)
                        if i % 2 == 1:
                            t = i // 2
                            sp.wait_ge(x_turned, pair * XT + t + 1)
                            sp.dma_start(rows[t % ROWS][:], a["x"][0][ds((pair * XT + t) * P, P), :]
                                         ).then_inc(rows_loaded[t % ROWS], DMA)
                with nc.allow_non_contiguous_dma(reason="small parameter vectors as columns"):
                    for dst, src in ((p.b_gk, a["gla_b_gk"][0].rearrange("(h d) -> d h", d=P)),
                                     (p.norm_w, a["gla_norm_w"][0].rearrange("(j d) -> d j", d=P)),
                                     (p.b_grp, a["pool_b_grp"][0].rearrange("g (m d) -> d (g m)", d=P)),
                                     (p.scale, a["pool_scale"][0].rearrange("(m d) -> d m", d=P))):
                        sp.dma_start(dst[:], src).then_inc(columns, DMA)
                p.prefetch_values(sp)
                sp.wait_ge(columns, 4 * DMA)
                for s in range(2):
                    sp.wait_ge(stored[s], DMA * GROUPS * KT // 2)

            @block.gpsimd
            def _(pool):
                nc.gpsimd.memset(p.ident[:], 0.0).then_inc(cleared, 1)
                pool.wait_ge(cleared, 1)
                nc.gpsimd.affine_select(out=p.ident[:], in_=p.ident[:], compare_op=ALU.not_equal, fill=1.0,
                                        base=0, pattern=[[-1, P]], channel_multiplier=1).then_inc(ident_in, 1)
                nc.gpsimd.memset(p.mask[:], 1.0).then_inc(cleared, 1)
                pool.wait_ge(cleared, 2)
                nc.gpsimd.affine_select(out=p.mask[:], in_=p.mask[:], compare_op=ALU.is_ge, fill=0.0,
                                        base=0, pattern=[[0, HEADS], [1, P]], channel_multiplier=-1
                                        ).then_inc(masked, 1)
                pool.wait_ge(masked, 1)
                late = p.mask[:, :, CHUNK:P]
                nc.gpsimd.affine_select(out=late, in_=late, compare_op=ALU.is_ge, fill=0.0,
                                        base=-CHUNK, pattern=[[0, HEADS], [0, CHUNK]], channel_multiplier=1)

            @block.tensor
            def _(pe):
                pe.sem_inc(turned, IN)
                pe.sem_inc(x_turned, ROWS)

                def turn(pair, i):
                    s = i // KT
                    pe.wait_ge(in_loaded[i % IN], (pair * (PAIR // IN) + i // IN + 1) * DMA)
                    pe.wait_ge(lo, pair * PAIR + max(i - 1, 0))
                    for c in range(GT):
                        last = nc.tensor.transpose(turned_ps[i % 2][:, c * P:(c + 1) * P],
                                                   w_in[i % IN][:, c * P:(c + 1) * P], p.ident[:])
                    last.then_inc(turned, 1)

                def turn_x(pair, t):
                    pe.wait_ge(rows_loaded[t % ROWS], (pair * (XT // ROWS) + t // ROWS + 1) * DMA)
                    pe.wait_ge(x_lo, pair * XT + max(t - 1, 0))
                    for k in range(KT):
                        last = nc.tensor.transpose(x_ps[t % 2][:, k, :], rows[t % ROWS][:, k * P:(k + 1) * P],
                                                   p.ident[:])
                    last.then_inc(x_turned, 1)

                pe.wait_ge(ident_in, 1)
                with pe.Fori(0, GROUPS // 2) as pair:
                    turn(pair, 0)
                    for i in range(PAIR):
                        if i + 1 < PAIR:
                            turn(pair, i + 1)
                        if i % 2 == 1:
                            turn_x(pair, i // 2)
                        s = i // KT
                        pe.wait_ge(lo, pair * PAIR + i + 1)
                        pe.wait_ge(g_lo, pair * 2 + s + 1)
                        pe.wait_ge(copied, pair * PAIR + max(i - 1, 0))
                        for c in range(GT):
                            last = split_product(nc, out_ps[i % 2], t_hi[i % 2][:, c, :], t_lo[i % 2][:, c, :],
                                                 grp_hi[s][:, c, :], grp_lo[s][:, c, :], c == 0, c == GT - 1)
                        last.then_inc(multiplied, 1)

            @block.scalar
            def _(act):
                def copy_out(pair, i):
                    n = pair * PAIR + i
                    act.wait_ge(multiplied, n + 1)
                    act.wait_ge(stored[i % 2], (pair * KT + i // 2) * DMA)
                    nc.scalar.activation(out[i % 2][:], out_ps[i % 2], ACT.Copy).then_inc(copied, 1)
                    act.wait_ge(copied, n + 1)
                    act.dma_start(p.w_fused[ds((pair * 2 + i // KT) * GT, GT), :, i % KT, :].rearrange("m p c -> p m c"),
                                  out[i % 2][:].rearrange("p (m c) -> p m c", c=P)).then_inc(stored[i % 2], DMA)

                with act.Fori(0, GROUPS // 2) as pair:
                    for i in range(PAIR):
                        s, n = i // KT, pair * PAIR + i
                        if i in GRP_AT:
                            g = GRP_AT.index(i)
                            act.wait_ge(grp_loaded, (pair * 2 + g + 1) * DMA)
                            act.wait_ge(multiplied, pair * PAIR)
                            nc.scalar.activation(grp_hi[g][:], w_grp[:], ACT.Copy).then_inc(g_hi, 1)
                        act.wait_ge(turned, IN + n + 1)
                        act.wait_ge(multiplied, pair * PAIR + max(i - 1, 0))
                        nc.scalar.activation(t_hi[i % 2][:].rearrange("p c d -> p (c d)"), turned_ps[i % 2],
                                             ACT.Copy).then_inc(hi, 1)
                        if i % 2 == 0 and i > 0:
                            t = pair * XT + i // 2 - 1
                            act.wait_ge(x_turned, ROWS + t + 1)
                            nc.scalar.activation(p.x_hi[:, :, ds(t * P, P)], x_ps[(i // 2 - 1) % 2], ACT.Copy
                                                 ).then_inc(x_hi, 1)
                        if i >= 1:
                            copy_out(pair, i - 1)
                    t = pair * XT + XT - 1
                    act.wait_ge(x_turned, ROWS + t + 1)
                    nc.scalar.activation(p.x_hi[:, :, ds(t * P, P)], x_ps[(XT - 1) % 2], ACT.Copy).then_inc(x_hi, 1)
                    copy_out(pair, PAIR - 1)

            @block.vector
            def _(dve):
                nc.vector.memset(p.mean_w[:], 1.0 / DV)
                nc.vector.memset(p.eps_rms[:], RMS_EPS)
                nc.vector.memset(p.eps_ln[:], LN_EPS)
                nc.vector.memset(p.keep[:], 1.0).then_inc(ones_in, 1)
                nc.vector.memset(p.correct[:], 1.0).then_inc(ones_in, 1)
                dve.wait_ge(ones_in, 2)
                nc.vector.memset(p.keep[:].rearrange("p (c s) -> p c s", s=CHUNK)[:, :, 0:1], 0.0)
                for g, w in enumerate(WINDOWS):
                    for t in range(w - 1):
                        nc.vector.memset(p.correct[:, g, t:t + 1], w / (t + 1.0))

                def split_x(pair, t):
                    n = pair * XT + t
                    dve.wait_ge(x_hi, n + 1)
                    nc.vector.tensor_tensor(p.x_lo[:, :, ds(n * P, P)], x_ps[t % 2],
                                            p.x_hi[:, :, ds(n * P, P)].bitcast(F32), ALU.subtract).then_inc(x_lo, 1)

                with dve.Fori(0, GROUPS // 2) as pair:
                    for i in range(PAIR):
                        s, n = i // KT, pair * PAIR + i
                        if i in GRP_AT:
                            g = GRP_AT.index(i)
                            dve.wait_ge(g_hi, pair * 2 + g + 1)
                            nc.vector.tensor_tensor(grp_lo[g][:], w_grp[:], grp_hi[g][:].bitcast(F32),
                                                    ALU.subtract).then_inc(g_lo, 1)
                        dve.wait_ge(hi, n + 1)
                        nc.vector.tensor_tensor(t_lo[i % 2][:].rearrange("p c d -> p (c d)"), turned_ps[i % 2],
                                                t_hi[i % 2][:].rearrange("p c d -> p (c d)").bitcast(F32),
                                                ALU.subtract).then_inc(lo, 1)
                        if i % 2 == 0 and i > 0:
                            split_x(pair, i // 2 - 1)
                    split_x(pair, XT - 1)



def project(nc, p, a):
    HALVES, V_OUT, BANKS = 2, 4, 4
    p.at = p.stream_at
    v_hi = p.place("v_hi", [P, KT, BLK], F32R)
    v_lo = p.place("v_lo", [P, KT, BLK], F32R)
    v_out = [p.place(f"v_out{s}", [P, BLK]) for s in range(V_OUT)]
    v_raw = p.v_raw
    raw = [p.place(f"h_raw{s}", [P, KT, P]) for s in range(2)]
    w_hi0, w_lo0 = p.place("h_w_hi0", [P, KT, P], F32R), p.place("h_w_lo0", [P, KT, P], F32R)
    rank_raw = p.place("h_rank_raw", [P, KT, GATE_RANK])
    w_gk = p.place("h_w_gk", [2 * GATE_RANK, P])
    chunk_end = p.place("h_chunk_end", [P, SEQ // CHUNK])
    early_at = p.at
    rank_w = p.place("h_rank_w", [P, KT, P], F32R)
    p.at = early_at
    kn_out = [p.place(f"h_kn_out{s}", [P, BLK]) for s in range(2)]
    p.at = p.v_raw_at
    k_out = [p.place(f"h_k_out{s}", [P, BLK]) for s in range(2)]
    g_out = [p.place(f"h_g_out{s}", [P, BLK]) for s in range(2)]
    p.at = p.stream_at
    w_hi1, w_lo1 = p.place("h_w_hi1", [P, KT, P], F32R), p.place("h_w_lo1", [P, KT, P], F32R)
    rank = p.place("h_rank", [2 * GATE_RANK, SEQ])
    e_q = p.place("h_e_q", [P, SEQ])
    e_k = p.place("h_e_k", [P, SEQ])
    sums_at = p.at
    p.at = early_at + 2 * BLK * 4
    q_out = [p.place(f"h_q_out{s}", [P, BLK]) for s in range(2)]
    assert p.at <= p.v_raw_at
    p.at = sums_at
    sums = p.place("h_sums", [P, SEQ])
    w_hi, w_lo = [w_hi0, w_hi1], [w_lo0, w_lo1]

    phase = ExitStack()
    sem = lambda name: phase.enter_context(nc.semaphore("h_" + name))
    loaded, v_stored = [sem(f"loaded{s}") for s in range(2)], [sem(f"v_stored{s}") for s in range(V_OUT)]
    v_loaded = p.v_loaded
    rank_loaded, gk_loaded = sem("rank_loaded"), sem("gk_loaded")
    (zeroed, rank_hi, rank_lo, rank_mm, rank_ready, hi, lo, gk_mm, abs_done, scanned, ln_done, chain,
     sums_ready, exps_ready, qk_done, tiles_mm, turned, kn_copied, silu, g_done, v_hi_done, v_lo_done, v_mm,
     v_copied) = (
        sem(n) for n in (
            "zeroed", "rank_hi", "rank_lo", "rank_mm", "rank_ready", "hi", "lo", "gk_mm", "abs", "scanned", "ln",
            "chain", "sums_ready", "exps_ready", "qk_done", "tiles_mm", "turned", "kn_copied", "silu", "g_done",
            "v_hi_done", "v_lo_done", "v_mm", "v_copied"))
    q_stored, k_stored, kn_stored, g_stored = ([sem(f"{n}_stored{s}") for s in range(2)] for n in ("q", "k", "kn", "g"))
    w_src = a["gla_w_in"][0].rearrange("(k p) c -> p k c", p=P)
    gk_ps = p.ps[:, NB:2 * NB, :].rearrange("p b t -> p (b t)")
    CHAINED = 3

    def w_cols(h, j):
        return (h * DK, h * DK + KD, h * DV + 2 * KD + VD, h * DV + 2 * KD + VD + P)[j]

    with phase, nc.Block() as block:

        @block.sync
        def _(sp):
            def load(h, j):
                sp.dma_start(raw[j % 2][:], w_src[:, :, ds(w_cols(h, j), P)]).then_inc(loaded[j % 2], DMA)

            def load_gk(h):
                for r in range(2):
                    sp.dma_start(w_gk[r * GATE_RANK:(r + 1) * GATE_RANK, :],
                                 a["gla_w_gk"][0][:, ds(h * DK, DK)]).then_inc(gk_loaded, DMA)

            def store(scratch, unit, n, out, sem):
                sp.dma_start(scratch[n * NB:(n + 1) * NB, :, ds(unit * P, P)].rearrange("t p c -> p t c"),
                             out[n % 2][:].rearrange("p (t c) -> p t c", c=P)).then_inc(sem[n % 2], DMA)

            def head(h, last):
                sp.wait_ge(lo, h * 4 + 1)
                load(h, 2)
                for n in range(NB):
                    sp.wait_ge(qk_done, h * 8 + n + 1)
                    store(p.q_tiles, h, n, q_out, q_stored)
                sp.wait_ge(lo, h * 4 + 2)
                load(h, 3)
                for n in range(NB):
                    sp.wait_ge(qk_done, h * 8 + NB + n + 1)
                    store(p.k_tiles, h, n, k_out, k_stored)
                if not last:
                    sp.wait_ge(gk_mm, h * NB + NB)
                    load_gk(h + 1)
                    sp.wait_ge(lo, h * 4 + 3)
                    load(h + 1, 0)
                for n in range(NB):
                    sp.wait_ge(g_done, h * 8 + n + 1)
                    store(p.g_tiles, h * 2, n, g_out, g_stored)
                if not last:
                    sp.wait_ge(lo, h * 4 + 4)
                    load(h + 1, 1)
                for n in range(NB):
                    sp.wait_ge(kn_copied, h * NB + n + 1)
                    store(p.kn_tiles, h, n, kn_out, kn_stored)
                for n in range(NB):
                    sp.wait_ge(g_done, h * 8 + NB + n + 1)
                    store(p.g_tiles, h * 2 + 1, n, g_out, g_stored)

            for n in range(p.V_PREFETCHED, HALVES * KT):
                half, k = n // KT, n % KT
                if n >= p.V_RAW:
                    sp.wait_ge(v_lo_done, n - p.V_RAW + 1)
                sp.dma_start(v_raw[n % p.V_RAW][:], w_src[:, k, half * BLK + 2 * KD:(half + 1) * BLK + 2 * KD]
                             ).then_inc(v_loaded[n % p.V_RAW], DMA)
            with nc.allow_non_contiguous_dma(reason="16 columns of the gates' first factor"):
                sp.dma_start(rank_raw[:], w_src[:, :, 2 * KD + 2 * VD:2 * KD + 2 * VD + GATE_RANK]
                             ).then_inc(rank_loaded, DMA)
            load_gk(0)
            load(0, 0)
            load(0, 1)
            with sp.Fori(0, HEADS - 1) as h:
                head(h, False)
            head(HEADS - 1, True)
            for s in range(2):
                for sem, units in ((q_stored, 1), (k_stored, 1), (kn_stored, 1), (g_stored, 2)):
                    sp.wait_ge(sem[s], HEADS * units * NB // 2 * DMA)

        @block.tensor
        def _(pe):
            with pe.Fori(0, HALVES) as half:
                for t in range(NT):
                    pe.wait_ge(v_copied, half * NT + max(t - BANKS + 1, 0))
                    for k in range(KT):
                        if t == 0:
                            pe.wait_ge(v_lo_done, half * KT + k + 1)
                        last = split_product(nc, p.ps[:, t % BANKS, :], p.x_hi[:, k, t * P:(t + 1) * P],
                                             p.x_lo[:, k, t * P:(t + 1) * P], v_hi[:, k, :], v_lo[:, k, :],
                                             k == 0, k == KT - 1)
                    last.then_inc(v_mm, 1)
            pe.wait_ge(rank_lo, 1)
            for n in range(NB):
                pe.wait_ge(v_copied, HALVES * NT - BANKS + n + 1)
                for k in range(KT):
                    nc.tensor.matmul(p.ps[:, n, :], rank_w[:, k, :], p.x_hi[:, k, n * BLK:(n + 1) * BLK],
                                     start=k == 0, stop=False)
                    last = nc.tensor.matmul(p.ps[:, n, :], rank_w[:, k, :], p.x_lo[:, k, n * BLK:(n + 1) * BLK],
                                            start=False, stop=k == KT - 1)
                last.then_inc(rank_mm, 1)

            def tile(w, j, bank_free):
                pe.wait_ge(lo, w + 1)
                for n in range(NB):
                    pe.wait_ge(*bank_free(n))
                    for k in range(KT):
                        last = split_product(nc, p.ps[:, n, :], w_hi[j % 2][:, k, :], w_lo[j % 2][:, k, :],
                                             p.x_hi[:, k, n * BLK:(n + 1) * BLK],
                                             p.x_lo[:, k, n * BLK:(n + 1) * BLK], k == 0, k == KT - 1)
                    last.then_inc(tiles_mm, 1)

            with pe.Fori(0, HEADS) as h:
                pe.wait_ge(gk_loaded, (h + 1) * 2 * DMA)
                pe.wait_ge(rank_ready, NB)
                pe.wait_ge(kn_copied, h * NB)
                for n in range(NB):
                    nc.tensor.matmul(p.ps[:, NB + n, :], w_gk[:], rank[:, n * BLK:(n + 1) * BLK],
                                     start=True, stop=True).then_inc(gk_mm, 1)
                tile(h * 4, 0, lambda n: (g_done, h * 8))
                tile(h * 4 + 1, 1, lambda n: (qk_done, h * 8 + n + 1))
                tile(h * 4 + 2, 2, lambda n: (qk_done, h * 8 + NB + n + 1))
                for n in range(NB):
                    pe.wait_ge(qk_done, h * 8 + NB + n + 1)
                    for c in range(NB):
                        last = nc.tensor.transpose(p.ps[:, NB + n, c * P:(c + 1) * P],
                                                   sums[:, (n * NB + c) * P:(n * NB + c + 1) * P], p.ident[:])
                    last.then_inc(turned, 1)
                tile(h * 4 + 3, 3, lambda n: (silu, h * 8 + n + 1))

        def first_parts(act):
            act.wait_ge(rank_loaded, DMA)
            act.wait_ge(zeroed, 1)
            nc.scalar.activation(rank_w[:, :, 0:GATE_RANK], rank_raw[:], ACT.Copy).then_inc(rank_hi, 1)
            act.wait_ge(loaded[0], DMA)
            nc.scalar.activation(w_hi[0][:], raw[0][:], ACT.Copy).then_inc(hi, 1)

        @block.scalar
        def _(act):
            for half in range(HALVES):
                if half:
                    act.wait_ge(v_mm, half * NT)
                for k in range(KT):
                    n = half * KT + k
                    act.wait_ge(v_loaded[n % p.V_RAW], (n // p.V_RAW + 1) * DMA)
                    nc.scalar.activation(v_hi[:, k, :], v_raw[n % p.V_RAW][:], ACT.Copy).then_inc(v_hi_done, 1)
                if half == HALVES - 1:
                    first_parts(act)
                for t in range(NT):
                    n = half * NT + t
                    act.wait_ge(v_mm, n + 1)
                    if n >= V_OUT:
                        act.wait_ge(v_stored[t % V_OUT], n // V_OUT * DMA)
                    nc.scalar.activation(v_out[t % V_OUT][:], p.ps[:, t % BANKS, :], ACT.Copy).then_inc(v_copied, 1)
                    act.wait_ge(v_copied, n + 1)
                    act.dma_start(p.v_tiles[t, :, half * BLK:(half + 1) * BLK], v_out[t % V_OUT][:]
                                  ).then_inc(v_stored[t % V_OUT], DMA)
            for s in range(V_OUT):
                act.wait_ge(v_stored[s], HALVES * NT // V_OUT * DMA)
            for n in range(NB):
                act.wait_ge(rank_mm, n + 1)
                nc.scalar.activation(rank[:, n * BLK:(n + 1) * BLK], p.ps[0:2 * GATE_RANK, n, :],
                                     ACT.Copy).then_inc(rank_ready, 1)

            def part(h, j, w):
                act.wait_ge(loaded[j % 2], (h * 2 + j // 2 + 1) * DMA)
                if isinstance(w, int) and w < 2:
                    pass
                else:
                    act.wait_ge(tiles_mm, (w - 1) * NB)
                nc.scalar.activation(w_hi[j % 2][:], raw[j % 2][:], ACT.Copy).then_inc(hi, 1)

            def head(h, last):
                nc.scalar.preload_act_table_set("natural_log_exp_and_others")
                act.wait_ge(gk_mm, h * NB + NB)
                act.wait_ge(qk_done, h * 8)
                nc.scalar.activation(e_q[:], gk_ps, ACT.Abs, bias=p.b_gk[:, ds(h, 1)]).then_inc(abs_done, 1)
                act.wait_ge(abs_done, h + 1)
                nc.scalar.activation(e_q[:], e_q[:], ACT.Exp, scale=-1.0).then_inc(ln_done, 1)
                act.wait_ge(ln_done, h * 2 + 1)
                nc.scalar.activation(e_q[:], e_q[:], ACT.Ln, bias=1.0).then_inc(ln_done, 1)
                act.wait_ge(loaded[1], (h * 2 + 1) * DMA)
                act.wait_ge(tiles_mm, h * 4 * NB)
                nc.scalar.activation(w_hi[1][:], raw[1][:], ACT.Copy).then_inc(hi, 1)
                act.wait_ge(sums_ready, h + 1)
                nc.scalar.activation(e_q[:], sums[:], ACT.Exp, scale=1.0 / GATE_NORMALIZER)
                nc.scalar.activation(e_k[:], sums[:], ACT.Exp, scale=-1.0 / GATE_NORMALIZER)
                nc.scalar.activation(p.decay[:, ds(h, 1), :].rearrange("p o c -> p (o c)"), chunk_end[:], ACT.Exp,
                                     scale=1.0 / GATE_NORMALIZER).then_inc(exps_ready, 1)
                act.wait_ge(chain, h * CHAINED + 3)
                nc.scalar.activation(sums[:], sums[:], ACT.Exp, scale=1.0 / GATE_NORMALIZER).then_inc(exps_ready, 1)
                part(h, 2, h * 4 + 2)
                part(h, 3, h * 4 + 3)

                def gate(j, n):
                    act.wait_ge(tiles_mm, (h * 4 + j) * NB + n + 1)
                    act.wait_ge(g_stored[n % 2], (h * 4 + (j - 2) * 2 + n // 2) * DMA)
                    nc.scalar.activation(g_out[n % 2][:], p.ps[:, n, :], ACT.Silu).then_inc(silu, 1)

                for n in range(NB):
                    gate(2, n)
                if not last:
                    part(h + 1, 0, h * 4 + 4)
                for n in range(NB):
                    act.wait_ge(turned, h * NB + n + 1)
                    act.wait_ge(kn_stored[n % 2], (h * 2 + n // 2) * DMA)
                    nc.scalar.activation(kn_out[n % 2][:], p.ps[:, NB + n, :], ACT.Copy).then_inc(kn_copied, 1)
                for n in range(NB):
                    gate(3, n)

            with act.Fori(0, HEADS - 1) as h:
                head(h, False)
            head(HEADS - 1, True)

        @block.vector
        def _(dve):
            nc.vector.memset(rank_w[:].bitcast(F32), 0.0).then_inc(zeroed, 1)
            for n in range(HALVES * KT):
                dve.wait_ge(v_hi_done, n + 1)
                nc.vector.tensor_tensor(v_lo[:, n % KT, :], v_raw[n % p.V_RAW][:], v_hi[:, n % KT, :].bitcast(F32),
                                        ALU.subtract).then_inc(v_lo_done, 1)
            dve.wait_ge(rank_hi, 1)
            nc.vector.tensor_tensor(rank_w[:, :, GATE_RANK:2 * GATE_RANK], rank_raw[:],
                                    rank_w[:, :, 0:GATE_RANK].bitcast(F32), ALU.subtract).then_inc(rank_lo, 1)

            def part(w, s):
                dve.wait_ge(hi, w + 1)
                nc.vector.tensor_tensor(w_lo[s][:], raw[s][:], w_hi[s][:].bitcast(F32), ALU.subtract).then_inc(lo, 1)

            def head(h, last):
                dve.wait_ge(abs_done, h + 1)
                dve.wait_ge(qk_done, h * 8)
                dve.wait_ge(turned, h * NB)
                nc.vector.tensor_scalar(e_k[:], gk_ps, p.b_gk[:, ds(h, 1)], 0.0, ALU.add, ALU.min).then_inc(chain, 1)
                dve.wait_ge(ln_done, h * 2 + 2)
                dve.wait_ge(chain, h * CHAINED + 1)
                nc.vector.tensor_tensor(e_k[:], e_k[:], e_q[:], ALU.subtract).then_inc(chain, 1)
                part(h * 4 + 1, 1)
                dve.wait_ge(chain, h * CHAINED + 2)
                for n in range(NB):
                    cols = slice(n * BLK, (n + 1) * BLK)
                    scan = nc.vector.tensor_tensor_scan(sums[:, cols], p.keep[:], e_k[:, cols], 0.0, ALU.mult, ALU.add)
                scan.then_inc(scanned, 1)
                dve.wait_ge(scanned, h + 1)
                by_chunk = sums[:].rearrange("p (c s) -> p c s", s=CHUNK)
                nc.vector.tensor_copy(chunk_end[:], by_chunk[:, :, CHUNK - 1]).then_inc(sums_ready, 1)
                dve.wait_ge(sums_ready, h + 1)
                dve.wait_ge(exps_ready, h * 2 + 1)
                nc.vector.tensor_tensor(by_chunk, chunk_end[:].unsqueeze(2).to_broadcast([P, SEQ // CHUNK, CHUNK]),
                                        by_chunk, ALU.subtract).then_inc(chain, 1)
                for n in range(NB):
                    dve.wait_ge(tiles_mm, h * 4 * NB + n + 1)
                    dve.wait_ge(q_stored[n % 2], (h * 2 + n // 2) * DMA)
                    nc.vector.scalar_tensor_tensor(out=q_out[n % 2][:], in0=p.ps[:, n, :], scalar=float(DK) ** -0.5,
                                                   in1=e_q[:, n * BLK:(n + 1) * BLK], op0=ALU.mult, op1=ALU.mult
                                                   ).then_inc(qk_done, 1)
                part(h * 4 + 2, 0)
                dve.wait_ge(exps_ready, h * 2 + 2)
                for n in range(NB):
                    cols = slice(n * BLK, (n + 1) * BLK)
                    dve.wait_ge(tiles_mm, (h * 4 + 1) * NB + n + 1)
                    dve.wait_ge(k_stored[n % 2], (h * 2 + n // 2) * DMA)
                    nc.vector.tensor_tensor(k_out[n % 2][:], p.ps[:, n, :], e_k[:, cols], ALU.mult)
                    nc.vector.tensor_tensor(sums[:, cols], p.ps[:, n, :], sums[:, cols], ALU.mult).then_inc(qk_done, 1)
                part(h * 4 + 3, 1)

                def gate(j, n):
                    dve.wait_ge(silu, h * 8 + (j - 2) * NB + n + 1)
                    nc.vector.tensor_scalar(g_out[n % 2][:], g_out[n % 2][:], p.norm_w[:, j - 2:j - 1], None,
                                            ALU.mult).then_inc(g_done, 1)

                for n in range(NB):
                    gate(2, n)
                if not last:
                    part(h * 4 + 4, 0)
                for n in range(NB):
                    gate(3, n)

            dve.wait_ge(hi, 1)
            nc.vector.tensor_tensor(w_lo[0][:], raw[0][:], w_hi[0][:].bitcast(F32), ALU.subtract).then_inc(lo, 1)
            for s in range(V_OUT):
                dve.wait_ge(v_stored[s], HALVES * NT // V_OUT * DMA)
            with dve.Fori(0, HEADS - 1) as h:
                head(h, False)
            head(HEADS - 1, True)


def attend_and_norm(nc, p, a):
    p.at = p.ln_at
    ln_g = p.place("a_ln_g", [P, D])
    ln_b = p.place("a_ln_b", [P, D])
    w_hi = p.place("a_w_hi", [P, KT, D], F32R)
    w_lo = p.place("a_w_lo", [P, KT, D], F32R)
    q, k, kn, scores = ([p.place(f"a_{n}{s}", [P, KD]) for s in range(2)] for n in ("q", "k", "kn", "scores"))
    v, g, x = ([p.place(f"a_{n}{s}", [P, D]) for s in range(2)] for n in ("v", "g", "x"))
    STATES = 4
    state = [p.place(f"a_state{s}", [P, VD]) for s in range(STATES)]
    square = p.place("a_square", [P, VD])
    square_sum = p.place("a_square_sum", [P, KD])
    rms = p.place("a_rms", [P, HEADS, P])
    gated = p.place("a_gated", [P, VD])
    o_hi = [p.place(f"a_o_hi{s}", [P, KT, P], F32R) for s in range(2)]
    o_lo = [p.place(f"a_o_lo{s}", [P, KT, P], F32R) for s in range(2)]
    res = p.place("a_res", [P, D])
    stats = p.place("a_stats", [P, 2, 6])
    moments = p.place("a_moments", [P, 2])
    rstd = p.place("a_rstd", [P, 1])
    out = [p.place(f"a_out{s}", [P, D]) for s in range(2)]
    assert p.at <= p.mix_raw_at
    p.at, RAW = p.rows_at, 4
    raw = [p.place(f"a_raw{s}", [P, D]) for s in range(RAW)]

    phase = ExitStack()
    sem = lambda name: phase.enter_context(nc.semaphore("a_" + name))
    ln_loaded, summed_squares = sem("ln_loaded"), sem("summed_squares")
    raw_loaded = [sem(f"raw_loaded{s}") for s in range(RAW)]
    in_loaded, g_loaded, x_loaded, out_stored = (
        [sem(f"{n}{s}") for s in range(2)] for n in ("in_loaded", "g_loaded", "x_loaded", "out_stored"))
    (w_hi_done, w_lo_done, zeroed, scored, masked, kv_mm, states, o_mm, squared, summed, rms_mid, rms_done, o_read,
     gated_done, o_hi_done, o_lo_done, y_mm, y_read, stats_done, moments_done, rstd_mid, rstd_done, normed,
     scaled, out_done) = (
        sem(n) for n in (
            "w_hi_done", "w_lo_done", "zeroed", "scored", "masked", "kv_mm", "states", "o_mm", "squared", "summed",
            "rms_mid", "rms_done", "o_read", "gated_done", "o_hi_done", "o_lo_done", "y_mm", "y_read", "stats_done",
            "moments_done", "rstd_mid", "rstd_done", "normed", "scaled", "out_done"))

    w_src = a["gla_w_out"][0].rearrange("(k p) c -> p k c", p=P)
    score_ps = p.ps[:, 0, :]
    o_ps = p.ps[:, 1:3, :].rearrange("p b c -> p (b c)")
    kv_ps = p.ps[:, 3:5, :].rearrange("p b c -> p (b c)")
    sum_ps = p.ps[:, 5, :]
    y_ps = [p.ps[:, 6 + half, :] for half in range(2)]
    LAG, TAIL = 2, 3

    def run(engine, step):
        for t in range(TAIL + 1):
            step(t, t % 2, min(t, TAIL), t // 2)
        with engine.Fori((TAIL + 1) // 2, NT // 2) as pair:
            for s in range(2):
                step(pair * 2 + s, s, TAIL, pair)
        for t in range(NT, NT + TAIL):
            step(t, t % 2, TAIL, t // 2)

    def has(t, lag, behind):
        return lag >= behind and not (isinstance(t, int) and t - behind >= NT)

    with phase, nc.Block() as block:

        @block.sync
        def _(sp):
            def load(t, s):
                for dst, src in ((q, p.q_tiles), (k, p.k_tiles), (kn, p.kn_tiles), (v, p.v_tiles)):
                    sp.dma_start(dst[s][:], src[ds(t, 1), :, :].rearrange("o p c -> (o p) c")).then_inc(in_loaded[s], DMA)

            def load_g(t, s):
                sp.dma_start(g[s][:], p.g_tiles[ds(t, 1), :, :].rearrange("o p c -> (o p) c")).then_inc(g_loaded[s], DMA)

            def load_x(t, s):
                sp.dma_start(x[s][:], a["x"][0][ds(t * P, P), :]).then_inc(x_loaded[s], DMA)

            def load_w(kt):
                if kt >= RAW:
                    sp.wait_ge(w_lo_done, kt - RAW + 1)
                sp.dma_start(raw[kt % RAW][:], w_src[:, kt, :]).then_inc(raw_loaded[kt % RAW], DMA)

            load(0, 0)
            load(1, 1)
            for kt in range(RAW):
                load_w(kt)
            load_g(0, 0)
            load_g(1, 1)
            load_x(0, 0)
            load_x(1, 1)
            for ln, src in ((ln_g, a["ln_g"]), (ln_b, a["ln_b"])):
                sp.dma_start(ln[:], src[0:1, :].to_broadcast([P, D])).then_inc(ln_loaded, DMA)
            for kt in range(RAW, KT):
                load_w(kt)

            def step(t, s, lag):
                static = isinstance(t, int)
                if lag >= 1 and not (static and t + 1 >= NT):
                    sp.wait_ge(gated_done, t)
                    load_g(t + 1, 1 - s)
                if has(t, lag, TAIL):
                    sp.wait_ge(out_done, t - TAIL + 1)
                    sp.dma_start(p.x1[ds((t - TAIL) * P, P), :], out[1 - s][:]).then_inc(out_stored[1 - s], DMA)
                if lag >= LAG and not (static and t >= NT):
                    sp.wait_ge(y_read, (t - LAG) * 2 + 2)
                    load_x(t, s)
                if not (static and t + 2 >= NT):
                    sp.wait_ge(o_mm, t + 1)
                    load(t + 2, s)

            for t in range(TAIL + 1):
                step(t, t % 2, min(t, TAIL))
            with sp.Fori((TAIL + 1) // 2, NT // 2 - 1) as pair:
                for s in range(2):
                    step(pair * 2 + s, s, TAIL)
            for t in range(NT - 2, NT + TAIL):
                step(t, t % 2, TAIL)
                if t == NT:
                    sp.wait_ge(w_lo_done, KT)
                    for i in range(2):
                        sp.wait_ge(out_stored[i], p.ROWS_PREFETCHED // 2 * DMA)
                    p.prefetch_mix(sp)
            for s in range(2):
                sp.wait_ge(out_stored[s], NT // 2 * DMA)

        @block.tensor
        def _(pe):
            def y_half(t, s, half):
                u = t - LAG
                if half == 0:
                    pe.wait_ge(o_lo_done, u + 1)
                    pe.wait_ge(w_lo_done, KT)
                    pe.wait_ge(y_read, u * 2)
                for kt in range(KT):
                    last = split_product(nc, y_ps[half], o_hi[s][:, kt, :], o_lo[s][:, kt, :],
                                         w_hi[:, kt, half * BLK:(half + 1) * BLK],
                                         w_lo[:, kt, half * BLK:(half + 1) * BLK], kt == 0, kt == KT - 1)
                last.then_inc(y_mm, 1)

            def kv(s, c):
                rows = slice(c * CHUNK, (c + 1) * CHUNK)
                for h in range(HEADS):
                    last = nc.tensor.matmul(kv_ps[:, h * DV:(h + 1) * DV], kn[s][rows, h * DK:(h + 1) * DK],
                                            v[s][rows, h * DV:(h + 1) * DV], start=True, stop=True)
                last.then_inc(kv_mm, 1)

            def inter(s, c, b, last_group):
                st = state[(2 * s + c) % STATES]
                for j in range(4 * b, 4 * b + 4):
                    cols = slice(j * P + c * CHUNK, j * P + (c + 1) * CHUNK)
                    h = j // 2
                    last = nc.tensor.matmul(o_ps[:, cols], st[:, j * P:(j + 1) * P],
                                            q[s][:, h * DK + c * CHUNK:h * DK + (c + 1) * CHUNK],
                                            start=False, stop=last_group, skip_group_check=True)
                return last

            def step(t, s, lag, pair):
                attends = not (isinstance(t, int) and t >= NT)
                if attends:
                    pe.wait_ge(in_loaded[s], (pair + 1) * (4 * DMA))
                    pe.wait_ge(masked, t)
                    for h in range(HEADS):
                        last = nc.tensor.matmul(score_ps[:, h * P:(h + 1) * P], k[s][:, h * P:(h + 1) * P],
                                                q[s][:, h * P:(h + 1) * P], start=True, stop=True)
                    last.then_inc(scored, 1)
                    pe.wait_ge(states, t * 2)
                    kv(s, 0)
                if has(t, lag, 1):
                    pe.wait_ge(summed_squares, t)
                    pe.wait_ge(rms_mid, t - 1)
                    nc.tensor.matmul(sum_ps, p.mean_w[:], square_sum[:], start=True, stop=True).then_inc(summed, 1)
                if has(t, lag, LAG):
                    y_half(t, s, 0)
                if attends:
                    pe.wait_ge(masked, t + 1)
                    pe.wait_ge(zeroed, 1)
                    pe.wait_ge(o_read, t)
                    for b in range(2):
                        for j in range(4 * b, 4 * b + 4):
                            h = j // 2
                            nc.tensor.matmul(o_ps[:, j * P:(j + 1) * P], v[s][:, j * P:(j + 1) * P],
                                             scores[s][:, h * P:(h + 1) * P], start=j == 4 * b, stop=False,
                                             skip_group_check=True)
                        inter(s, 0, b, False)
                    pe.wait_ge(states, t * 2 + 1)
                    kv(s, 1)
                if has(t, lag, LAG):
                    y_half(t, s, 1)
                if attends:
                    inter(s, 1, 0, True)
                    inter(s, 1, 1, True).then_inc(o_mm, 1)

            run(pe, step)

        @block.scalar
        def _(act):
            nc.scalar.preload_act_table_set("natural_log_exp_and_others")

            def step(t, s, lag, pair):
                if has(t, lag, 1):
                    u = t - 1
                    act.wait_ge(summed, t)
                    act.wait_ge(o_read, u)
                    nc.scalar.activation(rms[:].rearrange("p h c -> p (h c)"), sum_ps, ACT.Ln,
                                         bias=p.eps_rms[:]).then_inc(rms_mid, 1)
                    act.wait_ge(rms_mid, t)
                    nc.scalar.activation(rms[:], rms[:], ACT.Exp, scale=-0.5).then_inc(rms_done, 1)
                    act.wait_ge(gated_done, t)
                    if lag >= TAIL:
                        act.wait_ge(y_mm, t * 2 - 4)
                    nc.scalar.activation(o_hi[1 - s][:].rearrange("p k c -> p (k c)"), gated[:], ACT.Copy
                                         ).then_inc(o_hi_done, 1)
                if has(t, lag, 0):
                    act.wait_ge(o_mm, t + 1)
                    nc.scalar.activation(square[:], o_ps, ACT.Square).then_inc(squared, 1)
                if isinstance(t, int) and t in (0, 1):
                    for kt in range(t * RAW, (t + 1) * RAW):
                        act.wait_ge(raw_loaded[kt % RAW], (kt // RAW + 1) * DMA)
                        nc.scalar.activation(w_hi[:, kt, :], raw[kt % RAW][:], ACT.Copy).then_inc(w_hi_done, 1)
                if has(t, lag, LAG):
                    u = t - LAG
                    act.wait_ge(moments_done, u + 1)
                    act.wait_ge(normed, u)
                    nc.scalar.activation(rstd[:], moments[:, 1:2], ACT.Ln, bias=p.eps_ln[:]).then_inc(rstd_mid, 1)
                    act.wait_ge(rstd_mid, u + 1)
                    nc.scalar.activation(rstd[:], rstd[:], ACT.Exp, scale=-0.5).then_inc(rstd_done, 1)

            run(act, step)

        @block.vector
        def _(dve):
            for s in range(2):
                nc.vector.memset(scores[s][:], 0.0)
            nc.vector.memset(state[0][:], 0.0).then_inc(zeroed, 1)
            dve.wait_ge(zeroed, 1)

            def advance(t, s, c):
                now, then = state[(2 * s + c) % STATES], state[(2 * s + c + 1) % STATES]
                dve.wait_ge(kv_mm, t * 2 + c + 1)
                dve.wait_ge(states, t * 2 + c)
                for h in range(HEADS):
                    cols = slice(h * DV, (h + 1) * DV)
                    last = nc.vector.scalar_tensor_tensor(
                        out=then[:, cols], in0=now[:, cols], scalar=p.decay[:, h, ds(t * 2 + c, 1)],
                        in1=kv_ps[:, cols], op0=ALU.mult, op1=ALU.add)
                last.then_inc(states, 1)

            def gate(t, s, pair):
                by_head = lambda ap: ap.rearrange("p (h j c) -> p h j c", j=2, c=P)
                dve.wait_ge(rms_done, t)
                dve.wait_ge(o_lo_done, t - 1)
                nc.vector.tensor_tensor(by_head(gated[:]), by_head(o_ps),
                                        rms[:].unsqueeze(2).to_broadcast([P, HEADS, 2, P]), ALU.mult
                                        ).then_inc(o_read, 1)
                dve.wait_ge(o_read, t)
                dve.wait_ge(g_loaded[1 - s], (pair + s) * DMA)
                nc.vector.tensor_tensor(gated[:], gated[:], g[1 - s][:], ALU.mult).then_inc(gated_done, 1)

            def norm_end(t, s, pair):
                u = t - TAIL
                dve.wait_ge(rstd_done, u + 1)
                dve.wait_ge(moments_done, u + 1)
                dve.wait_ge(out_stored[1 - s], (pair + s - 2) * DMA)
                nc.vector.tensor_scalar(out[1 - s][:], res[:], moments[:, 0:1], rstd[:, 0:1], ALU.subtract, ALU.mult
                                        ).then_inc(normed, 1)
                dve.wait_ge(normed, u + 1)
                nc.vector.tensor_tensor(out[1 - s][:], out[1 - s][:], ln_g[:], ALU.mult).then_inc(scaled, 1)
                dve.wait_ge(scaled, u + 1)
                nc.vector.tensor_tensor(out[1 - s][:], out[1 - s][:], ln_b[:], ALU.add).then_inc(out_done, 1)

            def residual(t, s, pair):
                u = t - LAG
                dve.wait_ge(x_loaded[s], pair * DMA)
                dve.wait_ge(normed, u)
                for half in range(2):
                    cols = slice(half * BLK, (half + 1) * BLK)
                    dve.wait_ge(y_mm, u * 2 + half + 1)
                    nc.vector.scalar_tensor_tensor(out=res[:, cols], in0=x[s][:, cols], scalar=ALPHA,
                                                   in1=y_ps[half], op0=ALU.mult, op1=ALU.add).then_inc(y_read, 1)
                    dve.wait_ge(y_read, u * 2 + half + 1)
                    nc.vector.bn_stats(stats[:, half, :], res[:, cols]).then_inc(stats_done, 1)
                dve.wait_ge(stats_done, u * 2 + 2)
                nc.vector.memset(p.stats_carrier[:], 0.0)
                nc.vector.bn_aggr(moments[:], stats[:].rearrange("p a b -> p (a b)")).then_inc(moments_done, 1)

            def step(t, s, lag, pair):
                if has(t, lag, 1):
                    dve.wait_ge(squared, t)
                    two = square[:].rearrange("p (h j c) -> p h j c", j=2, c=P)
                    nc.vector.tensor_tensor(square_sum[:].rearrange("p (h c) -> p h c", c=P), two[:, :, 0, :],
                                            two[:, :, 1, :], ALU.add).then_inc(summed_squares, 1)
                if has(t, lag, 0):
                    dve.wait_ge(scored, t + 1)
                    nc.vector.memset(p.score_carrier[:], 0.0)
                    nc.vector.copy_predicated(scores[s][:], p.mask[:].rearrange("p h c -> p (h c)").bitcast(I32),
                                              score_ps).then_inc(masked, 1)
                    advance(t, s, 0)
                if has(t, lag, 1):
                    gate(t, s, pair)
                if has(t, lag, TAIL):
                    norm_end(t, s, pair)
                if has(t, lag, 0):
                    advance(t, s, 1)
                if has(t, lag, 1):
                    dve.wait_ge(o_hi_done, t)
                    dve.wait_ge(gated_done, t)
                    nc.vector.tensor_tensor(o_lo[1 - s][:].rearrange("p k c -> p (k c)"), gated[:],
                                            o_hi[1 - s][:].rearrange("p k c -> p (k c)").bitcast(F32), ALU.subtract
                                            ).then_inc(o_lo_done, 1)
                if isinstance(t, int) and t in (0, 1):
                    for kt in range(t * RAW, (t + 1) * RAW):
                        dve.wait_ge(w_hi_done, kt + 1)
                        nc.vector.tensor_tensor(w_lo[:, kt, :], raw[kt % RAW][:], w_hi[:, kt, :].bitcast(F32),
                                                ALU.subtract).then_inc(w_lo_done, 1)
                    dve.wait_ge(ln_loaded, 2 * DMA)
                if has(t, lag, LAG):
                    residual(t, s, pair)

            run(dve, step)


def pool_mix(nc, p, a):
    p.at = p.stream_at
    w_hi = [p.place(f"m_w_hi{s}", [P, KT, P], F32R) for s in range(2)]
    w_lo = [p.place(f"m_w_lo{s}", [P, KT, P], F32R) for s in range(2)]
    h_in, win_a, win_b = (p.place(f"m_{n}", [P, PAD + SEQ]) for n in ("h", "win_a", "win_b"))
    z = p.place("m_z", [P, SEQ])
    assert p.at <= p.out_m_at
    raw, rows, loaded, rows_loaded, ROWS = p.mix_raw, p.rows, p.mix_loaded, p.rows_loaded, p.ROWS
    phase = ExitStack()
    sem = lambda name: phase.enter_context(nc.semaphore("m_" + name))
    stored, hi, lo, h_mm, z_mm, h_copied, silu, chain, pooled, mixed, x_turned, x_hi, x_lo = (
        sem(n) for n in ("stored", "hi", "lo", "h_mm", "z_mm", "h_copied", "silu", "chain", "pooled", "mixed",
                         "x_turned", "x_hi", "x_lo"))
    FIRST = [("x", 0), ("x", 1), ("x", 2), ("x", 3), ("h", 0), ("x", 4), ("x", 5), ("z", 0), ("x", 6), ("x", 7),
             ("h", 1), ("x", 8), ("x", 9), ("z", 1), ("x", 10), ("x", 11), ("x", 12), ("x", 13), ("h", 2), ("x", 14),
             ("x", 15), ("z", 2), ("h", 3), ("z", 3)]
    REUSED_FROM = 12

    def x_banks(t):
        first = t % 2 * NB + (0 if t >= REUSED_FROM else 2)
        return p.ps[:, first:first + 2, :].rearrange("p b (k t) -> p (b k) t", t=P)

    def x_part(x, t):
        return x[:, :, t * P:(t + 1) * P]

    with phase, nc.Block() as block:

        @block.sync
        def _(sp):
            for t in range(p.ROWS_PREFETCHED, NT):
                if t >= ROWS:
                    sp.wait_ge(x_turned, t - ROWS + 1)
                sp.dma_start(rows[t % ROWS][:], p.x1[t * P:(t + 1) * P, :]).then_inc(rows_loaded[t % ROWS], DMA)
            with sp.Fori(1, MT) as m:
                sp.wait_ge(lo, m * 2)
                p.load_mix(sp, m)
                sp.wait_ge(mixed, m)
                sp.dma_start(p.mixed[ds(m - 1, 1), :, :].rearrange("o p c -> (o p) c"), z[:]).then_inc(stored, DMA)
            sp.wait_ge(x_turned, NT)
            sp.wait_ge(stored, DMA)
            p.prefetch_out(sp)
            sp.wait_ge(mixed, MT)
            sp.dma_start(p.mixed[MT - 1, :, :], z[:]).then_inc(stored, DMA)
            sp.wait_ge(stored, MT * DMA)

        @block.tensor
        def _(pe):
            def product(s, n):
                for k in range(KT):
                    last = split_product(nc, p.ps[:, s * NB + n, :], w_hi[s][:, k, :], w_lo[s][:, k, :],
                                         p.x_hi[:, k, n * BLK:(n + 1) * BLK],
                                         p.x_lo[:, k, n * BLK:(n + 1) * BLK], k == 0, k == KT - 1)
                last.then_inc((h_mm, z_mm)[s], 1)

            for what, n in FIRST:
                if what == "x":
                    pe.wait_ge(rows_loaded[n % ROWS], (n // ROWS + 1) * DMA)
                    if n in (REUSED_FROM, REUSED_FROM + 1):
                        pe.wait_ge((h_copied, silu)[n % 2], 2)
                    elif n >= 2:
                        pe.wait_ge(x_lo, n - 1)
                    for k in range(KT):
                        last = nc.tensor.transpose(x_banks(n)[:, k, :], rows[n % ROWS][:, k * P:(k + 1) * P],
                                                   p.ident[:])
                    last.then_inc(x_turned, 1)
                else:
                    s = "hz".index(what)
                    pe.wait_ge(lo, s + 1)
                    pe.wait_ge(x_lo, (n + 1) * NB)
                    product(s, n)
            with pe.Fori(1, MT) as m:
                for s, free in ((0, h_copied), (1, silu)):
                    pe.wait_ge(lo, m * 2 + s + 1)
                    pe.wait_ge(free, m * NB)
                    for n in range(NB):
                        product(s, n)

        @block.scalar
        def _(act):
            def part(s, m):
                act.wait_ge(loaded[s], (m + 1) * DMA)
                nc.scalar.activation(w_hi[s][:], raw[s][:], ACT.Copy).then_inc(hi, 1)

            def copy_h(m, n):
                act.wait_ge(h_mm, m * NB + n + 1)
                nc.scalar.activation(h_in[:, PAD + n * BLK:PAD + (n + 1) * BLK], p.ps[:, n, :],
                                     ACT.Copy).then_inc(h_copied, 1)

            def silu_z(m, n):
                act.wait_ge(z_mm, m * NB + n + 1)
                nc.scalar.activation(z[:, n * BLK:(n + 1) * BLK], p.ps[:, NB + n, :], ACT.Silu).then_inc(silu, 1)

            part(0, 0)
            for i, (what, n) in enumerate(FIRST):
                if what == "x":
                    act.wait_ge(x_turned, n + 1)
                    nc.scalar.activation(x_part(p.x_hi, n), x_banks(n), ACT.Copy).then_inc(x_hi, 1)
                elif what == "h":
                    copy_h(0, n)
                else:
                    silu_z(0, n)
                if i == 0:
                    part(1, 0)
                if (what, n) == ("h", NB - 1):
                    part(0, 1)

            def tile(m, last):
                act.wait_ge(z_mm, m * NB)
                part(1, m)
                act.wait_ge(pooled, m)
                for n in range(NB):
                    copy_h(m, n)
                if not last:
                    part(0, m + 1)
                act.wait_ge(stored, m * DMA)
                for n in range(NB):
                    silu_z(m, n)

            with act.Fori(1, MT - 1) as m:
                tile(m, False)
            tile(MT - 1, True)

        @block.vector
        def _(dve):
            for n, t in enumerate((h_in, win_a, win_b)):
                last = nc.vector.memset(t[:, 0:PAD], 0.0)
            last.then_inc(chain, 1)
            dve.wait_ge(chain, 1)
            dve.wait_ge(hi, 1)
            nc.vector.tensor_tensor(w_lo[0][:], raw[0][:], w_hi[0][:].bitcast(F32), ALU.subtract).then_inc(lo, 1)
            body = slice(PAD, PAD + SEQ)
            base = 1

            def tile(m, g, base, last):
                dve.wait_ge(hi, m * 2 + 2)
                nc.vector.tensor_tensor(w_lo[1][:], raw[1][:], w_hi[1][:].bitcast(F32), ALU.subtract).then_inc(lo, 1)
                if isinstance(m, int) and m == 0:
                    for t in range(NT):
                        dve.wait_ge(x_hi, t + 1)
                        nc.vector.tensor_tensor(x_part(p.x_lo, t), x_banks(t), x_part(p.x_hi, t).bitcast(F32),
                                                ALU.subtract).then_inc(x_lo, 1)
                if not last:
                    dve.wait_ge(hi, m * 2 + 3)
                    nc.vector.tensor_tensor(w_lo[0][:], raw[0][:], w_hi[0][:].bitcast(F32), ALU.subtract).then_inc(lo, 1)
                dve.wait_ge(mixed, m)
                dve.wait_ge(h_copied, m * NB + NB)
                src, step = h_in, 1
                for i in range(g + 1):
                    dst = (win_a, win_b)[i % 2]
                    nc.vector.tensor_tensor(dst[:, body], src[:, body], src[:, PAD - step:PAD + SEQ - step],
                                            ALU.add).then_inc(chain, 1)
                    dve.wait_ge(chain, base + i + 1)
                    src, step = dst, step * 2
                nc.vector.tensor_tensor(src[:, PAD:2 * PAD], src[:, PAD:2 * PAD], p.correct[:, g, :],
                                        ALU.mult).then_inc(chain, 1)
                dve.wait_ge(chain, base + g + 2)
                other = win_b if src is win_a else win_a
                nc.vector.scalar_tensor_tensor(out=other[:, body], in0=src[:, body], scalar=1.0 / WINDOWS[g],
                                               in1=h_in[:, body], op0=ALU.mult, op1=ALU.subtract).then_inc(pooled, 1)
                dve.wait_ge(pooled, m + 1)
                nc.vector.tensor_scalar(other[:, body], other[:, body], p.b_grp[:, ds(m, 1)], p.scale[:, ds(m, 1)],
                                        ALU.add, ALU.mult).then_inc(chain, 1)
                dve.wait_ge(chain, base + g + 3)
                dve.wait_ge(silu, m * NB + NB)
                nc.vector.tensor_tensor(z[:], z[:], other[:, body], ALU.mult).then_inc(mixed, 1)

            for g in range(GROUPS):
                per_tile = g + 3
                rolled = GT - 1 if g == GROUPS - 1 else GT
                if g == 0:
                    tile(0, g, base, False)
                with dve.Fori(1 if g == 0 else 0, rolled) as i:
                    tile(i + g * GT, g, i * per_tile + base, False)
                if rolled < GT:
                    tile(MT - 1, g, base + rolled * per_tile, True)
                base += GT * per_tile


def pool_out_and_norm(nc, p, a, out_dram):
    TB = 2
    BT = TB * P
    BLOCKS = SEQ // BT
    SLOTS = p.M_RAW
    p.at = p.ln_at
    ln_g = p.place("o_ln_g", [P, D])
    ln_b = p.place("o_ln_b", [P, D])
    w_hi = p.place("o_w_hi", [P, MT, D], F32R)
    w_lo = p.place("o_w_lo", [P, MT, D], F32R)
    m_hi = [p.place(f"o_m_hi{s}", [P, BT], F32R) for s in range(SLOTS)]
    m_lo = [p.place(f"o_m_lo{s}", [P, BT], F32R) for s in range(SLOTS)]
    m_raw = [p.m_raw0] + [p.place(f"o_m_raw{s}", [P, BT]) for s in range(1, SLOTS)]
    x = [p.place(f"o_x{s}", [P, D]) for s in range(TB)]
    res = [[p.place(f"o_res{b}{i}", [P, D]) for i in range(TB)] for b in range(2)]
    stats = [p.place(f"o_stats{i}", [P, 2, 6]) for i in range(TB)]
    moments = [p.place(f"o_moments{i}", [P, 2]) for i in range(TB)]
    rstd = [p.place(f"o_rstd{i}", [P, 1]) for i in range(TB)]
    assert p.at <= p.out_m_at
    raw, raw_loaded, RAW, m_loaded = p.out_raw, p.out_raw_loaded, p.ROWS, p.m_loaded
    phase = ExitStack()
    sem = lambda name: phase.enter_context(nc.semaphore("o_" + name))
    ln_loaded = sem("ln_loaded")
    x_loaded = [sem(f"x_loaded{i}") for i in range(TB)]
    stored = [[sem(f"stored{b}{i}") for i in range(TB)] for b in range(2)]
    (w_hi_done, w_lo_done, hi, lo, step_mm, y_mm, y_read, stats_done, moments_done, rstd_mid, rstd_done, normed,
     scaled, out_done) = (
        sem(n) for n in ("w_hi_done", "w_lo_done", "hi", "lo", "step_mm", "y_mm", "y_read", "stats_done",
                         "moments_done", "rstd_mid", "rstd_done", "normed", "scaled", "out_done"))
    RESIDUAL_AFTER = 1
    NORM_AFTER = {4: 0, 8: 1}
    STORE_AFTER = {9: 0, 13: 1}
    READ_BASE = TB * 2

    def banks(parity, i):
        return [p.ps[:, parity * 4 + i * 2 + half, :] for half in range(2)]

    def run(engine, block):
        for parity in range(2):
            block(parity, parity, 0)
        with engine.Fori(1, BLOCKS // 2) as pair:
            for parity in range(2):
                block(pair * 2 + parity, parity, pair)

    def is_first(b):
        return isinstance(b, int) and b == 0

    with phase, nc.Block() as block:

        @block.sync
        def _(sp):
            def load_x(b):
                for i in range(TB):
                    sp.dma_start(x[i][:], p.x1[ds((b * TB + i) * P, P), :]).then_inc(x_loaded[i], DMA)

            def store(b, parity, i):
                sp.wait_ge(out_done, b * TB + i + 1)
                sp.dma_start(out_dram[ds((b * TB + i) * P, P), :], res[parity][i][:]).then_inc(stored[parity][i], DMA)

            def blk(b, parity, pair):
                for k in range(MT):
                    if is_first(b):
                        if k >= p.M_PREFETCHED:
                            if k >= SLOTS:
                                sp.wait_ge(lo, k - SLOTS + 1)
                            p.load_m(sp, m_raw, 0, k)
                        if k >= p.OUT_PREFETCHED:
                            sp.wait_ge(w_lo_done, k - RAW + 1)
                            p.load_out(sp, k)
                    else:
                        sp.wait_ge(lo, b * MT + k - SLOTS + 1)
                        p.load_m(sp, m_raw, b, k)
                        if k == RESIDUAL_AFTER + SLOTS:
                            sp.wait_ge(y_read, READ_BASE + b * TB * 2)
                            load_x(b)
                        if k in STORE_AFTER:
                            store(b - 1, 1 - parity, STORE_AFTER[k])
                if is_first(b):
                    for ln, src in ((ln_g, a["ln_g"]), (ln_b, a["ln_b"])):
                        sp.dma_start(ln[:], src[1:2, :].to_broadcast([P, D])).then_inc(ln_loaded, DMA)
                    load_x(0)

            run(sp, blk)
            for i in range(TB):
                store(BLOCKS - 1, 1, i)
            for b in range(2):
                for i in range(TB):
                    sp.wait_ge(stored[b][i], BLOCKS // 2 * DMA)

        @block.tensor
        def _(pe):
            with pe.Fori(0, BLOCKS // 2) as pair:
                for parity in range(2):
                    b = pair * 2 + parity
                    for k in range(MT):
                        pe.wait_ge(lo, b * MT + k + 1)
                        pe.wait_ge(w_lo_done, k + 1)
                        if k == 0:
                            pe.wait_ge(y_read, b * TB * 2)
                        for i in range(TB):
                            for half in range(2):
                                cols = slice(half * BLK, (half + 1) * BLK)
                                last = split_product(nc, banks(parity, i)[half],
                                                     m_hi[k % SLOTS][:, i * P:(i + 1) * P],
                                                     m_lo[k % SLOTS][:, i * P:(i + 1) * P],
                                                     w_hi[:, k, cols], w_lo[:, k, cols], k == 0, k == MT - 1)
                                if k == MT - 1:
                                    last.then_inc(y_mm, 1)
                        if k < MT - 1:
                            last.then_inc(step_mm, 1)

        STEPS = MT - 1

        @block.scalar
        def _(act):
            def norm_rstd(b, i):
                t = b * TB + i
                act.wait_ge(moments_done, t + 1)
                nc.scalar.activation(rstd[i][:], moments[i][:, 1:2], ACT.Ln, bias=p.eps_ln[:]).then_inc(rstd_mid, 1)
                act.wait_ge(rstd_mid, t + 1)
                nc.scalar.activation(rstd[i][:], rstd[i][:], ACT.Exp, scale=-0.5).then_inc(rstd_done, 1)

            def blk(b, parity, pair):
                for k in range(MT):
                    if is_first(b):
                        act.wait_ge(m_loaded[k % SLOTS], (k // SLOTS + 1) * DMA)
                        if k >= SLOTS:
                            act.wait_ge(step_mm, k - SLOTS + 1)
                    else:
                        act.wait_ge(m_loaded[k % SLOTS], (b * (MT // SLOTS) + k // SLOTS + 1) * DMA)
                        if k >= SLOTS:
                            act.wait_ge(step_mm, b * STEPS + k - SLOTS + 1)
                        elif k == SLOTS - 1:
                            act.wait_ge(y_mm, b * TB * 2)
                        else:
                            act.wait_ge(step_mm, (b - 1) * STEPS + MT + k - SLOTS + 1)
                    nc.scalar.activation(m_hi[k % SLOTS][:], m_raw[k % SLOTS][:], ACT.Copy).then_inc(hi, 1)
                    if is_first(b):
                        act.wait_ge(raw_loaded[k % RAW], (k // RAW + 1) * DMA)
                        nc.scalar.activation(w_hi[:, k, :], raw[k % RAW][:], ACT.Copy).then_inc(w_hi_done, 1)
                    elif k in NORM_AFTER:
                        norm_rstd(b - 1, NORM_AFTER[k])

            nc.scalar.preload_act_table_set("natural_log_exp_and_others")
            run(act, blk)
            for i in range(TB):
                norm_rstd(BLOCKS - 1, i)

        @block.vector
        def _(dve):
            dve.sem_inc(y_read, READ_BASE)

            def residual(b, parity, pair, i):
                dve.wait_ge(x_loaded[i], (b + 1) * DMA)
                dve.wait_ge(stored[parity][i], pair * DMA)
                for half in range(2):
                    cols = slice(half * BLK, (half + 1) * BLK)
                    dve.wait_ge(y_mm, (b * TB + i) * 2 + half + 1)
                    nc.vector.scalar_tensor_tensor(out=res[parity][i][:, cols], in0=x[i][:, cols], scalar=ALPHA,
                                                   in1=banks(parity, i)[half], op0=ALU.mult, op1=ALU.add
                                                   ).then_inc(y_read, 1)

            def norm_moments(b, parity, i):
                t = b * TB + i
                dve.wait_ge(y_read, READ_BASE + t * 2 + 2)
                for half in range(2):
                    nc.vector.bn_stats(stats[i][:, half, :], res[parity][i][:, half * BLK:(half + 1) * BLK]
                                       ).then_inc(stats_done, 1)
                dve.wait_ge(stats_done, t * 2 + 2)
                nc.vector.memset(p.stats_carrier[:], 0.0)
                nc.vector.bn_aggr(moments[i][:], stats[i][:].rearrange("p a b -> p (a b)")).then_inc(moments_done, 1)

            def norm_end(b, parity, i):
                t, r = b * TB + i, res[parity][i]
                dve.wait_ge(moments_done, t + 1)
                dve.wait_ge(rstd_done, t + 1)
                nc.vector.tensor_scalar(r[:], r[:], moments[i][:, 0:1], rstd[i][:, 0:1], ALU.subtract, ALU.mult
                                        ).then_inc(normed, 1)
                dve.wait_ge(normed, t + 1)
                nc.vector.tensor_tensor(r[:], r[:], ln_g[:], ALU.mult).then_inc(scaled, 1)
                dve.wait_ge(scaled, t + 1)
                nc.vector.tensor_tensor(r[:], r[:], ln_b[:], ALU.add).then_inc(out_done, 1)

            def blk(b, parity, pair):
                for k in range(MT):
                    dve.wait_ge(hi, b * MT + k + 1)
                    nc.vector.tensor_tensor(m_lo[k % SLOTS][:], m_raw[k % SLOTS][:], m_hi[k % SLOTS][:].bitcast(F32),
                                            ALU.subtract).then_inc(lo, 1)
                    if is_first(b):
                        dve.wait_ge(w_hi_done, k + 1)
                        nc.vector.tensor_tensor(w_lo[:, k, :], raw[k % RAW][:], w_hi[:, k, :].bitcast(F32),
                                                ALU.subtract).then_inc(w_lo_done, 1)
                    else:
                        if k == RESIDUAL_AFTER:
                            for i in range(TB):
                                residual(b - 1, 1 - parity, pair - 1 + parity, i)
                        if k in NORM_AFTER:
                            norm_moments(b - 1, 1 - parity, NORM_AFTER[k])
                            norm_end(b - 1, 1 - parity, NORM_AFTER[k])
                if is_first(b):
                    dve.wait_ge(ln_loaded, 2 * DMA)

            run(dve, blk)
            for i in range(TB):
                residual(BLOCKS - 1, 1, BLOCKS // 2 - 1, i)
                norm_moments(BLOCKS - 1, 1, i)
            for i in range(TB):
                norm_end(BLOCKS - 1, 1, i)


def gla_pool_trunk(nc, a, out_dram):
    with ExitStack() as ctx:
        p = Program(nc, ctx, a)
        prepare(nc, p, a)
        project(nc, p, a)
        attend_and_norm(nc, p, a)
        pool_mix(nc, p, a)
        pool_out_and_norm(nc, p, a, out_dram)


_INS = ["x", "gla_w_in", "gla_w_gk", "gla_b_gk", "gla_norm_w", "gla_w_out", "pool_w_in", "pool_w_grp",
        "pool_b_grp", "pool_scale", "pool_w_out", "ln_g", "ln_b"]


def kernel(**inputs):
    import numpy as np
    import concourse.bacc as bacc
    from concourse.bass_utils import run_bass_kernel_spmd

    nc = bacc.Bacc("TRN2", target_bir_lowering=False, num_devices=1)
    arrays, a = {}, {}
    for name in _INS:
        arrays[f"in_{name}"] = np.ascontiguousarray(inputs[name])
        a[name] = nc.dram_tensor(f"in_{name}", arrays[f"in_{name}"].shape, F32, kind="ExternalInput").ap()
    out = nc.dram_tensor("out", (1, SEQ, D), F32, kind="ExternalOutput").ap()
    gla_pool_trunk(nc, a, out[0])
    r = run_bass_kernel_spmd(nc, [arrays], core_ids=[0])
    return r.results[0]["out"]
```

```python
import concourse.bass as bass
from concourse import mybir
from contextlib import ExitStack

F32 = mybir.dt.float32
F32R = mybir.dt.float32r
I32 = mybir.dt.int32
ALU = mybir.AluOpType
ACT = mybir.ActivationFunctionType
ds = bass.ds

P = 128
SEQ = 2048
D = 1024
KT = D // P
HEADS = 4
DK = 128
DV = 256
CHUNK = 64
GATE_RANK = 16
GATE_NORMALIZER = 16.0
NT = SEQ // P
BLK = 512
NB = SEQ // BLK
KD = HEADS * DK
VD = HEADS * DV
POOL_W = 2048
WINDOWS = (2, 4, 8, 16)
GROUPS = len(WINDOWS)
GW = POOL_W // GROUPS
GT = GW // P
MT = POOL_W // P
PAD = max(WINDOWS)
ALPHA = 4.0 ** 0.25
LN_EPS = 1e-5
RMS_EPS = 1e-6
SBUF_START, SBUF_END = 16512, 229344
DMA = 16



class Program:

    V_RAW, V_PREFETCHED = 4, 2
    ROWS, ROWS_PREFETCHED = 4, 4
    OUT_PREFETCHED = 4
    M_RAW, M_PREFETCHED = 4, 4
    QKV_LOADS = 5
    REUSED_FROM = 12
    TURNED_AHEAD = 2
    BT = 2 * P

    def __init__(self, nc, ctx, a):
        self.nc, self.at, self.a = nc, SBUF_START, a
        sems = lambda name, n: [ctx.enter_context(nc.semaphore(f"{name}{i}")) for i in range(n)]
        self.ps = ctx.enter_context(nc.psum_tensor("banks", [P, 8, BLK], F32))
        scratch = lambda name, shape: nc.dram_tensor(name, shape, F32).ap()
        self.w_fused = scratch("w_fused", [MT, P, KT, P])
        self.q_tiles, self.k_tiles, self.k2_tiles, self.kn_tiles = (
            scratch(n, [NT, P, KD]) for n in ("q_tiles", "k_tiles", "k2_tiles", "kn_tiles"))
        self.v_tiles, self.g_tiles = (scratch(n, [NT, P, VD]) for n in ("v_tiles", "g_tiles"))
        self.x1 = scratch("x1", [SEQ, D])
        self.mixed = scratch("mixed", [MT, P, SEQ])
        self.ident = self.place("ident", [P, P])
        self.mean_w = self.place("mean_w", [P, P], F32R)
        self.mask = self.place("mask", [P, HEADS, P])
        self.keep = self.place("keep", [P, BLK])
        self.correct = self.place("correct", [P, GROUPS, PAD])
        self.decay = self.place("decay", [P, HEADS, SEQ // CHUNK])
        self.b_gk = self.place("b_gk", [P, HEADS])
        self.norm_w = self.place("norm_w", [P, DV // P])
        self.b_grp = self.place("b_grp", [P, MT])
        self.scale = self.place("scale", [P, MT])
        self.score_carrier = self.place("score_carrier", [P, 1])
        self.stats_carrier = self.place("stats_carrier", [P, 1])
        self.eps_rms = self.place("eps_rms", [P, 1])
        self.eps_ln = self.place("eps_ln", [P, 1])
        self.ln_at = self.at
        self.x_hi = self.place("x_hi", [P, KT, SEQ], F32R)
        self.x_lo = self.place("x_lo", [P, KT, SEQ], F32R)
        self.stream_at = self.at
        self.qkv_at = self.at = self.stream_at + 2 * KT * P * 4
        self.q = [self.place(f"q{s}", [P, HEADS, P + CHUNK]) for s in range(2)]
        self.k, self.k2, self.kn = ([self.place(f"{n}{s}", [P, KD]) for s in range(2)] for n in ("k", "k2", "kn"))
        self.v = [self.place(f"v{s}", [P, VD]) for s in range(2)]
        self.qkv_end = self.at
        self.qkv_loaded = sems("qkv_loaded", 2)
        self.fused_stored, self.g_stored, self.x1_stored = (
            sems(n, 2) for n in ("fused_stored", "g_stored", "x1_stored"))
        self.mixed_stored = sems("mixed_stored", 1)[0]
        self.v_raw_at = SBUF_END - self.V_RAW * BLK * 4
        self.at = self.v_raw_at
        late = [self.place(f"v_raw{s}", [P, BLK]) for s in (2, 3)]
        self.v_raw = [self.place(f"v_raw{s}", [P, BLK]) for s in (0, 1)] + late
        self.v_loaded = sems("v_loaded", self.V_RAW)
        self.rows_at = SBUF_END - self.ROWS * D * 4
        self.at = self.rows_at
        self.rows = [self.place(f"rows{s}", [P, D]) for s in range(self.ROWS)]
        self.rows_loaded = sems("rows_loaded", self.ROWS)
        self.x1_turned = sems("x1_turned", 1)[0]
        self.at = self.rows_at
        self.out_raw = [self.place(f"out_raw{s}", [P, D]) for s in range(self.ROWS)]
        self.out_raw_loaded = sems("out_raw_loaded", self.ROWS)
        self.mix_raw_at = self.rows_at - 2 * KT * P * 4
        self.at = self.mix_raw_at
        self.mix_raw = [self.place(f"mix_raw{s}", [P, KT, P]) for s in range(2)]
        self.mix_loaded = sems("mix_loaded", 2)
        self.at = self.stream_at
        self.mix_hi = [self.place(f"mix_hi{s}", [P, KT, P], F32R) for s in range(2)]
        self.mix_lo = [self.place(f"mix_lo{s}", [P, KT, P], F32R) for s in range(2)]
        self.mix_end = self.at
        self.mix_hi_done, self.mix_lo_done = sems("mix_hi_done", 1)[0], sems("mix_lo_done", 1)[0]
        self.at = self.mix_raw_at
        self.m_raw = [self.place(f"m_raw{s}", [P, self.BT]) for s in range(self.M_RAW)]
        self.m_loaded = sems("m_loaded", self.M_RAW)

    def place(self, name, shape, dtype=F32):
        size = 4
        for n in shape[1:]:
            size *= n
        t = self.nc.alloc_sbuf_tensor_at(name, shape, dtype, offset=self.at)
        self.at += (size + 31) // 32 * 32
        return t

    def prefetch_values(self, sp):
        w_src = self.a["gla_w_in"][0].rearrange("(k p) c -> p k c", p=P)
        for k in range(self.V_PREFETCHED):
            sp.dma_start(self.v_raw[k][:], w_src[:, k, 2 * KD:2 * KD + BLK]).then_inc(self.v_loaded[k], DMA)

    def load_qkv(self, sp, t, s):
        sp.dma_start(self.q[s][:, :, 0:P], self.q_tiles[ds(t, 1), :, :].rearrange("o p (h c) -> (o p) h c", c=P)
                     ).then_inc(self.qkv_loaded[s], DMA)
        for dst, src in ((self.k, self.k_tiles), (self.k2, self.k2_tiles), (self.kn, self.kn_tiles),
                         (self.v, self.v_tiles)):
            sp.dma_start(dst[s][:], src[ds(t, 1), :, :].rearrange("o p c -> (o p) c")).then_inc(self.qkv_loaded[s], DMA)

    def load_mix(self, sp, m):
        z_src = self.a["pool_w_in"][0].rearrange("(k p) c -> p k c", p=P)
        sp.dma_start(self.mix_raw[0][:], self.w_fused[ds(m, 1), :, :, :].rearrange("o p k c -> (o p) k c")
                     ).then_inc(self.mix_loaded[0], DMA)
        sp.dma_start(self.mix_raw[1][:], z_src[:, :, ds(m * P + POOL_W, P)]).then_inc(self.mix_loaded[1], DMA)

    def mix_hi_part(self, act, s, m):
        act.wait_ge(self.mix_loaded[s], (m + 1) * DMA)
        self.nc.scalar.activation(self.mix_hi[s][:], self.mix_raw[s][:], ACT.Copy).then_inc(self.mix_hi_done, 1)

    def mix_lo_part(self, dve, s, m):
        dve.wait_ge(self.mix_hi_done, m * 2 + s + 1)
        self.nc.vector.tensor_tensor(self.mix_lo[s][:], self.mix_raw[s][:], self.mix_hi[s][:].bitcast(F32),
                                     ALU.subtract).then_inc(self.mix_lo_done, 1)

    def x_banks(self, t):
        first = NB if t == 1 else t % 2 * NB + (0 if t >= self.REUSED_FROM else 2)
        return self.ps[:, first:first + 2, :].rearrange("p b (k t) -> p (b k) t", t=P)

    def turn_x1(self, pe, t):
        pe.wait_ge(self.rows_loaded[t % self.ROWS], (t // self.ROWS + 1) * DMA)
        for k in range(KT):
            last = self.nc.tensor.transpose(self.x_banks(t)[:, k, :], self.rows[t % self.ROWS][:, k * P:(k + 1) * P],
                                            self.ident[:])
        last.then_inc(self.x1_turned, 1)

    def prefetch_mix(self, sp):
        self.load_mix(sp, 0)
        for t in range(self.ROWS_PREFETCHED):
            sp.dma_start(self.rows[t][:], self.x1[t * P:(t + 1) * P, :]).then_inc(self.rows_loaded[t], DMA)

    def load_m(self, sp, b, k):
        sp.dma_start(self.m_raw[k % self.M_RAW][:], self.mixed[k, :, ds(b * self.BT, self.BT)]
                     ).then_inc(self.m_loaded[k % self.M_RAW], DMA)

    def load_out(self, sp, k):
        w_src = self.a["pool_w_out"][0].rearrange("(k p) c -> p k c", p=P)
        sp.dma_start(self.out_raw[k % self.ROWS][:], w_src[:, k, :]).then_inc(self.out_raw_loaded[k % self.ROWS], DMA)

    def prefetch_out(self, sp):
        for k in range(self.OUT_PREFETCHED):
            self.load_out(sp, k)
        for k in range(self.M_PREFETCHED):
            self.load_m(sp, 0, k)


def split_product(nc, out, a_hi, a_lo, b_hi, b_lo, first, last):
    nc.tensor.matmul(out, a_hi, b_hi, start=first, stop=False, skip_group_check=True)
    nc.tensor.matmul(out, a_hi, b_lo, start=False, stop=False, skip_group_check=True)
    return nc.tensor.matmul(out, a_lo, b_hi, start=False, stop=last, skip_group_check=True)


def prepare(nc, p, a):
    IN, ROWS = 4, 2
    p.at = p.stream_at
    w_in = [p.place(f"p_in{s}", [P, GW]) for s in range(IN)]
    w_grp = p.place("p_grp", [P, GT, GW])
    grp_hi = [p.place(f"p_grp_hi{s}", [P, GT, GW], F32R) for s in range(2)]
    grp_lo = [p.place(f"p_grp_lo{s}", [P, GT, GW], F32R) for s in range(2)]
    t_hi = [p.place(f"p_t_hi{s}", [P, GT, P], F32R) for s in range(2)]
    t_lo = [p.place(f"p_t_lo{s}", [P, GT, P], F32R) for s in range(2)]
    out = [p.place(f"p_out{s}", [P, GW]) for s in range(2)]
    rows = [p.place(f"p_rows{s}", [P, D]) for s in range(ROWS)]
    with ExitStack() as phase:
        sem = lambda name: phase.enter_context(nc.semaphore("p_" + name))
        in_loaded = [sem(f"in_loaded{s}") for s in range(IN)]
        rows_loaded = [sem(f"rows_loaded{s}") for s in range(ROWS)]
        stored = p.fused_stored
        grp_loaded = [sem(f"grp_loaded{c}") for c in range(GT)]
        (g_hi, g_lo, turned, hi, lo, multiplied, copied, x_turned, x_hi, x_lo, pool_done, ones_in,
         columns) = (
            sem(n) for n in ("g_hi", "g_lo", "turned", "hi", "lo", "multiplied", "copied", "x_turned",
                             "x_hi", "x_lo", "pool_done", "ones_in", "columns"))
        src_in = a["pool_w_in"][0].rearrange("(k p) c -> k p c", p=P)
        src_grp = a["pool_w_grp"][0].rearrange("g (k p) c -> p g k c", p=P)
        turned_ps = [p.ps[:, s, :] for s in range(2)]
        out_ps = [p.ps[:, 2 + s, :] for s in range(2)]
        x_ps = [p.ps[:, 4 + 2 * s:6 + 2 * s, :].rearrange("p b (k t) -> p (b k) t", t=P) for s in range(2)]
        TILES = GROUPS * KT
        SPLIT_AT = 2

        def x_tile(n):
            return n // 2 if n % 2 else None

        def constants(dve):
            nc.vector.memset(p.mean_w[:].bitcast(F32), 1.0 / DV)
            nc.vector.memset(p.eps_rms[:], RMS_EPS)
            nc.vector.memset(p.eps_ln[:], LN_EPS)
            nc.vector.memset(p.keep[:], 1.0).then_inc(ones_in, 1)
            nc.vector.memset(p.correct[:], 1.0).then_inc(ones_in, 1)
            dve.wait_ge(ones_in, 2)
            nc.vector.memset(p.keep[:].rearrange("p (c s) -> p c s", s=CHUNK)[:, :, 0:1], 0.0)
            for g, w in enumerate(WINDOWS):
                for t in range(w - 1):
                    nc.vector.memset(p.correct[:, g, t:t + 1], w / (t + 1.0))

        with nc.Block() as block:

            @block.sync
            def _(sp):
                def load_in(n):
                    if n >= IN:
                        sp.wait_ge(turned, n - IN + 1)
                    sp.dma_start(w_in[n % IN][:], src_in[n % KT, :, n // KT * GW:(n // KT + 1) * GW]
                                 ).then_inc(in_loaded[n % IN], DMA)

                def load_x(t):
                    if t >= ROWS:
                        sp.wait_ge(x_turned, t - ROWS + 1)
                    sp.dma_start(rows[t % ROWS][:], a["x"][0][t * P:(t + 1) * P, :]).then_inc(rows_loaded[t % ROWS], DMA)

                def load_grp(g):
                    for c in range(GT):
                        if g:
                            sp.wait_ge(g_lo, (g - 1) * GT + c + 1)
                        sp.dma_start(w_grp[:, c, :], src_grp[:, g, c, :]).then_inc(grp_loaded[c], DMA)

                def store(n):
                    sp.wait_ge(copied, n + 1)
                    sp.dma_start(p.w_fused[n // KT * GT:(n // KT + 1) * GT, :, n % KT, :].rearrange("m p c -> p m c"),
                                 out[n % 2][:].rearrange("p (m c) -> p m c", c=P)).then_inc(stored[n % 2], DMA)

                def load_columns():
                    with nc.allow_non_contiguous_dma(reason="small parameter vectors as columns"):
                        for dst, src in ((p.b_gk, a["gla_b_gk"][0].rearrange("(h d) -> d h", d=P)),
                                         (p.norm_w, a["gla_norm_w"][0].rearrange("(j d) -> d j", d=P)),
                                         (p.b_grp, a["pool_b_grp"][0].rearrange("g (m d) -> d (g m)", d=P)),
                                         (p.scale, a["pool_scale"][0].rearrange("(m d) -> d m", d=P))):
                            sp.dma_start(dst[:], src).then_inc(columns, DMA)

                load_in(0)
                load_grp(0)
                for n in range(1, IN - 1):
                    load_in(n)
                load_x(0)
                for n in range(TILES):
                    if n + IN - 1 < TILES:
                        load_in(n + IN - 1)
                    if x_tile(n) is not None and x_tile(n) + 1 < NT:
                        load_x(x_tile(n) + 1)
                    if n >= 2:
                        store(n - 2)
                    if n % KT == 0 and n // KT + 1 < GROUPS:
                        load_grp(n // KT + 1)
                    if n == TILES // 2:
                        load_columns()
                    if n == TILES - 4:
                        p.prefetch_values(sp)
                for n in (TILES - 2, TILES - 1):
                    store(n)
                sp.wait_ge(columns, 4 * DMA)

            @block.gpsimd
            def _(pool):
                nc.gpsimd.memset(p.ident[:], 0.0).then_inc(pool_done, 1)
                pool.wait_ge(pool_done, 1)
                nc.gpsimd.affine_select(out=p.ident[:], in_=p.ident[:], compare_op=ALU.not_equal, fill=1.0,
                                        base=0, pattern=[[-1, P]], channel_multiplier=1).then_inc(pool_done, 1)
                nc.gpsimd.memset(p.mask[:], 1.0).then_inc(pool_done, 1)
                pool.wait_ge(pool_done, 3)
                nc.gpsimd.affine_select(out=p.mask[:], in_=p.mask[:], compare_op=ALU.is_ge, fill=0.0,
                                        base=0, pattern=[[0, HEADS], [1, P]], channel_multiplier=-1
                                        )

            @block.tensor
            def _(pe):
                def turn(n):
                    pe.wait_ge(in_loaded[n % IN], (n // IN + 1) * DMA)
                    if n >= 2:
                        pe.wait_ge(lo, n - 1)
                    for c in range(GT):
                        last = nc.tensor.transpose(turned_ps[n % 2][:, c * P:(c + 1) * P],
                                                   w_in[n % IN][:, c * P:(c + 1) * P], p.ident[:])
                    last.then_inc(turned, 1)

                def turn_x(t):
                    pe.wait_ge(rows_loaded[t % ROWS], (t // ROWS + 1) * DMA)
                    if t >= 2:
                        pe.wait_ge(x_lo, t - 1)
                    for k in range(KT):
                        last = nc.tensor.transpose(x_ps[t % 2][:, k, :], rows[t % ROWS][:, k * P:(k + 1) * P],
                                                   p.ident[:])
                    last.then_inc(x_turned, 1)

                pe.wait_ge(pool_done, 2)
                turn(0)
                for n in range(TILES):
                    if n + 1 < TILES:
                        turn(n + 1)
                    if x_tile(n) is not None:
                        turn_x(x_tile(n))
                    g = n // KT
                    pe.wait_ge(lo, n + 1)
                    if n >= 2:
                        pe.wait_ge(copied, n - 1)
                    for c in range(GT):
                        if n % KT == 0:
                            pe.wait_ge(g_lo, g * GT + c + 1)
                        last = split_product(nc, out_ps[n % 2], t_hi[n % 2][:, c, :], t_lo[n % 2][:, c, :],
                                             grp_hi[g % 2][:, c, :], grp_lo[g % 2][:, c, :], c == 0, c == GT - 1)
                    last.then_inc(multiplied, 1)

            @block.scalar
            def _(act):
                def copy_out(n):
                    act.wait_ge(multiplied, n + 1)
                    if n >= 2:
                        act.wait_ge(stored[n % 2], n // 2 * DMA)
                    nc.scalar.activation(out[n % 2][:], out_ps[n % 2], ACT.Copy).then_inc(copied, 1)

                def grp_part(g, c):
                    act.wait_ge(grp_loaded[c], (g + 1) * DMA)
                    if g >= 2:
                        act.wait_ge(multiplied, (g - 1) * KT)
                    nc.scalar.activation(grp_hi[g % 2][:, c, :], w_grp[:, c, :], ACT.Copy).then_inc(g_hi, 1)

                for n in range(TILES):
                    act.wait_ge(turned, n + 1)
                    if n >= 2:
                        act.wait_ge(multiplied, n - 1)
                    nc.scalar.activation(t_hi[n % 2][:].rearrange("p c d -> p (c d)"), turned_ps[n % 2],
                                         ACT.Copy).then_inc(hi, 1)
                    if n == 0:
                        for c in range(GT):
                            grp_part(0, c)
                    elif 0 <= n % KT - SPLIT_AT < GT and n // KT + 1 < GROUPS:
                        grp_part(n // KT + 1, n % KT - SPLIT_AT)
                    if x_tile(n) is not None:
                        t = x_tile(n)
                        act.wait_ge(x_turned, t + 1)
                        nc.scalar.activation(p.x_hi[:, :, t * P:(t + 1) * P], x_ps[t % 2], ACT.Copy).then_inc(x_hi, 1)
                    if n >= 1:
                        copy_out(n - 1)
                copy_out(TILES - 1)

            @block.vector
            def _(dve):
                def grp_part(g, c):
                    dve.wait_ge(g_hi, g * GT + c + 1)
                    nc.vector.tensor_tensor(grp_lo[g % 2][:, c, :], w_grp[:, c, :], grp_hi[g % 2][:, c, :].bitcast(F32),
                                            ALU.subtract).then_inc(g_lo, 1)

                for n in range(TILES):
                    dve.wait_ge(hi, n + 1)
                    nc.vector.tensor_tensor(t_lo[n % 2][:].rearrange("p c d -> p (c d)"), turned_ps[n % 2],
                                            t_hi[n % 2][:].rearrange("p c d -> p (c d)").bitcast(F32),
                                            ALU.subtract).then_inc(lo, 1)
                    if n == 0:
                        for c in range(GT):
                            grp_part(0, c)
                        constants(dve)
                    elif 0 <= n % KT - SPLIT_AT < GT and n // KT + 1 < GROUPS:
                        grp_part(n // KT + 1, n % KT - SPLIT_AT)
                    if x_tile(n) is not None:
                        t = x_tile(n)
                        dve.wait_ge(x_hi, t + 1)
                        nc.vector.tensor_tensor(p.x_lo[:, :, t * P:(t + 1) * P], x_ps[t % 2],
                                                p.x_hi[:, :, t * P:(t + 1) * P].bitcast(F32), ALU.subtract
                                                ).then_inc(x_lo, 1)


def project(nc, p, a):
    HALVES, V_OUT, BANKS = 2, 2, 4
    PAIR_ROWS = 2 * GATE_RANK
    RANK_ROWS = 3 * PAIR_ROWS
    p.at = p.stream_at
    v_hi = p.place("v_hi", [P, KT, BLK], F32R)
    v_lo = p.place("v_lo", [P, KT, BLK], F32R)
    v_out = [p.place(f"v_out{s}", [P, BLK]) for s in range(V_OUT)]
    v_raw = p.v_raw
    p.at = p.qkv_at + 4 * SEQ * 4
    raw = [p.place(f"h_raw{s}", [P, KT, P]) for s in range(2)]
    w_hi0, w_lo0 = p.place("h_w_hi0", [P, KT, P], F32R), p.place("h_w_lo0", [P, KT, P], F32R)
    rank_raw = p.place("h_rank_raw", [P, KT, GATE_RANK])
    w_gk_raw = p.place("h_w_gk_raw", [RANK_ROWS, P])
    w_gk = p.place("h_w_gk", [RANK_ROWS, P], F32R)
    chunk_end = p.place("h_chunk_end", [P, SEQ // CHUNK])
    early_at = p.at
    rank_w = p.place("h_rank_w", [P, KT, P], F32R)
    p.at = early_at
    kn_out = [p.place(f"h_kn_out{s}", [P, BLK]) for s in range(2)]
    p.at = p.v_raw_at
    k2_out = [p.place(f"h_k2_out{s}", [P, BLK]) for s in range(2)]
    g_out = [p.place(f"h_g_out{s}", [P, BLK]) for s in range(2)]
    p.at = p.stream_at
    w_hi1, w_lo1 = p.place("h_w_hi1", [P, KT, P], F32R), p.place("h_w_lo1", [P, KT, P], F32R)
    assert p.at == p.qkv_at
    rank = p.place("h_rank", [RANK_ROWS, SEQ], F32R)
    e_q = p.place("h_e_q", [P, SEQ])
    e_k = p.place("h_e_k", [P, SEQ])
    sums_at = p.at
    p.at = early_at + 2 * BLK * 4
    q_out = [p.place(f"h_q_out{s}", [P, BLK]) for s in range(2)]
    assert p.at <= p.v_raw_at
    p.at = sums_at
    sums = p.place("h_sums", [P, SEQ])
    w_hi, w_lo = [w_hi0, w_hi1], [w_lo0, w_lo1]

    phase = ExitStack()
    sem = lambda name: phase.enter_context(nc.semaphore("h_" + name))
    loaded, v_stored = [sem(f"loaded{s}") for s in range(2)], [sem(f"v_stored{s}") for s in range(V_OUT)]
    v_loaded = p.v_loaded
    rank_loaded, gk_loaded = sem("rank_loaded"), sem("gk_loaded")
    (zeroed, rank_hi, rank_lo, rank_mm, rank_ready, hi, lo, gk_mm, scanned, ln_done, chain,
     sums_ready, exps_ready, qk_done, tiles_mm, turned, kn_copied, silu, g_done, v_hi_done, v_lo_done, v_mm,
     v_copied, v_free, gk_hi, gk_lo, rank_rounded) = (
        sem(n) for n in (
            "zeroed", "rank_hi", "rank_lo", "rank_mm", "rank_ready", "hi", "lo", "gk_mm", "scanned", "ln",
            "chain", "sums_ready", "exps_ready", "qk_done", "tiles_mm", "turned", "kn_copied", "silu", "g_done",
            "v_hi_done", "v_lo_done", "v_mm", "v_copied",
            "v_free", "gk_hi", "gk_lo", "rank_rounded"))
    q_stored, k_stored, kn_stored = ([sem(f"{n}_stored{s}") for s in range(2)] for n in ("q", "k", "kn"))
    g_stored = p.g_stored
    w_src = a["gla_w_in"][0].rearrange("(k p) c -> p k c", p=P)
    gk_ps = p.ps[:, NB:2 * NB, :].rearrange("p b t -> p (b t)")
    CHAINED = 3 + NB
    K_STORED = 2 * DMA

    def w_cols(h, j):
        return (h * DK, h * DK + KD, h * DV + 2 * KD + VD, h * DV + 2 * KD + VD + P)[j]

    with phase, nc.Block() as block:

        @block.sync
        def _(sp):
            def load(h, j):
                sp.dma_start(raw[j % 2][:], w_src[:, :, ds(w_cols(h, j), P)]).then_inc(loaded[j % 2], DMA)

            def load_gk(h):
                for r in range(RANK_ROWS // GATE_RANK):
                    sp.dma_start(w_gk_raw[r * GATE_RANK:(r + 1) * GATE_RANK, :],
                                 a["gla_w_gk"][0][:, ds(h * DK, DK)]).then_inc(gk_loaded, DMA)

            def store(scratch, unit, n, out, sem):
                sp.dma_start(scratch[n * NB:(n + 1) * NB, :, ds(unit * P, P)].rearrange("t p c -> p t c"),
                             out[n % 2][:].rearrange("p (t c) -> p t c", c=P)).then_inc(sem[n % 2], DMA)

            def head(h, last):
                sp.wait_ge(lo, h * 4 + 1)
                load(h, 2)
                for n in range(NB):
                    sp.wait_ge(qk_done, h * 8 + n + 1)
                    store(p.q_tiles, h, n, q_out, q_stored)
                sp.wait_ge(lo, h * 4 + 2)
                load(h, 3)
                for n in range(NB):
                    sp.wait_ge(qk_done, h * 8 + NB + n + 1)
                    sp.dma_start(p.k_tiles[n * NB:(n + 1) * NB, :, ds(h * P, P)].rearrange("t p c -> p t c"),
                                 e_k[:, n * BLK:(n + 1) * BLK].rearrange("p (t c) -> p t c", c=P)
                                 ).then_inc(k_stored[n % 2], DMA)
                    store(p.k2_tiles, h, n, k2_out, k_stored)
                if not last:
                    sp.wait_ge(gk_lo, h + 1)
                    load_gk(h + 1)
                    sp.wait_ge(lo, h * 4 + 3)
                    load(h + 1, 0)
                for n in range(NB):
                    sp.wait_ge(g_done, h * 8 + n + 1)
                    store(p.g_tiles, h * 2, n, g_out, g_stored)
                if not last:
                    sp.wait_ge(lo, h * 4 + 4)
                    load(h + 1, 1)
                for n in range(NB):
                    sp.wait_ge(kn_copied, h * NB + n + 1)
                    store(p.kn_tiles, h, n, kn_out, kn_stored)
                if last:
                    for s in range(V_OUT):
                        sp.wait_ge(v_stored[s], HALVES * NT // V_OUT * DMA)
                    for s in range(2):
                        for sem, each in ((q_stored, DMA), (k_stored, K_STORED), (kn_stored, DMA)):
                            sp.wait_ge(sem[s], HEADS * NB // 2 * each)
                    sp.wait_ge(gk_mm, HEADS * NB)
                    sp.wait_ge(qk_done, HEADS * 8)
                    sp.wait_ge(turned, HEADS * NB)
                    for s in range(2):
                        p.load_qkv(sp, s, s)
                for n in range(NB):
                    sp.wait_ge(g_done, h * 8 + NB + n + 1)
                    store(p.g_tiles, h * 2 + 1, n, g_out, g_stored)

            for n in range(p.V_PREFETCHED, HALVES * KT):
                half, k = n // KT, n % KT
                if n >= p.V_RAW:
                    sp.wait_ge(v_lo_done, n - p.V_RAW + 1)
                sp.dma_start(v_raw[n % p.V_RAW][:], w_src[:, k, half * BLK + 2 * KD:(half + 1) * BLK + 2 * KD]
                             ).then_inc(v_loaded[n % p.V_RAW], DMA)
            for s in range(2):
                sp.wait_ge(p.fused_stored[s], GROUPS * KT // 2 * DMA)
            with nc.allow_non_contiguous_dma(reason="16 columns of the gates' first factor"):
                sp.dma_start(rank_raw[:], w_src[:, :, 2 * KD + 2 * VD:2 * KD + 2 * VD + GATE_RANK]
                             ).then_inc(rank_loaded, DMA)
            load_gk(0)
            load(0, 0)
            load(0, 1)
            with sp.Fori(0, HEADS - 1) as h:
                head(h, False)
            head(HEADS - 1, True)

        @block.tensor
        def _(pe):
            with pe.Fori(0, HALVES) as half:
                for t in range(NT):
                    pe.wait_ge(v_copied, half * NT + t)
                    for k in range(KT):
                        if t == 0:
                            pe.wait_ge(v_lo_done, half * KT + k + 1)
                        last = split_product(nc, p.ps[:, t % BANKS, :], p.x_hi[:, k, t * P:(t + 1) * P],
                                             p.x_lo[:, k, t * P:(t + 1) * P], v_hi[:, k, :], v_lo[:, k, :],
                                             k == 0, k == KT - 1)
                        if t == NT - 1 and k < KT - 1:
                            last.then_inc(v_free, 1)
                    last.then_inc(v_mm, 1)
            pe.wait_ge(rank_lo, 3)
            for n in range(NB):
                pe.wait_ge(v_copied, HALVES * NT + n)
                for k in range(KT):
                    nc.tensor.matmul(p.ps[:, n, :], rank_w[:, k, :], p.x_hi[:, k, n * BLK:(n + 1) * BLK],
                                     start=k == 0, stop=False)
                    last = nc.tensor.matmul(p.ps[:, n, :], rank_w[:, k, :], p.x_lo[:, k, n * BLK:(n + 1) * BLK],
                                            start=False, stop=k == KT - 1)
                last.then_inc(rank_mm, 1)

            def tile(w, j, bank_free):
                pe.wait_ge(lo, w + 1)
                for n in range(NB):
                    pe.wait_ge(*bank_free(n))
                    for k in range(KT):
                        last = split_product(nc, p.ps[:, n, :], w_hi[j % 2][:, k, :], w_lo[j % 2][:, k, :],
                                             p.x_hi[:, k, n * BLK:(n + 1) * BLK],
                                             p.x_lo[:, k, n * BLK:(n + 1) * BLK], k == 0, k == KT - 1)
                    last.then_inc(tiles_mm, 1)

            with pe.Fori(0, HEADS) as h:
                pe.wait_ge(gk_lo, h + 1)
                pe.wait_ge(rank_ready, NB)
                pe.wait_ge(kn_copied, h * NB)
                for n in range(NB):
                    nc.tensor.matmul(p.ps[:, NB + n, :], w_gk[:], rank[:, n * BLK:(n + 1) * BLK],
                                     start=True, stop=True).then_inc(gk_mm, 1)
                tile(h * 4, 0, lambda n: (g_done, h * 8))
                tile(h * 4 + 1, 1, lambda n: (qk_done, h * 8 + n + 1))
                tile(h * 4 + 2, 2, lambda n: (qk_done, h * 8 + NB + n + 1))
                for n in range(NB):
                    pe.wait_ge(qk_done, h * 8 + NB + n + 1)
                    for c in range(NB):
                        last = nc.tensor.transpose(p.ps[:, NB + n, c * P:(c + 1) * P],
                                                   sums[:, (n * NB + c) * P:(n * NB + c + 1) * P], p.ident[:])
                    last.then_inc(turned, 1)
                tile(h * 4 + 3, 3, lambda n: (silu, h * 8 + n + 1))

        def first_parts(act):
            act.wait_ge(rank_loaded, DMA)
            act.wait_ge(zeroed, 1)
            nc.scalar.activation(rank_w[:, :, 0:GATE_RANK], rank_raw[:], ACT.Copy).then_inc(rank_hi, 1)
            for r in (1, 2):
                nc.scalar.activation(rank_w[:, :, r * PAIR_ROWS:r * PAIR_ROWS + GATE_RANK], rank_raw[:], ACT.Copy
                                     ).then_inc(rank_hi, 1)
            gk_part(act, 0)
            act.wait_ge(loaded[0], DMA)
            nc.scalar.activation(w_hi[0][:], raw[0][:], ACT.Copy).then_inc(hi, 1)

        def gk_part(act, h):
            act.wait_ge(gk_loaded, (h + 1) * (RANK_ROWS // GATE_RANK) * DMA)
            act.wait_ge(gk_mm, h * NB)
            nc.scalar.activation(w_gk[:], w_gk_raw[:], ACT.Copy).then_inc(gk_hi, 1)

        @block.scalar
        def _(act):
            def v_parts(half):
                for k in range(KT):
                    n = half * KT + k
                    act.wait_ge(v_loaded[n % p.V_RAW], (n // p.V_RAW + 1) * DMA)
                    if half:
                        act.wait_ge(*((v_free, k + 1) if k < KT - 1 else (v_mm, NT)))
                    nc.scalar.activation(v_hi[:, k, :], v_raw[n % p.V_RAW][:], ACT.Copy).then_inc(v_hi_done, 1)

            act.sem_inc(v_copied, BANKS - 1)
            v_parts(0)
            for half in range(HALVES):
                for t in range(NT):
                    if half == 1 and t == NT // 2:
                        first_parts(act)
                    if half == 0 and t == NT - 1:
                        v_parts(1)
                    n = half * NT + t
                    act.wait_ge(v_mm, n + 1)
                    if n >= V_OUT:
                        act.wait_ge(v_stored[t % V_OUT], n // V_OUT * DMA)
                    nc.scalar.activation(v_out[t % V_OUT][:], p.ps[:, t % BANKS, :], ACT.Copy).then_inc(v_copied, 1)
                    act.wait_ge(v_copied, n + BANKS)
                    act.dma_start(p.v_tiles[t, :, half * BLK:(half + 1) * BLK], v_out[t % V_OUT][:]
                                  ).then_inc(v_stored[t % V_OUT], DMA)
            for s in range(V_OUT):
                act.wait_ge(v_stored[s], HALVES * NT // V_OUT * DMA)
            for n in range(NB):
                act.wait_ge(rank_mm, n + 1)
                nc.scalar.activation(rank[:, n * BLK:(n + 1) * BLK], p.ps[0:RANK_ROWS, n, :],
                                     ACT.Copy).then_inc(rank_rounded, 1)

            def part(h, j, w):
                act.wait_ge(loaded[j % 2], (h * 2 + j // 2 + 1) * DMA)
                if isinstance(w, int) and w < 2:
                    pass
                else:
                    act.wait_ge(tiles_mm, (w - 1) * NB)
                nc.scalar.activation(w_hi[j % 2][:], raw[j % 2][:], ACT.Copy).then_inc(hi, 1)

            def head(h, last):
                nc.scalar.preload_act_table_set("natural_log_exp_and_others")
                act.wait_ge(gk_mm, h * NB + NB)
                act.wait_ge(qk_done, h * 8)
                nc.scalar.activation(e_q[:], gk_ps, ACT.Abs, bias=p.b_gk[:, ds(h, 1)]).then_inc(ln_done, 1)
                act.wait_ge(ln_done, h * 3 + 1)
                nc.scalar.activation(e_q[:], e_q[:], ACT.Exp, scale=-1.0).then_inc(ln_done, 1)
                act.wait_ge(ln_done, h * 3 + 2)
                nc.scalar.activation(e_q[:], e_q[:], ACT.Ln, bias=1.0).then_inc(ln_done, 1)
                act.wait_ge(loaded[1], (h * 2 + 1) * DMA)
                act.wait_ge(tiles_mm, h * 4 * NB)
                nc.scalar.activation(w_hi[1][:], raw[1][:], ACT.Copy).then_inc(hi, 1)
                act.wait_ge(sums_ready, h + 1)
                nc.scalar.activation(e_q[:], sums[:], ACT.Exp, scale=1.0 / GATE_NORMALIZER)
                nc.scalar.activation(e_k[:], sums[:], ACT.Exp, scale=-1.0 / GATE_NORMALIZER)
                nc.scalar.activation(p.decay[:, ds(h, 1), :].rearrange("p o c -> p (o c)"), chunk_end[:], ACT.Exp,
                                     scale=1.0 / GATE_NORMALIZER).then_inc(exps_ready, 1)
                act.wait_ge(chain, h * CHAINED + 3)
                nc.scalar.activation(sums[:], sums[:], ACT.Exp, scale=1.0 / GATE_NORMALIZER).then_inc(exps_ready, 1)
                part(h, 2, h * 4 + 2)
                part(h, 3, h * 4 + 3)

                def gate(j, n):
                    act.wait_ge(tiles_mm, (h * 4 + j) * NB + n + 1)
                    act.wait_ge(g_stored[n % 2], (h * 4 + (j - 2) * 2 + n // 2) * DMA)
                    nc.scalar.activation(g_out[n % 2][:], p.ps[:, n, :], ACT.Silu).then_inc(silu, 1)

                for n in range(NB):
                    gate(2, n)
                if not last:
                    part(h + 1, 0, h * 4 + 4)
                    gk_part(act, h + 1)
                for n in range(NB):
                    act.wait_ge(turned, h * NB + n + 1)
                    act.wait_ge(kn_stored[n % 2], (h * 2 + n // 2) * DMA)
                    nc.scalar.activation(kn_out[n % 2][:], p.ps[:, NB + n, :], ACT.Copy).then_inc(kn_copied, 1)
                for n in range(NB):
                    gate(3, n)

            with act.Fori(0, HEADS - 1) as h:
                head(h, False)
            head(HEADS - 1, True)

        @block.vector
        def _(dve):
            for n in range(HALVES * KT):
                if n == KT:
                    for s in range(2):
                        dve.wait_ge(p.fused_stored[s], GROUPS * KT // 2 * DMA)
                    nc.vector.memset(rank_w[:].bitcast(F32), 0.0).then_inc(zeroed, 1)
                dve.wait_ge(v_hi_done, n + 1)
                nc.vector.tensor_tensor(v_lo[:, n % KT, :], v_raw[n % p.V_RAW][:], v_hi[:, n % KT, :].bitcast(F32),
                                        ALU.subtract).then_inc(v_lo_done, 1)
            for r in range(3):
                dve.wait_ge(rank_hi, r + 1)
                first = r * PAIR_ROWS
                nc.vector.tensor_tensor(rank_w[:, :, first + GATE_RANK:first + PAIR_ROWS], rank_raw[:],
                                        rank_w[:, :, first:first + GATE_RANK].bitcast(F32), ALU.subtract
                                        ).then_inc(rank_lo, 1)

            def gk_part(h):
                dve.wait_ge(gk_hi, h + 1)
                rows = slice(PAIR_ROWS, 2 * PAIR_ROWS)
                nc.vector.tensor_tensor(w_gk[rows, :], w_gk_raw[rows, :], w_gk[rows, :].bitcast(F32), ALU.subtract
                                        ).then_inc(gk_lo, 1)

            def part(w, s):
                dve.wait_ge(hi, w + 1)
                nc.vector.tensor_tensor(w_lo[s][:], raw[s][:], w_hi[s][:].bitcast(F32), ALU.subtract).then_inc(lo, 1)

            def chunks(block):
                return block.rearrange("p (o t two c) -> p o t two c", o=1, two=2, c=CHUNK)

            def head(h, last):
                dve.wait_ge(ln_done, h * 3 + 1)
                dve.wait_ge(qk_done, h * 8)
                dve.wait_ge(turned, h * NB)
                for s in range(2):
                    dve.wait_ge(k_stored[s], h * (NB // 2 * K_STORED))
                nc.vector.tensor_scalar(e_k[:], gk_ps, p.b_gk[:, ds(h, 1)], 0.0, ALU.add, ALU.min).then_inc(chain, 1)
                dve.wait_ge(ln_done, h * 3 + 3)
                dve.wait_ge(chain, h * CHAINED + 1)
                nc.vector.tensor_tensor(e_k[:], e_k[:], e_q[:], ALU.subtract).then_inc(chain, 1)
                part(h * 4 + 1, 1)
                dve.wait_ge(chain, h * CHAINED + 2)
                for n in range(NB):
                    cols = slice(n * BLK, (n + 1) * BLK)
                    scan = nc.vector.tensor_tensor_scan(sums[:, cols], p.keep[:], e_k[:, cols], 0.0, ALU.mult, ALU.add)
                scan.then_inc(scanned, 1)
                dve.wait_ge(scanned, h + 1)
                by_chunk = sums[:].rearrange("p (c s) -> p c s", s=CHUNK)
                nc.vector.tensor_copy(chunk_end[:], by_chunk[:, :, CHUNK - 1]).then_inc(sums_ready, 1)
                dve.wait_ge(sums_ready, h + 1)
                dve.wait_ge(exps_ready, h * 2 + 1)
                nc.vector.tensor_tensor(by_chunk, chunk_end[:].unsqueeze(2).to_broadcast([P, SEQ // CHUNK, CHUNK]),
                                        by_chunk, ALU.subtract).then_inc(chain, 1)
                for n in range(NB):
                    dve.wait_ge(tiles_mm, h * 4 * NB + n + 1)
                    dve.wait_ge(q_stored[n % 2], (h * 2 + n // 2) * DMA)
                    nc.vector.scalar_tensor_tensor(out=q_out[n % 2][:], in0=p.ps[:, n, :], scalar=float(DK) ** -0.5,
                                                   in1=e_q[:, n * BLK:(n + 1) * BLK], op0=ALU.mult, op1=ALU.mult
                                                   ).then_inc(qk_done, 1)
                part(h * 4 + 2, 0)
                dve.wait_ge(exps_ready, h * 2 + 2)
                for n in range(NB):
                    cols = slice(n * BLK, (n + 1) * BLK)
                    dve.wait_ge(tiles_mm, (h * 4 + 1) * NB + n + 1)
                    dve.wait_ge(k_stored[n % 2], (h * 2 + n // 2) * K_STORED)
                    keys, ends, own, k2 = (chunks(ap) for ap in (p.ps[:, n, :], sums[:, cols], e_k[:, cols],
                                                                 k2_out[n % 2][:]))
                    nc.vector.tensor_tensor(e_k[:, cols], p.ps[:, n, :], e_k[:, cols], ALU.mult)
                    nc.vector.tensor_tensor(ends[:, :, :, 1, :], keys[:, :, :, 1, :], ends[:, :, :, 1, :], ALU.mult)
                    nc.vector.tensor_tensor(k2[:, :, :, 0, :], keys[:, :, :, 0, :], ends[:, :, :, 0, :], ALU.mult
                                            ).then_inc(chain, 1)
                    dve.wait_ge(chain, h * CHAINED + 3 + n + 1)
                    nc.vector.tensor_copy(k2[:, :, :, 1, :], own[:, :, :, 1, :])
                    second = p.decay[:].rearrange("p h (t two) -> p h t two", two=2)[:, ds(h, 1), n * NB:(n + 1) * NB, 1:2]
                    nc.vector.tensor_tensor(ends[:, :, :, 0, :], k2[:, :, :, 0, :],
                                            second.to_broadcast([P, 1, NB, CHUNK]), ALU.mult).then_inc(qk_done, 1)
                part(h * 4 + 3, 1)

                def gate(j, n):
                    dve.wait_ge(silu, h * 8 + (j - 2) * NB + n + 1)
                    nc.vector.tensor_scalar(g_out[n % 2][:], g_out[n % 2][:], p.norm_w[:, j - 2:j - 1], None,
                                            ALU.mult).then_inc(g_done, 1)

                for n in range(NB):
                    gate(2, n)
                if not last:
                    part(h * 4 + 4, 0)
                    gk_part(h + 1)
                for n in range(NB):
                    gate(3, n)

            gk_part(0)
            dve.wait_ge(hi, 1)
            nc.vector.tensor_tensor(w_lo[0][:], raw[0][:], w_hi[0][:].bitcast(F32), ALU.subtract).then_inc(lo, 1)
            for n in range(NB):
                dve.wait_ge(rank_rounded, n + 1)
                rows, cols = slice(2 * PAIR_ROWS, RANK_ROWS), slice(n * BLK, (n + 1) * BLK)
                nc.vector.tensor_tensor(rank[rows, cols], p.ps[rows, n, :], rank[rows, cols].bitcast(F32),
                                        ALU.subtract).then_inc(rank_ready, 1)
            for s in range(V_OUT):
                dve.wait_ge(v_stored[s], HALVES * NT // V_OUT * DMA)
            with dve.Fori(0, HEADS - 1) as h:
                head(h, False)
            head(HEADS - 1, True)


def attend_and_norm(nc, p, a):
    p.at = p.ln_at
    ln_g = p.place("a_ln_g", [P, D])
    ln_b = p.place("a_ln_b", [P, D])
    w_hi = p.place("a_w_hi", [P, KT, D], F32R)
    w_lo = p.place("a_w_lo", [P, KT, D], F32R)
    q, k, k2, kn, v, in_loaded = p.q, p.k, p.k2, p.kn, p.v, p.qkv_loaded
    scores = [p.place(f"a_scores{s}", [P, KD]) for s in range(2)]
    g, x = ([p.place(f"a_{n}{s}", [P, D]) for s in range(2)] for n in ("g", "x"))
    kn_hi, kn_lo = ([p.place(f"a_kn_{n}{s}", [P, KD], F32R) for s in range(2)] for n in ("hi", "lo"))
    square_at = p.at
    square = p.place("a_square", [P, VD])
    square_sum = p.place("a_square_sum", [P, KD])
    sum_at = p.at
    p.at = square_at
    sum_hi, sum_lo = p.place("a_sum_hi", [P, KD], F32R), p.place("a_sum_lo", [P, KD], F32R)
    p.at = sum_at
    rms = p.place("a_rms", [P, HEADS, P])
    gated = p.place("a_gated", [P, VD])
    o_hi = [p.place(f"a_o_hi{s}", [P, KT, P], F32R) for s in range(2)]
    o_lo = [p.place(f"a_o_lo{s}", [P, KT, P], F32R) for s in range(2)]
    state = [p.place(f"a_state{s}", [P, VD]) for s in range(2)]
    assert p.at == p.qkv_at
    p.at = p.qkv_end
    res = p.place("a_res", [P, D])
    stats = p.place("a_stats", [P, 2, 6])
    moments = p.place("a_moments", [P, 2])
    rstd = p.place("a_rstd", [P, 1])
    shift = p.place("a_shift", [P, 1])
    tile_decay = p.place("a_tile_decay", [P, HEADS, NT])
    out = [p.place(f"a_out{s}", [P, D]) for s in range(2)]
    assert p.at <= p.mix_raw_at
    p.at, RAW = p.mix_raw_at, 4
    v_hi0, v_lo0, v_hi1, v_lo1 = (p.place(f"a_v_{n}", [P, VD], F32R) for n in ("hi0", "lo0", "hi1", "lo1"))
    v_hi, v_lo = [v_hi0, v_hi1], [v_lo0, v_lo1]
    raw = [p.place(f"a_raw{s}", [P, D]) for s in range(2)] + out

    phase = ExitStack()
    sem = lambda name: phase.enter_context(nc.semaphore("a_" + name))
    ln_loaded, summed_squares = sem("ln_loaded"), sem("summed_squares")
    raw_loaded = [sem(f"raw_loaded{s}") for s in range(RAW)]
    g_loaded, x_loaded = ([sem(f"{n}{s}") for s in range(2)] for n in ("g_loaded", "x_loaded"))
    out_stored = p.x1_stored
    (w_hi_done, w_lo_done, zeroed, scored, masked, kv_mm, states, o_mm, squared, summed, rms_mid, rms_done, o_read,
     gated_done, o_hi_done, o_lo_done, y_mm, y_read, stats_done, moments_done, rstd_done, shifted, normed,
     out_done, kv_hi_done, kv_lo_done, sum_hi_done, sum_lo_done) = (
        sem(n) for n in (
            "w_hi_done", "w_lo_done", "zeroed", "scored", "masked", "kv_mm", "states", "o_mm", "squared", "summed",
            "rms_mid", "rms_done", "o_read", "gated_done", "o_hi_done", "o_lo_done", "y_mm", "y_read", "stats_done",
            "moments_done", "rstd_done", "shifted", "normed", "out_done", "kv_hi_done",
            "kv_lo_done", "sum_hi_done", "sum_lo_done"))

    w_src = a["gla_w_out"][0].rearrange("(k p) c -> p k c", p=P)
    score_ps = p.ps[:, 0, :]
    o_ps = p.ps[:, 1:3, :].rearrange("p b c -> p (b c)")
    kv_ps = p.ps[:, 3:5, :].rearrange("p b c -> p (b c)")
    sum_ps = p.ps[:, 5, :]
    y_ps = [p.ps[:, 6 + half, :] for half in range(2)]
    LAG, TAIL = 2, 3

    def run(engine, step):
        for t in range(TAIL + 1):
            step(t, t % 2, min(t, TAIL), t // 2)
        with engine.Fori((TAIL + 1) // 2, NT // 2 - 1) as pair:
            for s in range(2):
                step(pair * 2 + s, s, TAIL, pair)
        for t in range(NT - 2, NT + TAIL):
            step(t, t % 2, TAIL, t // 2)

    def has(t, lag, behind):
        return lag >= behind and not (isinstance(t, int) and t - behind >= NT)

    def has_next(t):
        return not (isinstance(t, int) and t + 1 >= NT)

    with phase, nc.Block() as block:

        @block.sync
        def _(sp):
            def load_g(t, s):
                sp.dma_start(g[s][:], p.g_tiles[ds(t, 1), :, :].rearrange("o p c -> (o p) c")).then_inc(g_loaded[s], DMA)

            def load_x(t, s):
                sp.dma_start(x[s][:], a["x"][0][ds(t * P, P), :]).then_inc(x_loaded[s], DMA)

            def load_w(kt):
                if kt >= RAW:
                    sp.wait_ge(w_lo_done, kt - RAW + 1)
                sp.dma_start(raw[kt % RAW][:], w_src[:, kt, :]).then_inc(raw_loaded[kt % RAW], DMA)

            for s in range(2):
                sp.wait_ge(p.g_stored[s], HEADS * NB * DMA)
            for kt in range(RAW):
                load_w(kt)
            load_g(0, 0)
            load_g(1, 1)
            for kt in range(RAW, RAW + 2):
                load_w(kt)
            load_x(0, 0)
            load_x(1, 1)
            for ln, src in ((ln_g, a["ln_g"]), (ln_b, a["ln_b"])):
                sp.dma_start(ln[:], src[0:1, :].to_broadcast([P, D])).then_inc(ln_loaded, DMA)
            def step(t, s, lag):
                static = isinstance(t, int)
                if lag >= 1 and not (static and t + 1 >= NT):
                    sp.wait_ge(gated_done, t)
                    load_g(t + 1, 1 - s)
                if has(t, lag, TAIL):
                    sp.wait_ge(out_done, (t - TAIL) * 2 + 2)
                    sp.dma_start(p.x1[ds((t - TAIL) * P, P), :], out[1 - s][:]).then_inc(out_stored[1 - s], DMA)
                if lag >= LAG and not (static and t >= NT):
                    sp.wait_ge(y_read, (t - LAG) * 2 + 2)
                    load_x(t, s)
                if not (static and t + 2 >= NT):
                    sp.wait_ge(o_mm, t + 1)
                    p.load_qkv(sp, t + 2, s)
                if static and t == 0:
                    for kt in range(RAW + 2, KT):
                        load_w(kt)

            for t in range(TAIL + 1):
                step(t, t % 2, min(t, TAIL))
            with sp.Fori((TAIL + 1) // 2, NT // 2 - 1) as pair:
                for s in range(2):
                    step(pair * 2 + s, s, TAIL)
            for t in range(NT - 2, NT + TAIL):
                step(t, t % 2, TAIL)
                if t == NT:
                    sp.wait_ge(w_lo_done, KT)
                    sp.wait_ge(o_mm, NT)
                    for i in range(2):
                        sp.wait_ge(out_stored[i], p.ROWS_PREFETCHED // 2 * DMA)
                    p.prefetch_mix(sp)

        @block.tensor
        def _(pe):
            def mean(t):
                pe.wait_ge(sum_lo_done, t)
                pe.wait_ge(rms_mid, t - 1)
                nc.tensor.matmul(sum_ps, p.mean_w[:], sum_hi[:], start=True, stop=False)
                nc.tensor.matmul(sum_ps, p.mean_w[:], sum_lo[:], start=False, stop=True).then_inc(summed, 1)

            def y_half(t, s, half, lag):
                u = t - LAG
                if half == 0:
                    pe.wait_ge(o_lo_done, u + 1)
                    pe.wait_ge(w_lo_done, KT)
                    pe.wait_ge(y_read, u * 2)
                for kt in range(KT):
                    if half == 0 and kt == KT // 4 and has(t, lag, 1):
                        mean(t)
                    last = split_product(nc, y_ps[half], o_hi[s][:, kt, :], o_lo[s][:, kt, :],
                                         w_hi[:, kt, half * BLK:(half + 1) * BLK],
                                         w_lo[:, kt, half * BLK:(half + 1) * BLK], kt == 0, kt == KT - 1)
                last.then_inc(y_mm, 1)

            def scores_of(s):
                for h in range(HEADS):
                    head = slice(h * P, (h + 1) * P)
                    nc.tensor.matmul(score_ps[:, h * P:h * P + CHUNK], k[s][:, head], q[s][:, h, 0:CHUNK],
                                     start=True, stop=True)
                    last = nc.tensor.matmul(score_ps[:, h * P + CHUNK:(h + 1) * P], k2[s][:, head],
                                            q[s][:, h, CHUNK:P], start=True, stop=True)
                last.then_inc(scored, 1)

            def kv(s):
                for h in range(HEADS):
                    keys, values = slice(h * DK, (h + 1) * DK), slice(h * DV, (h + 1) * DV)
                    last = split_product(nc, kv_ps[:, values], kn_hi[s][:, keys], kn_lo[s][:, keys],
                                         v_hi[s][:, values], v_lo[s][:, values], True, True)
                last.then_inc(kv_mm, 1)

            def outputs(s):
                for b in range(2):
                    for j in range(4 * b, 4 * b + 4):
                        h = j // 2
                        nc.tensor.matmul(o_ps[:, j * P:(j + 1) * P], v[s][:, j * P:(j + 1) * P],
                                         scores[s][:, h * P:(h + 1) * P], start=j == 4 * b, stop=False,
                                         skip_group_check=True)
                    for j in range(4 * b, 4 * b + 4):
                        queries = q[s][:, j // 2, :].rearrange("p (a c) -> p a c", c=CHUNK)[:, 0::2, :]
                        last = nc.tensor.matmul(o_ps[:, j * P:(j + 1) * P].rearrange("p (a c) -> p a c", c=CHUNK),
                                                state[s][:, j * P:(j + 1) * P], queries, start=False, stop=True,
                                                skip_group_check=True)
                last.then_inc(o_mm, 1)

            def step(t, s, lag, pair):
                attends = has(t, lag, 0)
                if attends:
                    pe.wait_ge(in_loaded[s], (pair + 1) * (p.QKV_LOADS * DMA))
                    pe.wait_ge(masked, t)
                    scores_of(s)
                    pe.wait_ge(states, t)
                    pe.wait_ge(kv_lo_done, t + 1)
                    if has_next(t):
                        kv(s)
                if has(t, lag, LAG):
                    y_half(t, s, 0, lag)
                elif has(t, lag, 1):
                    mean(t)
                if attends:
                    pe.wait_ge(masked, t + 1)
                    pe.wait_ge(zeroed, 1)
                    pe.wait_ge(o_read, t)
                    outputs(s)
                if has(t, lag, LAG):
                    y_half(t, s, 1, lag)

            run(pe, step)
            pe.wait_ge(o_read, NT)
            pe.wait_ge(states, NT - 1)
            for t in range(p.TURNED_AHEAD):
                p.turn_x1(pe, t)

        @block.scalar
        def _(act):
            def kv_parts(t, s, pair, lag):
                act.wait_ge(in_loaded[s], (pair + 1) * (p.QKV_LOADS * DMA))
                if lag >= 2:
                    act.wait_ge(kv_mm, t - 1)
                nc.scalar.activation(kn_hi[s][:], kn[s][:], ACT.Copy).then_inc(kv_hi_done, 1)
                nc.scalar.activation(v_hi[s][:], v[s][:], ACT.Copy).then_inc(kv_hi_done, 1)

            def w_parts(t, first, end):
                if isinstance(t, int) and t < LAG:
                    for kt in range(t * KT // LAG + first, t * KT // LAG + end):
                        act.wait_ge(raw_loaded[kt % RAW], (kt // RAW + 1) * DMA)
                        nc.scalar.activation(w_hi[:, kt, :], raw[kt % RAW][:], ACT.Copy).then_inc(w_hi_done, 1)

            def norm_scale(t, s, pair):
                u = t - TAIL
                act.wait_ge(shifted, u + 1)
                act.wait_ge(out_stored[1 - s], (pair + s - 2) * DMA)
                nc.scalar.activation(out[1 - s][:], res[:], ACT.Identity, scale=rstd[:, 0:1], bias=shift[:, 0:1]
                                     ).then_inc(normed, 1)

            kv_parts(0, 0, 0, 0)
            nc.scalar.preload_act_table_set("natural_log_exp_and_others")

            def step(t, s, lag, pair):
                if has(t, lag, 1):
                    act.wait_ge(summed_squares, t)
                    nc.scalar.activation(sum_hi[:], square_sum[:], ACT.Copy).then_inc(sum_hi_done, 1)
                if has(t, lag, TAIL):
                    norm_scale(t, s, pair)
                if has(t, lag, 1):
                    u = t - 1
                    act.wait_ge(summed, t)
                    act.wait_ge(o_read, u)
                    nc.scalar.activation(rms[:].rearrange("p h c -> p (h c)"), sum_ps, ACT.Ln,
                                         bias=p.eps_rms[:]).then_inc(rms_mid, 1)
                    act.wait_ge(rms_mid, t)
                    nc.scalar.activation(rms[:], rms[:], ACT.Exp, scale=-0.5).then_inc(rms_done, 1)
                    act.wait_ge(gated_done, t)
                    if lag >= TAIL:
                        act.wait_ge(y_mm, t * 2 - 4)
                    nc.scalar.activation(o_hi[1 - s][:].rearrange("p k c -> p (k c)"), gated[:], ACT.Copy
                                         ).then_inc(o_hi_done, 1)
                w_parts(t, 0, 2)
                if has_next(t):
                    kv_parts(t + 1, 1 - s, pair + s, lag + 1)
                if has(t, lag, 0):
                    act.wait_ge(o_mm, t + 1)
                    nc.scalar.activation(square[:], o_ps, ACT.Square).then_inc(squared, 1)
                w_parts(t, 2, 4)
                if isinstance(t, int) and t == NT + 1:
                    for i in range(2):
                        p.mix_hi_part(act, i, 0)
                if has(t, lag, LAG):
                    u = t - LAG
                    act.wait_ge(moments_done, u + 1)
                    act.wait_ge(normed, u)
                    nc.scalar.activation(rstd[:], moments[:, 1:2], ACT.Ln, bias=p.eps_ln[:]).then_inc(rstd_done, 1)
                    act.wait_ge(rstd_done, u * 2 + 1)
                    nc.scalar.activation(rstd[:], rstd[:], ACT.Exp, scale=-0.5).then_inc(rstd_done, 1)

            run(act, step)

        @block.vector
        def _(dve):
            def advance(t, s):
                dve.wait_ge(kv_mm, t + 1)
                dve.wait_ge(states, t)
                dve.wait_ge(o_mm, t)
                for h in range(HEADS):
                    cols = slice(h * DV, (h + 1) * DV)
                    last = nc.vector.scalar_tensor_tensor(
                        out=state[1 - s][:, cols], in0=state[s][:, cols], scalar=tile_decay[:, h, ds(t, 1)],
                        in1=kv_ps[:, cols], op0=ALU.mult, op1=ALU.add)
                last.then_inc(states, 1)

            def gate(t, s, pair):
                by_head = lambda ap: ap.rearrange("p (h j c) -> p h j c", j=2, c=P)
                dve.wait_ge(rms_done, t)
                dve.wait_ge(o_lo_done, t - 1)
                nc.vector.tensor_tensor(by_head(gated[:]), by_head(o_ps),
                                        rms[:].unsqueeze(2).to_broadcast([P, HEADS, 2, P]), ALU.mult
                                        ).then_inc(o_read, 1)
                dve.wait_ge(o_read, t)
                dve.wait_ge(g_loaded[1 - s], (pair + s) * DMA)
                nc.vector.tensor_tensor(gated[:], gated[:], g[1 - s][:], ALU.mult).then_inc(gated_done, 1)

            def norm_end(t, s, pair):
                u = t - TAIL
                dve.wait_ge(normed, u + 1)
                nc.vector.tensor_tensor(out[1 - s][:], out[1 - s][:], ln_g[:], ALU.mult).then_inc(out_done, 1)
                dve.wait_ge(out_done, u * 2 + 1)
                nc.vector.tensor_tensor(out[1 - s][:], out[1 - s][:], ln_b[:], ALU.add).then_inc(out_done, 1)

            def residual(t, s, pair):
                u = t - LAG
                dve.wait_ge(ln_loaded, 2 * DMA)
                dve.wait_ge(x_loaded[s], pair * DMA)
                dve.wait_ge(normed, u)
                for half in range(2):
                    cols = slice(half * BLK, (half + 1) * BLK)
                    dve.wait_ge(y_mm, u * 2 + half + 1)
                    nc.vector.scalar_tensor_tensor(out=res[:, cols], in0=x[s][:, cols], scalar=ALPHA,
                                                   in1=y_ps[half], op0=ALU.mult, op1=ALU.add).then_inc(y_read, 1)
                    dve.wait_ge(y_read, u * 2 + half + 1)
                    nc.vector.bn_stats(stats[:, half, :], res[:, cols]).then_inc(stats_done, 1)
                dve.wait_ge(stats_done, u * 2 + 2)
                nc.vector.memset(p.stats_carrier[:], 0.0)
                nc.vector.bn_aggr(moments[:], stats[:].rearrange("p a b -> p (a b)")).then_inc(moments_done, 1)

            def kv_parts(t, s):
                for i, (raw_rows, hi, lo) in enumerate(((kn, kn_hi, kn_lo), (v, v_hi, v_lo))):
                    dve.wait_ge(kv_hi_done, t * 2 + i + 1)
                    if i == 0:
                        nc.vector.tensor_tensor(q[s][:, :, P:P + CHUNK], q[s][:, :, CHUNK:P],
                                                p.decay[:, :, ds(t * 2, 1)].to_broadcast([P, HEADS, CHUNK]), ALU.mult)
                    last = nc.vector.tensor_tensor(lo[s][:], raw_rows[s][:], hi[s][:].bitcast(F32), ALU.subtract)
                last.then_inc(kv_lo_done, 1)

            def w_parts(t, first, end):
                if isinstance(t, int) and t < LAG:
                    for kt in range(t * KT // LAG + first, t * KT // LAG + end):
                        dve.wait_ge(w_hi_done, kt + 1)
                        nc.vector.tensor_tensor(w_lo[:, kt, :], raw[kt % RAW][:], w_hi[:, kt, :].bitcast(F32),
                                                ALU.subtract).then_inc(w_lo_done, 1)

            def norm_shift(t):
                u = t - TAIL
                dve.wait_ge(rstd_done, u * 2 + 2)
                dve.wait_ge(moments_done, u + 1)
                nc.vector.scalar_tensor_tensor(out=shift[:], in0=moments[:, 0:1], scalar=-1.0, in1=rstd[:, 0:1],
                                               op0=ALU.mult, op1=ALU.mult).then_inc(shifted, 1)

            nc.vector.memset(scores[0][:], 0.0)
            kv_parts(0, 0)
            nc.vector.memset(scores[1][:], 0.0)
            by_tile = p.decay[:].rearrange("p h (t two) -> p h t two", two=2)
            nc.vector.tensor_tensor(tile_decay[:], by_tile[:, :, :, 0], by_tile[:, :, :, 1], ALU.mult)
            nc.vector.memset(state[0][:], 0.0).then_inc(zeroed, 1)
            dve.wait_ge(zeroed, 1)

            def step(t, s, lag, pair):
                if has(t, lag, 1):
                    dve.wait_ge(squared, t)
                    two = square[:].rearrange("p (h j c) -> p h j c", j=2, c=P)
                    nc.vector.tensor_tensor(square_sum[:].rearrange("p (h c) -> p h c", c=P), two[:, :, 0, :],
                                            two[:, :, 1, :], ALU.add).then_inc(summed_squares, 1)
                    dve.wait_ge(sum_hi_done, t)
                    nc.vector.tensor_tensor(sum_lo[:], square_sum[:], sum_hi[:].bitcast(F32), ALU.subtract
                                            ).then_inc(sum_lo_done, 1)
                if has(t, lag, 0):
                    dve.wait_ge(scored, t + 1)
                    nc.vector.memset(p.score_carrier[:], 0.0)
                    nc.vector.copy_predicated(scores[s][:], p.mask[:].rearrange("p h c -> p (h c)").bitcast(I32),
                                              score_ps).then_inc(masked, 1)
                if has(t, lag, TAIL):
                    norm_shift(t)
                if has(t, lag, 0) and has_next(t):
                    advance(t, s)
                if has(t, lag, 1):
                    gate(t, s, pair)
                w_parts(t, 0, 2)
                if has(t, lag, TAIL):
                    norm_end(t, s, pair)
                if has(t, lag, 1):
                    dve.wait_ge(o_hi_done, t)
                    dve.wait_ge(gated_done, t)
                    nc.vector.tensor_tensor(o_lo[1 - s][:].rearrange("p k c -> p (k c)"), gated[:],
                                            o_hi[1 - s][:].rearrange("p k c -> p (k c)").bitcast(F32), ALU.subtract
                                            ).then_inc(o_lo_done, 1)
                if has_next(t):
                    kv_parts(t + 1, 1 - s)
                w_parts(t, 2, 4)
                if isinstance(t, int) and t == NT + 1:
                    for i in range(2):
                        p.mix_lo_part(dve, i, 0)
                if has(t, lag, LAG):
                    residual(t, s, pair)

            run(dve, step)


def pool_mix(nc, p, a):
    p.at = p.mix_end
    w_hi, w_lo, lo = p.mix_hi, p.mix_lo, p.mix_lo_done
    h_in, win_a, win_b = (p.place(f"m_{n}", [P, PAD + SEQ]) for n in ("h", "win_a", "win_b"))
    z = p.place("m_z", [P, SEQ])
    assert p.at <= p.mix_raw_at
    rows, rows_loaded, ROWS = p.rows, p.rows_loaded, p.ROWS
    phase = ExitStack()
    sem = lambda name: phase.enter_context(nc.semaphore("m_" + name))
    stored = p.mixed_stored
    x_turned = p.x1_turned
    h_mm, z_mm, h_copied, silu, chain, pooled, mixed, x_hi, x_lo = (
        sem(n) for n in ("h_mm", "z_mm", "h_copied", "silu", "chain", "pooled", "mixed",
                         "x_hi", "x_lo"))
    FIRST = [("x", 0), ("x", 1), ("x", 2), ("h", 0, 0), ("x", 3), ("z", 0, 0), ("x", 4), ("x", 5), ("h", 0, 1),
             ("x", 6), ("x", 7), ("z", 0, 1), ("h", 1), ("x", 8), ("x", 9), ("z", 1), ("x", 10), ("x", 11), ("x", 12),
             ("x", 13), ("h", 2), ("x", 14), ("x", 15), ("z", 2), ("h", 3), ("z", 3)]
    REUSED_FROM, x_banks = p.REUSED_FROM, p.x_banks

    def x_part(x, t):
        return x[:, :, t * P:(t + 1) * P]

    with phase, nc.Block() as block:

        @block.sync
        def _(sp):
            for t in range(p.ROWS_PREFETCHED, NT):
                if t >= ROWS:
                    sp.wait_ge(x_turned, t - ROWS + 1)
                if t >= NT - 3:
                    sp.wait_ge(p.x1_stored[t % 2], (t // 2 + 1) * DMA)
                sp.dma_start(rows[t % ROWS][:], p.x1[t * P:(t + 1) * P, :]).then_inc(rows_loaded[t % ROWS], DMA)
            with sp.Fori(1, MT) as m:
                sp.wait_ge(lo, m * 2)
                p.load_mix(sp, m)
                sp.wait_ge(mixed, m)
                sp.dma_start(p.mixed[ds(m - 1, 1), :, :].rearrange("o p c -> (o p) c"), z[:]).then_inc(stored, DMA)
            sp.wait_ge(x_turned, NT)
            sp.wait_ge(lo, MT * 2)
            sp.wait_ge(stored, (MT - 1) * DMA)
            p.prefetch_out(sp)
            for n in range(NB):
                sp.wait_ge(mixed, MT + n)
                cols = slice(n * BLK, (n + 1) * BLK)
                sp.dma_start(p.mixed[MT - 1, :, cols], z[:, cols]).then_inc(stored, DMA)

        @block.tensor
        def _(pe):
            def product(s, n, half=None):
                first, size = (0, BLK) if half is None else (half * BLK // 2, BLK // 2)
                tokens = slice(n * BLK + first, n * BLK + first + size)
                for k in range(KT):
                    last = split_product(nc, p.ps[:, s * NB + n, first:first + size], w_hi[s][:, k, :], w_lo[s][:, k, :],
                                         p.x_hi[:, k, tokens], p.x_lo[:, k, tokens], k == 0, k == KT - 1)
                if half != 0:
                    last.then_inc((h_mm, z_mm)[s], 1)

            for what, n, *half in FIRST:
                if what == "x" and n >= p.TURNED_AHEAD:
                    if n in (REUSED_FROM, REUSED_FROM + 1):
                        pe.wait_ge((h_copied, silu)[n % 2], 2)
                    elif n >= 2:
                        pe.wait_ge(x_lo, n - 1)
                    p.turn_x1(pe, n)
                elif what != "x":
                    s = "hz".index(what)
                    pe.wait_ge(lo, s + 1)
                    pe.wait_ge(x_lo, NB // 2 if half == [0] else (n + 1) * NB)
                    product(s, n, *half)
            with pe.Fori(1, MT) as m:
                for s, free in ((0, h_copied), (1, silu)):
                    pe.wait_ge(lo, m * 2 + s + 1)
                    pe.wait_ge(free, m * NB)
                    for n in range(NB):
                        product(s, n)

        @block.scalar
        def _(act):
            def copy_h(m, n):
                act.wait_ge(h_mm, m * NB + n + 1)
                nc.scalar.activation(h_in[:, PAD + n * BLK:PAD + (n + 1) * BLK], p.ps[:, n, :],
                                     ACT.Copy).then_inc(h_copied, 1)

            def silu_z(m, n):
                act.wait_ge(z_mm, m * NB + n + 1)
                nc.scalar.activation(z[:, n * BLK:(n + 1) * BLK], p.ps[:, NB + n, :], ACT.Silu).then_inc(silu, 1)

            nc.scalar.preload_act_table_set("silu_and_others")
            for what, n, *half in FIRST:
                if (what, n) == ("z", 0):
                    for s in range(2):
                        act.wait_ge(p.x1_stored[s], NT // 2 * DMA)
                if what == "x":
                    act.wait_ge(x_turned, n + 1)
                    nc.scalar.activation(x_part(p.x_hi, n), x_banks(n), ACT.Copy).then_inc(x_hi, 1)
                elif half != [0]:
                    (copy_h if what == "h" else silu_z)(0, n)
                if (what, n) == ("h", NB - 1):
                    p.mix_hi_part(act, 0, 1)

            def tile(m, last):
                act.wait_ge(z_mm, m * NB)
                p.mix_hi_part(act, 1, m)
                act.wait_ge(pooled, m)
                for n in range(NB):
                    copy_h(m, n)
                if not last:
                    p.mix_hi_part(act, 0, m + 1)
                act.wait_ge(stored, m * DMA)
                for n in range(NB):
                    silu_z(m, n)

            with act.Fori(1, MT - 1) as m:
                tile(m, False)
            tile(MT - 1, True)

        @block.vector
        def _(dve):
            for n, t in enumerate((h_in, win_a, win_b)):
                last = nc.vector.memset(t[:, 0:PAD], 0.0)
            last.then_inc(chain, 1)
            dve.wait_ge(chain, 1)
            body = slice(PAD, PAD + SEQ)
            base = 1

            def split_x():
                for t in range(NT):
                    dve.wait_ge(x_hi, t + 1)
                    nc.vector.tensor_tensor(x_part(p.x_lo, t), x_banks(t), x_part(p.x_hi, t).bitcast(F32),
                                            ALU.subtract).then_inc(x_lo, 1)

            def tile(m, g, base, last):
                if isinstance(m, int) and m == 0:
                    split_x()
                else:
                    p.mix_lo_part(dve, 1, m)
                if not last:
                    p.mix_lo_part(dve, 0, m + 1)
                dve.wait_ge(mixed, m)
                dve.wait_ge(h_copied, m * NB + NB)
                src, step = h_in, 1
                for i in range(g + 1):
                    dst = (win_a, win_b)[i % 2]
                    nc.vector.tensor_tensor(dst[:, body], src[:, body], src[:, PAD - step:PAD + SEQ - step],
                                            ALU.add).then_inc(chain, 1)
                    dve.wait_ge(chain, base + i + 1)
                    src, step = dst, step * 2
                nc.vector.tensor_tensor(src[:, PAD:2 * PAD], src[:, PAD:2 * PAD], p.correct[:, g, :],
                                        ALU.mult).then_inc(chain, 1)
                dve.wait_ge(chain, base + g + 2)
                other = win_b if src is win_a else win_a
                nc.vector.scalar_tensor_tensor(out=other[:, body], in0=src[:, body], scalar=1.0 / WINDOWS[g],
                                               in1=h_in[:, body], op0=ALU.mult, op1=ALU.subtract).then_inc(pooled, 1)
                dve.wait_ge(pooled, m + 1)
                nc.vector.tensor_scalar(other[:, body], other[:, body], p.b_grp[:, ds(m, 1)], p.scale[:, ds(m, 1)],
                                        ALU.add, ALU.mult).then_inc(chain, 1)
                dve.wait_ge(chain, base + g + 3)
                if not last:
                    dve.wait_ge(silu, m * NB + NB)
                    nc.vector.tensor_tensor(z[:], z[:], other[:, body], ALU.mult).then_inc(mixed, 1)
                else:
                    for n in range(NB):
                        dve.wait_ge(silu, m * NB + n + 1)
                        cols = slice(n * BLK, (n + 1) * BLK)
                        nc.vector.tensor_tensor(z[:, cols], z[:, cols], other[:, PAD + n * BLK:PAD + (n + 1) * BLK],
                                                ALU.mult).then_inc(mixed, 1)

            for g in range(GROUPS):
                per_tile = g + 3
                rolled = GT - 1 if g == GROUPS - 1 else GT
                if g == 0:
                    tile(0, g, base, False)
                with dve.Fori(1 if g == 0 else 0, rolled) as i:
                    tile(i + g * GT, g, i * per_tile + base, False)
                if rolled < GT:
                    tile(MT - 1, g, base + rolled * per_tile, True)
                base += GT * per_tile


def pool_out_and_norm(nc, p, a, out_dram):
    BT, TB = p.BT, p.BT // P
    BLOCKS = SEQ // BT
    SLOTS = p.M_RAW
    p.at = p.ln_at
    ln_g = p.place("o_ln_g", [P, D])
    ln_b = p.place("o_ln_b", [P, D])
    w_hi = p.place("o_w_hi", [P, MT, D], F32R)
    w_lo = p.place("o_w_lo", [P, MT, D], F32R)
    m_hi = [p.place(f"o_m_hi{s}", [P, BT], F32R) for s in range(SLOTS)]
    m_lo = [p.place(f"o_m_lo{s}", [P, BT], F32R) for s in range(SLOTS)]
    m_raw = p.m_raw
    x = [p.place(f"o_x{s}", [P, D]) for s in range(TB)]
    res = [[p.place(f"o_res{b}{i}", [P, D]) for i in range(TB)] for b in range(2)]
    stats = [p.place(f"o_stats{i}", [P, 2, 6]) for i in range(TB)]
    moments = [p.place(f"o_moments{i}", [P, 2]) for i in range(TB)]
    rstd = [p.place(f"o_rstd{i}", [P, 1]) for i in range(TB)]
    assert p.at <= p.mix_raw_at
    raw, raw_loaded, RAW, m_loaded = p.out_raw, p.out_raw_loaded, p.ROWS, p.m_loaded
    phase = ExitStack()
    sem = lambda name: phase.enter_context(nc.semaphore("o_" + name))
    ln_loaded = sem("ln_loaded")
    x_loaded = [sem(f"x_loaded{i}") for i in range(TB)]
    stored = [[sem(f"stored{b}{i}") for i in range(TB)] for b in range(2)]
    (w_hi_done, w_lo_done, hi, lo, step_mm, y_mm, y_read, stats_done, moments_done, rstd_done, out_done) = (
        sem(n) for n in ("w_hi_done", "w_lo_done", "hi", "lo", "step_mm", "y_mm", "y_read", "stats_done",
                         "moments_done", "rstd_done", "out_done"))
    RESIDUAL_AFTER = 1
    NORM_AFTER = {4: 0, 8: 1}
    STORE_AFTER = {9: 0, 13: 1}
    READ_BASE = TB * 2

    def banks(parity, i):
        return [p.ps[:, parity * 4 + i * 2 + half, :] for half in range(2)]

    def run(engine, block):
        for parity in range(2):
            block(parity, parity, 0)
        with engine.Fori(1, BLOCKS // 2) as pair:
            for parity in range(2):
                block(pair * 2 + parity, parity, pair)

    def is_first(b):
        return isinstance(b, int) and b == 0

    with phase, nc.Block() as block:

        @block.sync
        def _(sp):
            def load_x(b):
                for i in range(TB):
                    sp.dma_start(x[i][:], p.x1[ds((b * TB + i) * P, P), :]).then_inc(x_loaded[i], DMA)

            def store(b, parity, i):
                sp.wait_ge(out_done, (b * TB + i) * 3 + 3)
                sp.dma_start(out_dram[ds((b * TB + i) * P, P), :], res[parity][i][:]).then_inc(stored[parity][i], DMA)

            def blk(b, parity, pair):
                for k in range(MT):
                    if is_first(b):
                        if k >= p.M_PREFETCHED:
                            if k >= SLOTS:
                                sp.wait_ge(lo, k - SLOTS + 1)
                            if k == MT - 1:
                                sp.wait_ge(p.mixed_stored, (MT - 1 + NB) * DMA)
                            p.load_m(sp, 0, k)
                        if k >= p.OUT_PREFETCHED:
                            sp.wait_ge(w_lo_done, 2 * (k - RAW) + 2)
                            p.load_out(sp, k)
                    else:
                        sp.wait_ge(lo, b * MT + k - SLOTS + 1)
                        p.load_m(sp, b, k)
                        if k == RESIDUAL_AFTER + SLOTS:
                            sp.wait_ge(y_read, READ_BASE + b * TB * 2)
                            load_x(b)
                        if k in STORE_AFTER:
                            store(b - 1, 1 - parity, STORE_AFTER[k])
                if is_first(b):
                    for ln, src in ((ln_g, a["ln_g"]), (ln_b, a["ln_b"])):
                        sp.dma_start(ln[:], src[1:2, :].to_broadcast([P, D])).then_inc(ln_loaded, DMA)
                    load_x(0)

            run(sp, blk)
            for i in range(TB):
                store(BLOCKS - 1, 1, i)
            for b in range(2):
                for i in range(TB):
                    sp.wait_ge(stored[b][i], BLOCKS // 2 * DMA)

        @block.tensor
        def _(pe):
            def product(parity, k, i, half):
                cols = slice(half * BLK, (half + 1) * BLK)
                return split_product(nc, banks(parity, i)[half], m_hi[k % SLOTS][:, i * P:(i + 1) * P],
                                     m_lo[k % SLOTS][:, i * P:(i + 1) * P], w_hi[:, k, cols], w_lo[:, k, cols],
                                     k == 0, k == MT - 1)

            with pe.Fori(0, BLOCKS // 2) as pair:
                for parity in range(2):
                    b = pair * 2 + parity
                    for k in range(MT - SLOTS):
                        pe.wait_ge(lo, b * MT + k + 1)
                        pe.wait_ge(w_lo_done, 2 * k + 2)
                        if k == 0:
                            pe.wait_ge(y_read, b * TB * 2)
                        for i in range(TB):
                            for half in range(2):
                                last = product(parity, k, i, half)
                        last.then_inc(step_mm, 1)
                    for i in range(TB):
                        for half in range(2):
                            for k in range(MT - SLOTS, MT):
                                if i == half == 0:
                                    pe.wait_ge(lo, b * MT + k + 1)
                                    pe.wait_ge(w_lo_done, 2 * k + 2)
                                last = product(parity, k, i, half)
                                if i == TB - 1 and half == 1 and k < MT - 1:
                                    last.then_inc(step_mm, 1)
                            last.then_inc(y_mm, 1)

        STEPS = MT - 1

        @block.scalar
        def _(act):
            def norm_rstd(b, i):
                t = b * TB + i
                act.wait_ge(moments_done, t + 1)
                nc.scalar.activation(rstd[i][:], moments[i][:, 1:2], ACT.Ln, bias=p.eps_ln[:]).then_inc(rstd_done, 1)
                act.wait_ge(rstd_done, t * 2 + 1)
                nc.scalar.activation(rstd[i][:], rstd[i][:], ACT.Exp, scale=-0.5).then_inc(rstd_done, 1)

            def blk(b, parity, pair):
                for k in range(MT):
                    if is_first(b):
                        act.wait_ge(m_loaded[k % SLOTS], (k // SLOTS + 1) * DMA)
                        if k >= SLOTS:
                            act.wait_ge(step_mm, k - SLOTS + 1)
                    else:
                        act.wait_ge(m_loaded[k % SLOTS], (b * (MT // SLOTS) + k // SLOTS + 1) * DMA)
                        if k >= SLOTS:
                            act.wait_ge(step_mm, b * STEPS + k - SLOTS + 1)
                        elif k == SLOTS - 1:
                            act.wait_ge(y_mm, b * TB * 2)
                        else:
                            act.wait_ge(step_mm, (b - 1) * STEPS + MT + k - SLOTS + 1)
                    nc.scalar.activation(m_hi[k % SLOTS][:], m_raw[k % SLOTS][:], ACT.Copy).then_inc(hi, 1)
                    if is_first(b):
                        act.wait_ge(raw_loaded[k % RAW], (k // RAW + 1) * DMA)
                        for half in range(2):
                            cols = slice(half * BLK, (half + 1) * BLK)
                            nc.scalar.activation(w_hi[:, k, cols], raw[k % RAW][:, cols], ACT.Copy).then_inc(w_hi_done, 1)
                        if k == MT - 1:
                            nc.scalar.preload_act_table_set("natural_log_exp_and_others")
                    elif k in NORM_AFTER:
                        norm_rstd(b - 1, NORM_AFTER[k])

            run(act, blk)
            for i in range(TB):
                norm_rstd(BLOCKS - 1, i)

        @block.vector
        def _(dve):
            dve.sem_inc(y_read, READ_BASE)

            def residual(b, parity, pair, i):
                dve.wait_ge(x_loaded[i], (b + 1) * DMA)
                dve.wait_ge(stored[parity][i], pair * DMA)
                for half in range(2):
                    cols = slice(half * BLK, (half + 1) * BLK)
                    dve.wait_ge(y_mm, (b * TB + i) * 2 + half + 1)
                    nc.vector.scalar_tensor_tensor(out=res[parity][i][:, cols], in0=x[i][:, cols], scalar=ALPHA,
                                                   in1=banks(parity, i)[half], op0=ALU.mult, op1=ALU.add
                                                   ).then_inc(y_read, 1)

            def norm_moments(b, parity, i):
                t = b * TB + i
                dve.wait_ge(y_read, READ_BASE + t * 2 + 2)
                for half in range(2):
                    nc.vector.bn_stats(stats[i][:, half, :], res[parity][i][:, half * BLK:(half + 1) * BLK]
                                       ).then_inc(stats_done, 1)
                dve.wait_ge(stats_done, t * 2 + 2)
                nc.vector.memset(p.stats_carrier[:], 0.0)
                nc.vector.bn_aggr(moments[i][:], stats[i][:].rearrange("p a b -> p (a b)")).then_inc(moments_done, 1)

            def norm_end(b, parity, i):
                t, r = b * TB + i, res[parity][i]
                dve.wait_ge(moments_done, t + 1)
                dve.wait_ge(rstd_done, t * 2 + 2)
                nc.vector.tensor_scalar(r[:], r[:], moments[i][:, 0:1], rstd[i][:, 0:1], ALU.subtract, ALU.mult
                                        ).then_inc(out_done, 1)
                dve.wait_ge(out_done, t * 3 + 1)
                nc.vector.tensor_tensor(r[:], r[:], ln_g[:], ALU.mult).then_inc(out_done, 1)
                dve.wait_ge(out_done, t * 3 + 2)
                nc.vector.tensor_tensor(r[:], r[:], ln_b[:], ALU.add).then_inc(out_done, 1)

            def blk(b, parity, pair):
                for k in range(MT):
                    dve.wait_ge(hi, b * MT + k + 1)
                    nc.vector.tensor_tensor(m_lo[k % SLOTS][:], m_raw[k % SLOTS][:], m_hi[k % SLOTS][:].bitcast(F32),
                                            ALU.subtract).then_inc(lo, 1)
                    if is_first(b):
                        for half in range(2):
                            cols = slice(half * BLK, (half + 1) * BLK)
                            dve.wait_ge(w_hi_done, 2 * k + half + 1)
                            nc.vector.tensor_tensor(w_lo[:, k, cols], raw[k % RAW][:, cols],
                                                    w_hi[:, k, cols].bitcast(F32), ALU.subtract).then_inc(w_lo_done, 1)
                    else:
                        if k == RESIDUAL_AFTER:
                            for i in range(TB):
                                residual(b - 1, 1 - parity, pair - 1 + parity, i)
                        if k in NORM_AFTER:
                            norm_moments(b - 1, 1 - parity, NORM_AFTER[k])
                            norm_end(b - 1, 1 - parity, NORM_AFTER[k])
                if is_first(b):
                    dve.wait_ge(ln_loaded, 2 * DMA)

            run(dve, blk)
            for i in range(TB):
                residual(BLOCKS - 1, 1, BLOCKS // 2 - 1, i)
                norm_moments(BLOCKS - 1, 1, i)
                norm_end(BLOCKS - 1, 1, i)


def gla_pool_trunk(nc, a, out_dram):
    with ExitStack() as ctx:
        p = Program(nc, ctx, a)
        prepare(nc, p, a)
        project(nc, p, a)
        attend_and_norm(nc, p, a)
        pool_mix(nc, p, a)
        pool_out_and_norm(nc, p, a, out_dram)


_INS = ["x", "gla_w_in", "gla_w_gk", "gla_b_gk", "gla_norm_w", "gla_w_out", "pool_w_in", "pool_w_grp",
        "pool_b_grp", "pool_scale", "pool_w_out", "ln_g", "ln_b"]


def kernel(**inputs):
    import numpy as np
    import concourse.bacc as bacc
    from concourse.bass_utils import run_bass_kernel_spmd

    nc = bacc.Bacc("TRN2", target_bir_lowering=False, num_devices=1)
    arrays, a = {}, {}
    for name in _INS:
        arrays[f"in_{name}"] = np.ascontiguousarray(inputs[name])
        a[name] = nc.dram_tensor(f"in_{name}", arrays[f"in_{name}"].shape, F32, kind="ExternalInput").ap()
    out = nc.dram_tensor("out", (1, SEQ, D), F32, kind="ExternalOutput").ap()
    gla_pool_trunk(nc, a, out[0])
    r = run_bass_kernel_spmd(nc, [arrays], core_ids=[0])
    return r.results[0]["out"]
```
